# Optimizing a Trainium2 kernel written in Bass

```python
import jax, jax.numpy as jnp
from jax import lax
import numpy as np
import jax
import jax.numpy as jnp

D_MODEL = 1024
BATCH = 1
SEQ = 512
DEPTH = 1

N_BRANCH = 4
BRANCH_WIDTH = 512
ML_HEADS = 4
ML_DK = 128
ML_DV = 128
FX_HEADS = 4
FX_DH = 128
LRU_WIDTH = 512
LRU_BLOCKS = 8
LRU_BLOCK = 64
CONV_WIDTH = 4
LRU_C = 8.0
GLA_HEADS = 4
GLA_DK = 64
GLA_DV = 128
GLA_RANK = 16
GLA_TAU = 16.0
D_FF = 4 * D_MODEL
CHUNK = 64
Q_BLOCK = 128
EPS = 1e-6

IN_WIDTHS = (
    ML_HEADS * ML_DK, ML_HEADS * ML_DK, ML_HEADS * ML_DV, ML_HEADS * ML_DV, ML_HEADS, ML_HEADS,
    FX_HEADS * FX_DH, FX_HEADS * FX_DH, FX_HEADS * FX_DH, FX_HEADS,
    LRU_WIDTH, LRU_WIDTH,
    GLA_HEADS * GLA_DK, GLA_HEADS * GLA_DK, GLA_HEADS * GLA_DV, GLA_HEADS * GLA_DV, GLA_RANK,
    N_BRANCH * D_MODEL,
)
N_IN = sum(IN_WIDTHS)
ML_F_COL = 5
FX_F_COL = 9


def rms_norm(x, g):
    xf = x.astype(jnp.float32)
    y = xf * lax.rsqrt(jnp.mean(xf * xf, axis=-1, keepdims=True) + EPS)
    return (y * g.astype(jnp.float32)).astype(x.dtype)

def split_cols(z):
    offs = []
    acc = 0
    for w in IN_WIDTHS[:-1]:
        acc += w
        offs.append(acc)
    return jnp.split(z, offs, axis=-1)

def mlstm(q, k, v, i_pre, f_pre):
    f32 = jnp.float32
    B, S, H, dk = q.shape
    dv = v.shape[-1]
    nc = S // CHUNK

    def to_chunks(t):
        t = t.astype(f32).reshape((B, nc, CHUNK) + t.shape[2:])
        return jnp.swapaxes(t, 2, 3)

    qc = to_chunks(q) * (dk ** -0.5)
    kc = to_chunks(k)
    vc = to_chunks(v)
    log_i = to_chunks(i_pre)
    log_f = jax.nn.log_sigmoid(to_chunks(f_pre))
    b = jnp.cumsum(log_f, axis=-1)
    b_last = b[..., -1]

    w_end = b_last[..., None] - b + log_i
    m_loc = jnp.max(w_end, axis=-1)
    e_end = jnp.exp(w_end - m_loc[..., None])
    c_loc = jnp.einsum('bnhsk,bnhsv->bnhkv', kc * e_end[..., None], vc)
    n_loc = jnp.einsum('bnhs,bnhsk->bnhk', e_end, kc)

    def step(carry, inp):
        c, n, m = carry
        g, ml, cl, nl = inp
        m_new = jnp.maximum(g + m, ml)
        a = jnp.exp(g + m - m_new)
        bb = jnp.exp(ml - m_new)
        c_new = a[..., None, None] * c + bb[..., None, None] * cl
        n_new = a[..., None] * n + bb[..., None] * nl
        return (c_new, n_new, m_new), (c, n, m)

    init = (jnp.zeros((B, H, dk, dv), f32), jnp.zeros((B, H, dk), f32), jnp.zeros((B, H), f32))
    xs = (jnp.moveaxis(b_last, 1, 0), jnp.moveaxis(m_loc, 1, 0),
          jnp.moveaxis(c_loc, 1, 0), jnp.moveaxis(n_loc, 1, 0))
    _, (c_prev, n_prev, m_prev) = lax.scan(step, init, xs)
    c_prev = jnp.moveaxis(c_prev, 0, 1)
    n_prev = jnp.moveaxis(n_prev, 0, 1)
    m_prev = jnp.moveaxis(m_prev, 0, 1)

    causal = jnp.tril(jnp.ones((CHUNK, CHUNK), dtype=bool))
    d_ts = jnp.where(causal, b[..., :, None] - b[..., None, :] + log_i[..., None, :], -jnp.inf)
    inter_log = b + m_prev[..., None]
    m_t = jnp.maximum(inter_log, jnp.max(d_ts, axis=-1))
    s_qk = jnp.einsum('bnhtk,bnhsk->bnhts', qc, kc) * jnp.exp(d_ts - m_t[..., None])
    w_inter = jnp.exp(inter_log - m_t)
    num = (jnp.einsum('bnhts,bnhsv->bnhtv', s_qk, vc)
           + w_inter[..., None] * jnp.einsum('bnhtk,bnhkv->bnhtv', qc, c_prev))
    den = s_qk.sum(-1) + w_inter * jnp.einsum('bnhtk,bnhk->bnht', qc, n_prev)
    h = num / jnp.maximum(jnp.abs(den), jnp.exp(-m_t))[..., None]
    return jnp.swapaxes(h, 2, 3).reshape(B, S, H, dv)

def forgetting_attention(q, k, v, f_pre, gq, gk):
    f32 = jnp.float32
    B, S, H, Dh = q.shape
    q = rms_norm(q.astype(f32), gq) * (Dh ** -0.5)
    k = rms_norm(k.astype(f32), gk)
    v = v.astype(f32)
    F = jnp.cumsum(jax.nn.log_sigmoid(f_pre.astype(f32)), axis=1)
    Fk = jnp.transpose(F, (0, 2, 1))
    nb = S // Q_BLOCK
    qb = jnp.moveaxis(q.reshape(B, nb, Q_BLOCK, H, Dh), 1, 0)
    Fq = jnp.moveaxis(Fk.reshape(B, H, nb, Q_BLOCK), 2, 0)
    pos_k = jnp.arange(S)

    def block(args):
        qi, Fi, idx = args
        pos_q = idx * Q_BLOCK + jnp.arange(Q_BLOCK)
        s = jnp.einsum('bqhd,bkhd->bhqk', qi, k) + (Fi[..., :, None] - Fk[:, :, None, :])
        s = jnp.where(pos_k[None, :] <= pos_q[:, None], s, -jnp.inf)
        p = jax.nn.softmax(s, axis=-1)
        return jnp.einsum('bhqk,bkhd->bqhd', p, v)

    out = lax.map(block, (qb, Fq, jnp.arange(nb)))
    return jnp.moveaxis(out, 0, 1).reshape(B, S, H, Dh)

def rg_lru_branch(xb, yb, conv_w, conv_b, wa, ba, wx, bx, lam):
    f32 = jnp.float32
    B, S, W = xb.shape
    xf = xb.astype(f32)
    xc = lax.conv_general_dilated(xf, conv_w.astype(f32)[:, None, :], window_strides=(1,),
                                  padding=[(CONV_WIDTH - 1, 0)],
                                  dimension_numbers=('NWC', 'WIO', 'NWC'),
                                  feature_group_count=W) + conv_b.astype(f32)
    xg = xc.reshape(B, S, LRU_BLOCKS, LRU_BLOCK)
    r_gate = jax.nn.sigmoid(jnp.einsum('bsgi,gij->bsgj', xg, wa.astype(f32)).reshape(B, S, W) + ba.astype(f32))
    i_gate = jax.nn.sigmoid(jnp.einsum('bsgi,gij->bsgj', xg, wx.astype(f32)).reshape(B, S, W) + bx.astype(f32))
    log_a = -LRU_C * r_gate * jax.nn.softplus(-lam.astype(f32))
    a = jnp.exp(log_a)
    u = jnp.sqrt(-jnp.expm1(2.0 * log_a)) * (i_gate * xc)

    def combine(left, right):
        a1, b1 = left
        a2, b2 = right
        return a1 * a2, a2 * b1 + b2

    _, h = lax.associative_scan(combine, (a, u), axis=1)
    return h * jax.nn.gelu(yb.astype(f32))

def gla(q, k, v, log_alpha):
    f32 = jnp.float32
    B, S, H, dk = q.shape
    dv = v.shape[-1]
    nc = S // CHUNK

    def to_chunks(t):
        t = t.astype(f32).reshape((B, nc, CHUNK) + t.shape[2:])
        return jnp.swapaxes(t, 2, 3)

    qc = to_chunks(q) * (dk ** -0.5)
    kc = to_chunks(k)
    vc = to_chunks(v)
    bc = jnp.cumsum(to_chunks(log_alpha), axis=3)
    b_last = bc[..., -1, :]
    q_t = qc * jnp.exp(bc)
    k_t = kc * jnp.exp(-bc)
    causal = jnp.tril(jnp.ones((CHUNK, CHUNK), dtype=bool))
    attn = jnp.where(causal, jnp.einsum('bnhtk,bnhsk->bnhts', q_t, k_t), 0.0)
    o_intra = jnp.einsum('bnhts,bnhsv->bnhtv', attn, vc)
    ds = jnp.einsum('bnhsk,bnhsv->bnhkv', kc * jnp.exp(b_last[..., None, :] - bc), vc)

    def step(s, inp):
        decay, d = inp
        return decay[..., None] * s + d, s

    init = jnp.zeros((B, H, dk, dv), f32)
    _, s_prev = lax.scan(step, init, (jnp.moveaxis(jnp.exp(b_last), 1, 0), jnp.moveaxis(ds, 1, 0)))
    s_prev = jnp.moveaxis(s_prev, 0, 1)
    o = o_intra + jnp.einsum('bnhtk,bnhkv->bnhtv', q_t, s_prev)
    return jnp.swapaxes(o, 2, 3).reshape(B, S, H, dv)

def hybrid_layer(x, norm1_g, w_in, b_in, ml_norm_g, fx_qnorm_g, fx_knorm_g,
                 lru_conv_w, lru_conv_b, lru_wa, lru_ba, lru_wx, lru_bx, lru_lambda,
                 gla_w_alpha, gla_b_alpha, gla_norm_g, w_branch, w_o, norm2_g, w_up, w_down):
    f32 = jnp.float32
    B, S, _ = x.shape
    h = rms_norm(x, norm1_g)
    z = h @ w_in + b_in
    (mq, mk, mv, mo, mi, mf, fq, fk, fv, ff, rx, ry,
     gq, gk, gv, gg, ga, gates) = split_cols(z)

    y_ml = mlstm(mq.reshape(B, S, ML_HEADS, ML_DK), mk.reshape(B, S, ML_HEADS, ML_DK),
                 mv.reshape(B, S, ML_HEADS, ML_DV), mi, mf)
    y_ml = rms_norm(y_ml, ml_norm_g.reshape(ML_HEADS, ML_DV)).reshape(B, S, BRANCH_WIDTH)
    y_ml = y_ml * jax.nn.sigmoid(mo.astype(f32))

    y_fx = forgetting_attention(fq.reshape(B, S, FX_HEADS, FX_DH), fk.reshape(B, S, FX_HEADS, FX_DH),
                                fv.reshape(B, S, FX_HEADS, FX_DH), ff, fx_qnorm_g, fx_knorm_g)
    y_fx = y_fx.reshape(B, S, BRANCH_WIDTH)

    y_lru = rg_lru_branch(rx, ry, lru_conv_w, lru_conv_b, lru_wa, lru_ba, lru_wx, lru_bx, lru_lambda)

    log_alpha = jax.nn.log_sigmoid(ga.astype(f32) @ gla_w_alpha.astype(f32) + gla_b_alpha.astype(f32)) / GLA_TAU
    y_gla = gla(gq.reshape(B, S, GLA_HEADS, GLA_DK), gk.reshape(B, S, GLA_HEADS, GLA_DK),
                gv.reshape(B, S, GLA_HEADS, GLA_DV), log_alpha.reshape(B, S, GLA_HEADS, GLA_DK))
    y_gla = rms_norm(y_gla, gla_norm_g.reshape(GLA_HEADS, GLA_DV)).reshape(B, S, BRANCH_WIDTH)
    y_gla = y_gla * jax.nn.silu(gg.astype(f32))

    ycat = jnp.stack([y_ml, y_fx, y_lru, y_gla], axis=2).astype(x.dtype)
    yb = jnp.einsum('bsnw,nwd->bsnd', ycat, w_branch)
    g = jax.nn.sigmoid(gates.reshape(B, S, N_BRANCH, D_MODEL))
    merged = jnp.sum(g * yb, axis=2)
    x = x + merged @ w_o

    h2 = rms_norm(x, norm2_g)
    x = x + jnp.square(jax.nn.relu(h2 @ w_up)) @ w_down
    return x

def first_inputs(seed: int = 0) -> dict:
    key = jax.random.key(seed)
    ks = jax.random.split(key, 24)
    f32 = jnp.float32

    def nrm(k, shape, scale):
        return jax.random.normal(k, shape, f32) * scale

    x = nrm(ks[0], (BATCH, SEQ, D_MODEL), 1.0)
    norm1_g = 1.0 + nrm(ks[1], (DEPTH, D_MODEL), 0.02)
    w_in = nrm(ks[2], (DEPTH, D_MODEL, N_IN), D_MODEL ** -0.5)
    b_in = nrm(ks[3], (DEPTH, N_IN), 0.02)
    ml_f_off = sum(IN_WIDTHS[:ML_F_COL])
    fx_f_off = sum(IN_WIDTHS[:FX_F_COL])
    b_in = b_in.at[:, ml_f_off:ml_f_off + ML_HEADS].add(jnp.linspace(3.0, 6.0, ML_HEADS, dtype=f32))
    b_in = b_in.at[:, fx_f_off:fx_f_off + FX_HEADS].add(jnp.linspace(3.0, 6.0, FX_HEADS, dtype=f32))
    ml_norm_g = 1.0 + nrm(ks[4], (DEPTH, ML_HEADS * ML_DV), 0.02)
    fx_qnorm_g = 1.0 + nrm(ks[5], (DEPTH, FX_DH), 0.02)
    fx_knorm_g = 1.0 + nrm(ks[6], (DEPTH, FX_DH), 0.02)
    lru_conv_w = nrm(ks[7], (DEPTH, CONV_WIDTH, LRU_WIDTH), CONV_WIDTH ** -0.5)
    lru_conv_b = nrm(ks[8], (DEPTH, LRU_WIDTH), 0.02)
    lru_wa = nrm(ks[9], (DEPTH, LRU_BLOCKS, LRU_BLOCK, LRU_BLOCK), LRU_BLOCK ** -0.5)
    lru_ba = nrm(ks[10], (DEPTH, LRU_WIDTH), 0.02)
    lru_wx = nrm(ks[11], (DEPTH, LRU_BLOCKS, LRU_BLOCK, LRU_BLOCK), LRU_BLOCK ** -0.5)
    lru_bx = nrm(ks[12], (DEPTH, LRU_WIDTH), 0.02)
    u = jax.random.uniform(ks[13], (DEPTH, LRU_WIDTH), f32, 0.9, 0.999)
    a0 = u ** (1.0 / LRU_C)
    lru_lambda = jnp.log(a0) - jnp.log1p(-a0)
    gla_w_alpha = nrm(ks[14], (DEPTH, GLA_RANK, GLA_HEADS * GLA_DK), GLA_RANK ** -0.5)
    gla_b_alpha = nrm(ks[15], (DEPTH, GLA_HEADS * GLA_DK), 0.02)
    gla_norm_g = 1.0 + nrm(ks[16], (DEPTH, GLA_HEADS * GLA_DV), 0.02)
    w_branch = nrm(ks[17], (DEPTH, N_BRANCH, BRANCH_WIDTH, D_MODEL), BRANCH_WIDTH ** -0.5)
    w_o = nrm(ks[18], (DEPTH, D_MODEL, D_MODEL), D_MODEL ** -0.5)
    norm2_g = 1.0 + nrm(ks[19], (DEPTH, D_MODEL), 0.02)
    w_up = nrm(ks[20], (DEPTH, D_MODEL, D_FF), D_MODEL ** -0.5)
    w_down = nrm(ks[21], (DEPTH, D_FF, D_MODEL), D_FF ** -0.5)
    return {"x": x, "norm1_g": norm1_g, "w_in": w_in, "b_in": b_in, "ml_norm_g": ml_norm_g,
            "fx_qnorm_g": fx_qnorm_g, "fx_knorm_g": fx_knorm_g, "lru_conv_w": lru_conv_w,
            "lru_conv_b": lru_conv_b, "lru_wa": lru_wa, "lru_ba": lru_ba, "lru_wx": lru_wx,
            "lru_bx": lru_bx, "lru_lambda": lru_lambda, "gla_w_alpha": gla_w_alpha,
            "gla_b_alpha": gla_b_alpha, "gla_norm_g": gla_norm_g, "w_branch": w_branch, "w_o": w_o,
            "norm2_g": norm2_g, "w_up": w_up, "w_down": w_down}

def first_block(x, norm1_g, w_in, b_in, ml_norm_g, fx_qnorm_g, fx_knorm_g, lru_conv_w, lru_conv_b,
              lru_wa, lru_ba, lru_wx, lru_bx, lru_lambda, gla_w_alpha, gla_b_alpha, gla_norm_g,
              w_branch, w_o, norm2_g, w_up, w_down):
    for l in range(DEPTH):
        x = hybrid_layer(x, norm1_g[l], w_in[l], b_in[l], ml_norm_g[l], fx_qnorm_g[l], fx_knorm_g[l],
                         lru_conv_w[l], lru_conv_b[l], lru_wa[l], lru_ba[l], lru_wx[l], lru_bx[l],
                         lru_lambda[l], gla_w_alpha[l], gla_b_alpha[l], gla_norm_g[l],
                         w_branch[l], w_o[l], norm2_g[l], w_up[l], w_down[l])
    return x


_first_inputs = first_inputs


def first_inputs(seed=0):
    import zlib

    import numpy as np

    out = dict(_first_inputs(seed))
    spreads = {}
    factors = {'norm1_g': 2.718,
     'ml_norm_g': 8.0,
     'fx_qnorm_g': 8.0,
     'fx_knorm_g': 8.0,
     'lru_ba': 8.0,
     'lru_bx': 8.0,
     'gla_b_alpha': 8.0,
     'gla_norm_g': 8.0,
     'norm2_g': 3.332}
    for name, (base, spread) in spreads.items():
        noise = np.random.default_rng([zlib.crc32(name.encode()), seed]).standard_normal(out[name].shape)
        drawn = base * np.exp(spread * noise) if base else spread * noise
        out[name] = __import__('jax').numpy.asarray(drawn.astype(out[name].dtype))
    for name, factor in factors.items():
        out[name] = (out[name] * factor).astype(out[name].dtype)
    return out


_narrow_inputs = first_inputs


def first_inputs(seed=0):

    out = dict(_narrow_inputs(seed))
    wider = {'ml_norm_g': 9.84,
     'lru_conv_b': 5.96,
     'lru_ba': 8.4,
     'lru_bx': 7.93,
     'gla_norm_g': 3.19,
     'norm2_g': 3.45}
    for name, times in wider.items():
        mean = out[name].mean()
        out[name] = (mean + times * (out[name] - mean)).astype(out[name].dtype)
    return out


DEPTH_2 = 2

N_GROUPS = 4
HEADS = 4
HEAD_DIM = 64
D_GROUP = HEADS * HEAD_DIM
D_MIX = N_GROUPS * D_GROUP
D_FF_2 = 2816
ROPE_THETA = 10000.0
MLA_Q_RANK = 256
MLA_KV_RANK = 128
MLA_D_NOPE = 64
MLA_D_ROPE = 32
MLA_D_V = 64
NSA_CMP_LEN = 32
NSA_CMP_STRIDE = 16
NSA_SEL_LEN = 64
NSA_N_SEL = 8
NSA_N_INIT = 1
NSA_N_LOCAL = 2
NSA_WINDOW = 512
DSA_TOPK = 256
DSA_IDX_HEADS = 8
DSA_IDX_DIM = 32
DN_ALPHA = (2.0 * DEPTH_2) ** 0.25
DN_BETA = (8.0 * DEPTH_2) ** -0.25
LN_EPS = 1e-5
RMS_EPS = 1e-6
NEG_INF = -1e30
FORCE_SCORE = 1e4

IN_SPLITS = (
    ('mla_cq', MLA_Q_RANK), ('mla_ckv', MLA_KV_RANK), ('mla_krope', MLA_D_ROPE),
    ('nsa_q', D_GROUP), ('nsa_k_cmp', HEAD_DIM), ('nsa_v_cmp', HEAD_DIM),
    ('nsa_k_slc', HEAD_DIM), ('nsa_v_slc', HEAD_DIM), ('nsa_k_win', HEAD_DIM),
    ('nsa_v_win', HEAD_DIM), ('nsa_gate', 3 * HEADS),
    ('dsa_q', D_GROUP), ('dsa_k', HEAD_DIM), ('dsa_v', HEAD_DIM),
    ('idx_q', DSA_IDX_HEADS * DSA_IDX_DIM), ('idx_k', DSA_IDX_DIM), ('idx_w', DSA_IDX_HEADS),
    ('sb_q', D_GROUP), ('sb_k', D_GROUP), ('sb_v', D_GROUP),
)
D_IN = sum(w for _, w in IN_SPLITS)


def layer_norm(x, g, b):
    xf = x.astype(jnp.float32)
    mu = jnp.mean(xf, -1, keepdims=True)
    var = jnp.mean(jnp.square(xf - mu), -1, keepdims=True)
    return ((xf - mu) * lax.rsqrt(var + LN_EPS) * g + b).astype(x.dtype)

def rms_norm_2(x, g):
    xf = x.astype(jnp.float32)
    return (xf * lax.rsqrt(jnp.mean(xf * xf, -1, keepdims=True) + RMS_EPS) * g).astype(x.dtype)

def swiglu(x, w1, w3, w2):
    return (jax.nn.silu(x @ w1) * (x @ w3)) @ w2

def rope_tables(seq, dim):
    inv = ROPE_THETA ** (-jnp.arange(0, dim, 2, dtype=jnp.float32) / dim)
    ang = jnp.arange(seq, dtype=jnp.float32)[:, None] * inv[None, :]
    return jnp.cos(ang), jnp.sin(ang)

def apply_rope(z, cos, sin):
    shape = (cos.shape[0],) + (1,) * (z.ndim - 3) + (cos.shape[1],)
    c = cos.reshape(shape).astype(z.dtype)
    s = sin.reshape(shape).astype(z.dtype)
    z1, z2 = jnp.split(z, 2, axis=-1)
    return jnp.concatenate([z1 * c - z2 * s, z1 * s + z2 * c], axis=-1)

def masked_softmax(s, mask):
    s = jnp.where(mask, s, NEG_INF)
    e = jnp.where(mask, jnp.exp(s - jnp.max(s, -1, keepdims=True)), 0.0)
    return e / jnp.maximum(jnp.sum(e, -1, keepdims=True), 1e-30)

def unblock(y):
    nb, b, qb = y.shape[:3]
    return jnp.moveaxis(y, 0, 1).reshape((b, nb * qb) + y.shape[3:])

def split_columns(h):
    parts = {}
    off = 0
    for name, width in IN_SPLITS:
        parts[name] = h[..., off:off + width]
        off += width
    return parts

def mla_mixer(c_q, c_kv, k_rope, q_norm_g, w_uq, kv_norm_g, w_ukv, cos_r, sin_r):
    B, S, _ = c_q.shape
    q = (rms_norm_2(c_q, q_norm_g) @ w_uq).reshape(B, S, HEADS, MLA_D_NOPE + MLA_D_ROPE)
    q_nope = q[..., :MLA_D_NOPE]
    q_pe = apply_rope(q[..., MLA_D_NOPE:], cos_r, sin_r)
    kv = (rms_norm_2(c_kv, kv_norm_g) @ w_ukv).reshape(B, S, HEADS, MLA_D_NOPE + MLA_D_V)
    k_nope = kv[..., :MLA_D_NOPE]
    v = kv[..., MLA_D_NOPE:]
    k_pe = apply_rope(k_rope, cos_r, sin_r)
    scale = (MLA_D_NOPE + MLA_D_ROPE) ** -0.5
    k_pos = jnp.arange(S)

    def block(i):
        q0 = i * Q_BLOCK
        qn = lax.dynamic_slice_in_dim(q_nope, q0, Q_BLOCK, 1)
        qp = lax.dynamic_slice_in_dim(q_pe, q0, Q_BLOCK, 1)
        s = jnp.einsum('bqhd,bkhd->bhqk', qn, k_nope) + jnp.einsum('bqhd,bkd->bhqk', qp, k_pe)
        q_pos = q0 + jnp.arange(Q_BLOCK)
        p = masked_softmax(s.astype(jnp.float32) * scale, k_pos[None, :] <= q_pos[:, None])
        return jnp.einsum('bhqk,bkhd->bqhd', p.astype(v.dtype), v)

    return unblock(lax.map(block, jnp.arange(S // Q_BLOCK))).reshape(B, S, D_GROUP)

def nsa_mixer(q, k_cmp, v_cmp, k_slc, v_slc, k_win, v_win, gate_logits,
              cmp_pos, wk1, wk2, wv1, wv2, cos_h, sin_h):
    B, S, _ = q.shape
    q = apply_rope(q.reshape(B, S, HEADS, HEAD_DIM), cos_h, sin_h)
    k_cmp = apply_rope(k_cmp, cos_h, sin_h)
    k_slc = apply_rope(k_slc, cos_h, sin_h)
    k_win = apply_rope(k_win, cos_h, sin_h)
    scale = HEAD_DIM ** -0.5
    t_pos = jnp.arange(S)

    n_cmp = (S - NSA_CMP_LEN) // NSA_CMP_STRIDE + 1
    tok = np.arange(n_cmp)[:, None] * NSA_CMP_STRIDE + np.arange(NSA_CMP_LEN)[None, :]

    def compress(z, w1, w2):
        blk = (z[:, tok] + cmp_pos).reshape(B, n_cmp, NSA_CMP_LEN * HEAD_DIM)
        return jax.nn.gelu(blk @ w1) @ w2

    kc = compress(k_cmp, wk1, wk2)
    vc = compress(v_cmp, wv1, wv2)
    s_c = jnp.einsum('bshd,bnd->bhsn', q, kc).astype(jnp.float32) * scale
    p_c = masked_softmax(s_c, tok[:, -1][None, :] <= t_pos[:, None])
    o_cmp = jnp.einsum('bhsn,bnd->bshd', p_c.astype(vc.dtype), vc)

    n_slc = S // NSA_SEL_LEN
    slc_start = np.arange(n_slc) * NSA_SEL_LEN
    overlap = ((tok[:, :1] <= slc_start[None, :] + NSA_SEL_LEN - 1)
               & (tok[:, -1:] >= slc_start[None, :])).astype(np.float32)
    imp = jnp.einsum('bhsn,nj->bsj', p_c, jnp.asarray(overlap))
    cur = (t_pos // NSA_SEL_LEN)[:, None]
    jb = jnp.arange(n_slc)[None, :]
    forced = (jb < NSA_N_INIT) | ((jb <= cur) & (jb > cur - NSA_N_LOCAL))
    imp = jnp.where(forced, FORCE_SCORE, jnp.where(jb <= cur, imp, NEG_INF))
    n_top = min(NSA_N_SEL, n_slc)
    _, sel = lax.top_k(imp, n_top)
    k_blk = k_slc.reshape(B, n_slc, NSA_SEL_LEN, HEAD_DIM)
    v_blk = v_slc.reshape(B, n_slc, NSA_SEL_LEN, HEAD_DIM)
    kw = jnp.pad(k_win, ((0, 0), (NSA_WINDOW, 0), (0, 0)))
    vw = jnp.pad(v_win, ((0, 0), (NSA_WINDOW, 0), (0, 0)))
    b_idx = jnp.arange(B)[:, None, None]
    n_sel_tok = n_top * NSA_SEL_LEN

    def block(i):
        q0 = i * Q_BLOCK
        qb = lax.dynamic_slice_in_dim(q, q0, Q_BLOCK, 1)
        q_pos = q0 + jnp.arange(Q_BLOCK)
        idx = lax.dynamic_slice_in_dim(sel, q0, Q_BLOCK, 1)
        kg = k_blk[b_idx, idx].reshape(B, Q_BLOCK, n_sel_tok, HEAD_DIM)
        vg = v_blk[b_idx, idx].reshape(B, Q_BLOCK, n_sel_tok, HEAD_DIM)
        g_pos = (idx[..., None] * NSA_SEL_LEN + jnp.arange(NSA_SEL_LEN)).reshape(B, Q_BLOCK, n_sel_tok)
        s = jnp.einsum('bqhd,bqkd->bhqk', qb, kg).astype(jnp.float32) * scale
        p = masked_softmax(s, (g_pos <= q_pos[None, :, None])[:, None])
        o_s = jnp.einsum('bhqk,bqkd->bqhd', p.astype(vg.dtype), vg)
        kb = lax.dynamic_slice_in_dim(kw, q0, NSA_WINDOW + Q_BLOCK, 1)
        vb = lax.dynamic_slice_in_dim(vw, q0, NSA_WINDOW + Q_BLOCK, 1)
        w_pos = q0 - NSA_WINDOW + jnp.arange(NSA_WINDOW + Q_BLOCK)
        dist = q_pos[:, None] - w_pos[None, :]
        s = jnp.einsum('bqhd,bkd->bhqk', qb, kb).astype(jnp.float32) * scale
        p = masked_softmax(s, (dist >= 0) & (dist < NSA_WINDOW) & (w_pos[None, :] >= 0))
        o_w = jnp.einsum('bhqk,bkd->bqhd', p.astype(vb.dtype), vb)
        return o_s, o_w

    o_slc, o_win = lax.map(block, jnp.arange(S // Q_BLOCK))
    o_slc = unblock(o_slc)
    o_win = unblock(o_win)
    g = jax.nn.sigmoid(gate_logits).reshape(B, S, 3, HEADS)[..., None]
    o = g[:, :, 0] * o_cmp + g[:, :, 1] * o_slc + g[:, :, 2] * o_win
    return o.reshape(B, S, D_GROUP)

def dsa_mixer(q, k, v, q_idx, k_idx, w_idx, cos_h, sin_h, cos_i, sin_i):
    B, S, _ = q.shape
    q = apply_rope(q.reshape(B, S, HEADS, HEAD_DIM), cos_h, sin_h)
    k = apply_rope(k, cos_h, sin_h)
    q_idx = apply_rope(q_idx.reshape(B, S, DSA_IDX_HEADS, DSA_IDX_DIM), cos_i, sin_i)
    k_idx = apply_rope(k_idx, cos_i, sin_i)
    w_idx = w_idx.astype(jnp.float32) * (DSA_IDX_HEADS * DSA_IDX_DIM) ** -0.5
    scale = HEAD_DIM ** -0.5
    n_top = min(DSA_TOPK, S // 4)
    k_pos = jnp.arange(S)
    b_idx = jnp.arange(B)[:, None, None]

    def block(i):
        q0 = i * Q_BLOCK
        q_pos = q0 + jnp.arange(Q_BLOCK)
        qi = lax.dynamic_slice_in_dim(q_idx, q0, Q_BLOCK, 1)
        wi = lax.dynamic_slice_in_dim(w_idx, q0, Q_BLOCK, 1)
        rel = jax.nn.relu(jnp.einsum('bqhd,bsd->bqhs', qi, k_idx).astype(jnp.float32))
        score = jnp.einsum('bqh,bqhs->bqs', wi, rel)
        score = jnp.where(k_pos[None, None, :] <= q_pos[None, :, None], score, NEG_INF)
        _, idx = lax.top_k(score, n_top)
        kg = k[b_idx, idx]
        vg = v[b_idx, idx]
        qb = lax.dynamic_slice_in_dim(q, q0, Q_BLOCK, 1)
        s = jnp.einsum('bqhd,bqkd->bhqk', qb, kg).astype(jnp.float32) * scale
        p = masked_softmax(s, (idx <= q_pos[None, :, None])[:, None])
        return jnp.einsum('bhqk,bqkd->bqhd', p.astype(vg.dtype), vg)

    return unblock(lax.map(block, jnp.arange(S // Q_BLOCK))).reshape(B, S, D_GROUP)

def stick_breaking_mixer(q, k, v):
    B, S, _ = q.shape
    q = q.reshape(B, S, HEADS, HEAD_DIM)
    k = k.reshape(B, S, HEADS, HEAD_DIM)
    v = v.reshape(B, S, HEADS, HEAD_DIM)
    scale = HEAD_DIM ** -0.5
    k_pos = jnp.arange(S)

    def block(i):
        q0 = i * Q_BLOCK
        qb = lax.dynamic_slice_in_dim(q, q0, Q_BLOCK, 1)
        q_pos = q0 + jnp.arange(Q_BLOCK)
        z = jnp.einsum('bqhd,bkhd->bhqk', qb, k).astype(jnp.float32) * scale
        mask = k_pos[None, :] < q_pos[:, None]
        log_1m = jnp.where(mask, jax.nn.log_sigmoid(-z), 0.0)
        after = lax.cumsum(log_1m, axis=3, reverse=True) - log_1m
        a = jnp.where(mask, jnp.exp(jax.nn.log_sigmoid(z) + after), 0.0)
        return jnp.einsum('bhqk,bkhd->bqhd', a.astype(v.dtype), v)

    return unblock(lax.map(block, jnp.arange(S // Q_BLOCK))).reshape(B, S, D_GROUP)

def hybrid_mixer(x, w_in, mla_q_norm, mla_w_uq, mla_kv_norm, mla_w_ukv, nsa_cmp_pos,
                 nsa_cmp_wk1, nsa_cmp_wk2, nsa_cmp_wv1, nsa_cmp_wv2, group_norm_g, w_out,
                 cos_h, sin_h, cos_r, sin_r, cos_i, sin_i):
    B, S, _ = x.shape
    h = split_columns(x @ w_in)
    y_a = mla_mixer(h['mla_cq'], h['mla_ckv'], h['mla_krope'], mla_q_norm, mla_w_uq,
                    mla_kv_norm, mla_w_ukv, cos_r, sin_r)
    y_b = nsa_mixer(h['nsa_q'], h['nsa_k_cmp'], h['nsa_v_cmp'], h['nsa_k_slc'], h['nsa_v_slc'],
                    h['nsa_k_win'], h['nsa_v_win'], h['nsa_gate'], nsa_cmp_pos,
                    nsa_cmp_wk1, nsa_cmp_wk2, nsa_cmp_wv1, nsa_cmp_wv2, cos_h, sin_h)
    y_c = dsa_mixer(h['dsa_q'], h['dsa_k'], h['dsa_v'], h['idx_q'], h['idx_k'], h['idx_w'],
                    cos_h, sin_h, cos_i, sin_i)
    y_d = stick_breaking_mixer(h['sb_q'], h['sb_k'], h['sb_v'])
    y = jnp.concatenate([y_a, y_b, y_c, y_d], axis=-1).reshape(B, S, N_GROUPS, D_GROUP)
    y = rms_norm_2(y, group_norm_g.reshape(N_GROUPS, D_GROUP)).reshape(B, S, D_MIX)
    return y @ w_out

def second_inputs(seed: int = 0) -> dict:
    key = jax.random.key(seed)
    keys = jax.random.split(key, 32)
    counter = [0]

    def nrm(shape, scale):
        k = keys[counter[0]]
        counter[0] += 1
        return jax.random.normal(k, shape, jnp.float32) * scale

    def gain(shape):
        return 1.0 + nrm(shape, 0.02)

    L, D = DEPTH_2, D_MODEL
    return {
        'x': nrm((BATCH, SEQ, D), 1.0),
        'ln1_g': gain((L, D)),
        'ln1_b': nrm((L, D), 0.02),
        'ffn1_w1': nrm((L, D, D_FF_2), D ** -0.5),
        'ffn1_w3': nrm((L, D, D_FF_2), D ** -0.5),
        'ffn1_w2': nrm((L, D_FF_2, D), DN_BETA * D_FF_2 ** -0.5),
        'w_in': nrm((L, D, D_IN), D ** -0.5),
        'mla_q_norm': gain((L, MLA_Q_RANK)),
        'mla_w_uq': nrm((L, MLA_Q_RANK, HEADS * (MLA_D_NOPE + MLA_D_ROPE)), MLA_Q_RANK ** -0.5),
        'mla_kv_norm': gain((L, MLA_KV_RANK)),
        'mla_w_ukv': nrm((L, MLA_KV_RANK, HEADS * (MLA_D_NOPE + MLA_D_V)), MLA_KV_RANK ** -0.5),
        'nsa_cmp_pos': nrm((L, NSA_CMP_LEN, HEAD_DIM), 0.1),
        'nsa_cmp_wk1': nrm((L, NSA_CMP_LEN * HEAD_DIM, HEAD_DIM), (NSA_CMP_LEN * HEAD_DIM) ** -0.5),
        'nsa_cmp_wk2': nrm((L, HEAD_DIM, HEAD_DIM), HEAD_DIM ** -0.5),
        'nsa_cmp_wv1': nrm((L, NSA_CMP_LEN * HEAD_DIM, HEAD_DIM), (NSA_CMP_LEN * HEAD_DIM) ** -0.5),
        'nsa_cmp_wv2': nrm((L, HEAD_DIM, HEAD_DIM), HEAD_DIM ** -0.5),
        'group_norm_g': gain((L, D_MIX)),
        'w_out': nrm((L, D_MIX, D), DN_BETA * D_MIX ** -0.5),
        'ln2_g': gain((L, D)),
        'ln2_b': nrm((L, D), 0.02),
        'ffn2_w1': nrm((L, D, D_FF_2), D ** -0.5),
        'ffn2_w3': nrm((L, D, D_FF_2), D ** -0.5),
        'ffn2_w2': nrm((L, D_FF_2, D), DN_BETA * D_FF_2 ** -0.5),
        'ln3_g': gain((L, D)),
        'ln3_b': nrm((L, D), 0.02),
    }

def second_block(x, ln1_g, ln1_b, ffn1_w1, ffn1_w3, ffn1_w2, w_in, mla_q_norm, mla_w_uq,
              mla_kv_norm, mla_w_ukv, nsa_cmp_pos, nsa_cmp_wk1, nsa_cmp_wk2, nsa_cmp_wv1,
              nsa_cmp_wv2, group_norm_g, w_out, ln2_g, ln2_b, ffn2_w1, ffn2_w3, ffn2_w2,
              ln3_g, ln3_b):
    S = x.shape[1]
    cos_h, sin_h = rope_tables(S, HEAD_DIM)
    cos_r, sin_r = rope_tables(S, MLA_D_ROPE)
    cos_i, sin_i = rope_tables(S, DSA_IDX_DIM)
    for l in range(DEPTH_2):
        x = layer_norm(DN_ALPHA * x + 0.5 * swiglu(x, ffn1_w1[l], ffn1_w3[l], ffn1_w2[l]),
                       ln1_g[l], ln1_b[l])
        y = hybrid_mixer(x, w_in[l], mla_q_norm[l], mla_w_uq[l], mla_kv_norm[l], mla_w_ukv[l],
                         nsa_cmp_pos[l], nsa_cmp_wk1[l], nsa_cmp_wk2[l], nsa_cmp_wv1[l],
                         nsa_cmp_wv2[l], group_norm_g[l], w_out[l],
                         cos_h, sin_h, cos_r, sin_r, cos_i, sin_i)
        x = layer_norm(DN_ALPHA * x + y, ln2_g[l], ln2_b[l])
        x = layer_norm(DN_ALPHA * x + 0.5 * swiglu(x, ffn2_w1[l], ffn2_w3[l], ffn2_w2[l]),
                       ln3_g[l], ln3_b[l])
    return x


def setup_inputs(seed=0):
    out = dict(first_inputs(seed))
    for name, value in second_inputs(seed + 1).items():
        if name != "x":
            out[name + "_2"] = value
    return out


def reference(
    x, norm1_g, w_in, b_in, ml_norm_g, fx_qnorm_g, fx_knorm_g, lru_conv_w, lru_conv_b, lru_wa,
    lru_ba, lru_wx, lru_bx, lru_lambda, gla_w_alpha, gla_b_alpha, gla_norm_g, w_branch, w_o,
    norm2_g, w_up, w_down, ln1_g_2, ln1_b_2, ffn1_w1_2, ffn1_w3_2, ffn1_w2_2, w_in_2,
    mla_q_norm_2, mla_w_uq_2, mla_kv_norm_2, mla_w_ukv_2, nsa_cmp_pos_2, nsa_cmp_wk1_2,
    nsa_cmp_wk2_2, nsa_cmp_wv1_2, nsa_cmp_wv2_2, group_norm_g_2, w_out_2, ln2_g_2, ln2_b_2,
    ffn2_w1_2, ffn2_w3_2, ffn2_w2_2, ln3_g_2, ln3_b_2,
):
    x = first_block(
        x, norm1_g, w_in, b_in, ml_norm_g, fx_qnorm_g, fx_knorm_g, lru_conv_w, lru_conv_b,
        lru_wa, lru_ba, lru_wx, lru_bx, lru_lambda, gla_w_alpha, gla_b_alpha, gla_norm_g,
        w_branch, w_o, norm2_g, w_up, w_down,
    )
    return second_block(
        x, ln1_g_2, ln1_b_2, ffn1_w1_2, ffn1_w3_2, ffn1_w2_2, w_in_2, mla_q_norm_2, mla_w_uq_2,
        mla_kv_norm_2, mla_w_ukv_2, nsa_cmp_pos_2, nsa_cmp_wk1_2, nsa_cmp_wk2_2, nsa_cmp_wv1_2,
        nsa_cmp_wv2_2, group_norm_g_2, w_out_2, ln2_g_2, ln2_b_2, ffn2_w1_2, ffn2_w3_2,
        ffn2_w2_2, ln3_g_2, ln3_b_2,
    )


_drawn_inputs = setup_inputs


def setup_inputs(seed=0):
    import zlib

    import numpy as np

    out = dict(_drawn_inputs(seed))
    spreads = {}
    factors = {'mla_q_norm_2': 8.0, 'mla_kv_norm_2': 8.0, 'group_norm_g_2': 4.961}
    for name, (base, spread) in spreads.items():
        noise = np.random.default_rng([zlib.crc32(name.encode()), seed]).standard_normal(out[name].shape)
        drawn = base * np.exp(spread * noise) if base else spread * noise
        out[name] = jnp.asarray(drawn.astype(out[name].dtype))
    for name, factor in factors.items():
        out[name] = (out[name] * factor).astype(out[name].dtype)
    return out
```

```python
from contextlib import ExitStack

import numpy as np

import concourse.bass as bass
from concourse import mybir

F32 = mybir.dt.float32
ALU = mybir.AluOpType
ACT = mybir.ActivationFunctionType
AX = mybir.AxisListType.X

P = 128
T = 512
QB = T // P
D = 1024
KD = D // P
NEG = -1e30
TAKEN = -3e38

BW = 512
FF1 = 4096
HEADS = 4
GLA_TAU = 16.0
LRU_C = 8.0
CHUNK = 64
NCHUNK = T // CHUNK
RMS_EPS, LN_EPS = 1e-6, 1e-5
W1 = (512, 512, 512, 512, 4, 4, 512, 512, 512, 4, 512, 512, 256, 256, 512, 512, 16, 4096)
O1 = np.concatenate([[0], np.cumsum(W1)])
(MQ, MK, MV, MO, MI, MF, FQ, FK, FV, FFG, RX, RY, GQ, GK, GV, GG, GA, GATES) = [int(o) for o in O1[:-1]]

LAYERS = 2
FF2 = 2816
KF2 = FF2 // P
ALPHA = (2.0 * LAYERS) ** 0.25
W2 = (256, 128, 32, 256, 64, 64, 64, 64, 64, 64, 12, 256, 64, 64, 256, 32, 8, 256, 256, 256)
O2 = np.concatenate([[0], np.cumsum(W2)])
(CQ, CKV, KROPE, NQ, NKC, NVC, NKS, NVS, NKW, NVW, NGATE, DQ, DK, DV, IQ, IK, IW, SQ, SK, SV) = [
    int(o) for o in O2[:-1]]
NCMP, CMP_LEN, CMP_STRIDE = 31, 32, 16
TOPK = T // 4
IDX_HEADS = 8
VS0, VW0, VD0, VB0, GT0, IW0 = 0, 64, 128, 192, 448, 460

SLAB = 16
RING = 4


class Stream:

    def __init__(self):
        self.tiles = []

    def align(self, n):
        while len(self.tiles) % n:
            self.tiles.append(None)

    def add(self, pieces):
        at = len(self.tiles)
        self.tiles.extend(pieces)
        return at

    def columns(self, name, layer, depth, cols):
        at = len(self.tiles)
        for k in range(depth):
            self.tiles.append([(name, layer, k * P, m, 0, c, P, n) for c, m, n in cols])
        return at

    def wide(self, name, layer, depth, cols):
        self.align(SLAB)
        at = len(self.tiles)
        for k in range(depth):
            for q in range(4):
                part = []
                for c, m, n in cols:
                    a, b = max(c, q * P), min(c + n, (q + 1) * P)
                    if a < b:
                        part.append((name, layer, k * P, m + a - c, 0, a - q * P, P, b - a))
                self.tiles.append(part)
        return at


def plan():
    s = Stream()
    w = {}
    one = lambda name, layer, depth, col, n: [
        s.columns(name, layer, depth, [(0, col + P * j, P)]) for j in range(n)]
    w["mv"], w["fv"], w["gv"] = [s.wide("w_in", 0, KD, [(0, c, 512)]) for c in (MV, FV, GV)]
    w["small"] = s.columns("w_in", 0, KD, [(0, MF, 4), (32, FFG, 4), (96, GA, 16)])
    w["mi"] = s.columns("w_in", 0, KD, [(0, MI, 4)])
    w["mq"] = one("w_in", 0, KD, MQ, 4)
    w["mk"] = one("w_in", 0, KD, MK, 4)
    w["mo"] = one("w_in", 0, KD, MO, 4)
    w["fq"] = one("w_in", 0, KD, FQ, 4)
    w["fk"] = one("w_in", 0, KD, FK, 4)
    w["rx"] = one("w_in", 0, KD, RX, 4)
    w["ry"] = one("w_in", 0, KD, RY, 4)
    for key, name in (("wa", "lru_wa"), ("wx", "lru_wx")):
        w[key] = [s.add([[(name, 0, (2 * j, 0), 0, 0, 0, 64, 64), (name, 0, (2 * j + 1, 0), 0, 64, 64, 64, 64)]])
                  for j in range(4)]
    w["gq"] = one("w_in", 0, KD, GQ, 2)
    w["gk"] = one("w_in", 0, KD, GK, 2)
    w["gg"] = one("w_in", 0, KD, GG, 4)
    w["walpha"] = [s.add([[("gla_w_alpha", 0, 0, P * j, 96, 0, 16, P)]]) for j in range(2)]
    w["merge"] = []
    for d in range(KD):
        for n in range(4):
            g = s.columns("w_in", 0, KD, [(0, GATES + D * n + P * d, P)])
            b = len(s.tiles)
            for k in range(4):
                s.tiles.append([("w_branch", 0, (n, k * P), P * d, 0, 0, P, P)])
            w["merge"].append((g, b))
    w["wo"] = one("w_o", 0, KD, 0, KD)
    w["up"] = one("w_up", 0, KD, 0, FF1 // P)
    w["down"] = one("w_down", 0, FF1 // P, 0, KD)
    s.align(SLAB)
    w["layers"] = []
    for l in range(LAYERS):
        v = {}

        def ffn(n):
            up = []
            for f in range(KF2):
                up.append(tuple(s.columns(f"ffn{n}_{m}_2", l, KD, [(0, P * f, P)]) for m in ("w1", "w3")))
            down = [s.columns(f"ffn{n}_w2_2", l, KF2, [(0, P * j, P)]) for j in range(KD)]
            return up, down

        v["ffn1"] = ffn(1)
        v["v"] = s.wide("w_in_2", l, KD, [(VS0, NVS, 64), (VW0, NVW, 64), (VD0, DV, 64), (VB0, SV, 256),
                                          (GT0, NGATE, 12), (IW0, IW, 8)])
        two = lambda c: [(0, c, 64), (64, c, 64)]
        for key, cols in (
            ("cq0", [(0, CQ, P)]), ("cq1", [(0, CQ + P, P)]), ("ckv", [(0, CKV, P)]),
            ("krope", [(64, KROPE, 32)]), ("kvcmp", [(0, NKC, 64), (64, NVC, 64)]),
            ("iq0", [(0, IQ, P)]), ("iq1", [(0, IQ + P, P)]), ("ik", [(32 * i, IK, 32) for i in range(4)]),
            ("nq0", [(0, NQ, P)]), ("nq1", [(0, NQ + P, P)]), ("ks", two(NKS)), ("kw", two(NKW)),
            ("dq0", [(0, DQ, P)]), ("dq1", [(0, DQ + P, P)]), ("dk", two(DK)),
            ("sq0", [(0, SQ, P)]), ("sq1", [(0, SQ + P, P)]), ("sk0", [(0, SK, P)]), ("sk1", [(0, SK + P, P)]),
        ):
            v[key] = s.columns("w_in_2", l, KD, cols)
        v["uq"] = [s.columns("mla_w_uq_2", l, 2, [(0, 96 * h, 96)]) for h in range(HEADS)]
        v["uk"] = [s.columns("mla_w_ukv_2", l, 1, [(0, 128 * h, 64)]) for h in range(HEADS)]
        s.align(2)
        v["uv"] = s.add([[("mla_w_ukv_2", l, 0, 128 * (2 * i + j) + 64, 0, 64 * j, P, 64) for j in range(2)]
                         for i in range(2)])
        v["c2"] = s.add([[("nsa_cmp_wk2_2", l, 0, 0, 0, 0, 64, 64), ("nsa_cmp_wk2_2", l, 0, 0, 0, 64, 64, 64),
                          ("nsa_cmp_wv2_2", l, 0, 0, 64, 0, 64, 64)]])
        v["c1"] = s.add([[(f"nsa_cmp_w{m}1_2", l, 64 * (2 * i + j), 0, r, 64 * j, 64, 64)
                          for m, r in (("k", 0), ("v", 64)) for j in range(2)] for i in range(16)])
        v["wout"] = [s.columns("w_out_2", l, KD, [(0, P * j, P)]) for j in range(KD)]
        v["ffn2"] = ffn(2)
        s.align(SLAB)
        w["layers"].append(v)
    s.align(SLAB)
    return s, w


STREAM, WHERE = plan()
NSLABS = len(STREAM.tiles) // SLAB


class Columns:

    def __init__(self):
        self.at, self.n = {}, 0

    def add(self, name, n):
        self.at[name] = (self.n, n)
        self.n += n


CONST = Columns()
for _n, _w in (("ident", P), ("ones", P), ("negident", 4), ("negroot", 4), ("rot_h2", P), ("rot_i4", P), ("rot_mq", P),
               ("rot_cmp", P), ("cos_h2", T), ("sin_h2", T), ("cos_i4", T), ("sin_i4", T), ("cos_mq", T),
               ("sin_mq", T), ("cos_cmp", T), ("sin_cmp", T), ("causal", T), ("strict", T), ("tri", P),
               ("chunk_tri", P), ("cmp_neg", QB * NCMP), ("cmp_keep", QB * NCMP), ("goes_on", T),
               ("rms_eps", 1), ("ln_eps", 1), ("one", 1)):
    CONST.add(_n, _w)

VEC1 = Columns()
for _n, _w in (("norm1_g", 8), ("norm2_g", 8), ("b_mq", 4), ("b_mk", 4), ("b_mo", 4), ("b_fq", 4), ("b_fk", 4),
               ("b_rx", 4), ("b_ry", 4), ("b_gq", 2), ("b_gk", 2), ("b_gg", 4), ("b_small", 1), ("b_mi", 1),
               ("b_gates", 32), ("ml_g", 4), ("gla_g", 4), ("fxq_g", 1), ("fxk_g", 1), ("conv_w", 16),
               ("conv_b", 4), ("lru_ba", 4), ("lru_bx", 4), ("lam", 4), ("b_alpha", 2), ("decay", 4), ("tmp", 4)):
    VEC1.add(_n, _w)
VEC2 = Columns()
for _n, _w in (("ln1_g", 8), ("ln1_b", 8), ("q_g", 2), ("kv_g", 1), ("group_g", 8), ("ln2_g", 8), ("ln2_b", 8),
               ("ln3_g", 8), ("ln3_b", 8), ("pos", CMP_LEN)):
    VEC2.add(_n, _w)
NVEC = max(VEC1.n, VEC2.n)
BROW = 3 * 512


def constants():
    c = np.zeros((P, CONST.n), np.float32)

    def put(name, a):
        at, n = CONST.at[name]
        c[: a.shape[0], at:at + n] = a

    put("ident", np.eye(P))
    put("ones", np.ones((P, P)))
    put("negident", -np.eye(4))
    put("negroot", -np.eye(4) * np.sqrt(128.0))

    def rotation(spans):
        r = np.zeros((P, P))
        for a, n in spans:
            for i in range(n // 2):
                r[a + n // 2 + i, a + i] = -1
                r[a + i, a + n // 2 + i] = 1
        return r

    def tables(spans):
        cos, sin = np.ones((P, T)), np.zeros((P, T))
        for a, n in spans:
            inv = np.float32(10000.0) ** (-np.arange(0, n, 2, dtype=np.float32) / np.float32(n))
            ang = (np.arange(T, dtype=np.float32)[None, :] * inv.astype(np.float32)[:, None]).astype(np.float32)
            for half in range(2):
                cos[a + half * n // 2:a + (half + 1) * n // 2] = np.cos(ang.astype(np.float64))
                sin[a + half * n // 2:a + (half + 1) * n // 2] = np.sin(ang.astype(np.float64))
        return cos, sin

    for kind, spans in (("h2", [(0, 64), (64, 64)]), ("i4", [(32 * i, 32) for i in range(4)]),
                        ("mq", [(64, 32)]), ("cmp", [(0, 64)])):
        put("rot_" + kind, rotation(spans))
        cos, sin = tables(spans)
        put("cos_" + kind, cos)
        put("sin_" + kind, sin)
    i = np.arange(P)
    before = np.zeros((P, T - P))
    put("causal", np.concatenate([before, np.where(i[None, :] <= i[:, None], 0, NEG)], 1))
    put("strict", np.concatenate([before, np.where(i[None, :] < i[:, None], 0, NEG)], 1))
    put("tri", (i[:, None] <= i[None, :]).astype(float))
    put("chunk_tri", ((i[:, None] <= i[None, :]) & (i[:, None] // CHUNK == i[None, :] // CHUNK)).astype(float))
    ends = np.arange(NCMP) * CMP_STRIDE + CMP_LEN - 1
    seen = ends[None, None, :] <= (np.arange(QB)[None, :, None] * P + i[:, None, None])
    put("cmp_keep", seen.astype(float).reshape(P, -1))
    put("cmp_neg", np.where(seen, 0, NEG).reshape(P, -1))
    put("goes_on", np.tile((np.arange(T) % CHUNK != 0).astype(float), (P, 1)))
    put("rms_eps", np.full((P, 1), RMS_EPS))
    put("ln_eps", np.full((P, 1), LN_EPS))
    put("one", np.ones((P, 1)))
    return c


class Signal:

    def __init__(self, sem):
        self, self.base = sem, 0


def wait(eng, signal, count):
    assert count >= 1
    eng.wait_ge(signal, signal.base + count)


class Core:

    def __init__(self, nc, ctx, weights):
        self.nc, self.ctx, self.weights = nc, ctx, weights
        sb = lambda name, shape: ctx.enter_context(nc.sbuf_tensor(name, shape, F32))
        self.x = sb("x_resid", [P, KD, T])
        self.act = sb("act", [P, KD, T])
        self.big = sb("big", [P, 44, T])
        self.scr = sb("scratch", [P, 12, T])
        self.ring = sb("ring", [P, RING, SLAB * P])
        self.const = sb("const_cols", [P, CONST.n])
        self.vec = sb("vector_cols", [P, NVEC])
        self.stat = sb("stats", [P, 2, 64])
        self.ps = ctx.enter_context(nc.psum_tensor("ps", [P, 8, T], F32))
        self.flags = {}
        self.base = {}
        self.slab_loaded = [ctx.enter_context(nc.semaphore(f"slab_loaded{i}")) for i in range(RING)]
        self.sums_done = self.flag("sums_done")
        self.loaded = 0
        self.last_sum = {}
        self.sums = 0
        self.seen_slab = -1
        self.vec_cols = VEC1

    def flag(self, name):
        if name not in self.flags:
            self.flags[name] = self.ctx.enter_context(self.nc.semaphore(name))
            self.base[name] = 0
        return self.flags[name]

    def at(self, flag, count):
        assert count >= 1
        return next(self.base[name] for name, f in self.flags.items() if f is flag) + count

    def passed(self, **counts):
        for name, n in counts.items():
            self.base[name] += n

    def c(self, name, rows=P):
        at, n = CONST.at[name]
        return self.const[0:rows, at:at + n]

    def v(self, name, j=0, n=1):
        at, _ = self.vec_cols.at[name]
        return self.vec[:, at + j:at + j + n]

    def wtile(self, i, n=1):
        slab, k = divmod(i, SLAB)
        return self.ring[:, slab % RING, k * P:(k + n) * P]

    def use(self, jobs):
        for j, tiles in enumerate(jobs):
            for i in tiles:
                self.last_sum[i // SLAB] = self.sums + j + 1
        self.sums += len(jobs)

    def load_slabs(self, sp):
        last = max(self.last_sum) if self.last_sum else 0
        while self.loaded < min(NSLABS, last + RING):
            n = self.loaded
            if n >= RING:
                sp.wait_ge(self.sums_done, self.last_sum[n - RING])
            sp.dma_start(self.ring[:, n % RING, :], self.weights[n]).then_inc(self.slab_loaded[n % RING], 16)
            self.loaded += 1

    def need(self, pe, i):
        slab = i // SLAB
        if self.seen_slab < slab:
            pe.wait_ge(self.slab_loaded[slab % RING], 16 * (slab // RING + 1))
            self.seen_slab = slab


def cols_of(job):
    return [m[2] for m in job["sum"] if m[2] is not None]


def gemm_phase(k, jobs):
    nc = k.nc
    base = k.sums
    k.use([cols_of(j) for j in jobs])
    taken, rotated, joined, part = [k.flag(n) for n in ("taken", "rotated", "joined", "rope_part")]
    ropes = [j for j, job in enumerate(jobs) if job.get("rope")]
    done = lambda eng, j: eng.wait_ge(k.sums_done, base + j + 1)

    with nc.Block() as block:
        @block.sync
        def _(sp):
            k.load_slabs(sp)

        @block.tensor
        def _(pe):

            def rotate(r):
                job = jobs[ropes[r]]
                pe.wait_ge(taken, k.at(taken, ropes[r] + 1))
                if r >= 2:
                    pe.wait_ge(joined, k.at(joined, r - 1))
                nc.tensor.matmul(k.ps[:, 4 + r % 2, :], k.c("rot_" + job["rope"]), job["out"],
                                 start=True, stop=True).then_inc(rotated, 1)

            for j, job in enumerate(jobs):
                if j >= 4:
                    pe.wait_ge(taken, k.at(taken, j - 3))
                out = k.ps[0:job.get("rows", P), j % 4, 0:job.get("n", T)]
                last = len(job["sum"]) - 1
                for m, (lhsT, rhs, i) in enumerate(job["sum"]):
                    if i is not None:
                        k.need(pe, i)
                    mm = nc.tensor.matmul(out, lhsT, rhs, start=(m == 0), stop=(m == last))
                mm.then_inc(k.sums_done, 1)
                if j - 1 in ropes:
                    rotate(ropes.index(j - 1))
            if len(jobs) - 1 in ropes:
                rotate(len(ropes) - 1)

        @block.scalar
        def _(act):
            for j, job in enumerate(jobs):
                done(act, j)
                rows = job.get("rows", P)
                nc.scalar.activation(job["out"], k.ps[0:rows, j % 4, 0:job.get("n", T)],
                                     job.get("func", ACT.Identity), bias=job.get("bias", 0.0),
                                     scale=job.get("scale", 1.0)).then_inc(taken, 1)

        if ropes:
            @block.vector
            def _(dve):
                for r, j in enumerate(ropes):
                    job = jobs[j]
                    turned = k.scr[:, 10 + r % 2, :]
                    dve.wait_ge(rotated, k.at(rotated, r + 1))
                    nc.vector.tensor_tensor(turned, k.ps[:, 4 + r % 2, :], k.c("sin_" + job["rope"]),
                                            ALU.mult).then_inc(part, 1)
                    nc.vector.tensor_tensor(job["out"], job["out"], k.c("cos_" + job["rope"]),
                                            ALU.mult).then_inc(part, 1)
                    dve.wait_ge(part, k.at(part, 2 * r + 2))
                    nc.vector.tensor_tensor(job["out"], job["out"], turned, ALU.add).then_inc(joined, 1)
    k.passed(taken=len(jobs), rotated=len(ropes), joined=len(ropes), rope_part=2 * len(ropes))


def rms_phase(k, groups, eps, width, post=1.0):
    nc = k.nc
    squared, summed, rooted, normed, step = [k.flag(n) for n in (
        "squared", "summed", "rooted", "normed", "norm_step")]
    flat = [(g, t) for g, group in enumerate(groups) for t in group]
    first = [sum(len(x) for x in groups[:g]) for g in range(len(groups) + 1)]
    gates = sum(1 for _, t in flat if t[3] is not None)
    with nc.Block() as block:
        @block.scalar
        def _(act):
            def roots(g):
                inv = k.scr[:, 8 + g % 2, :]
                act.wait_ge(summed, k.at(summed, first[g + 1]))
                if g >= 2:
                    act.wait_ge(normed, k.at(normed, first[g - 1]))
                nc.scalar.activation(inv, k.ps[:, g % 2, :], ACT.Ln, bias=k.c(eps), scale=1.0 / width)\
                    .then_inc(step, 1)
                act.wait_ge(step, k.at(step, g + 1))
                nc.scalar.activation(inv, inv, ACT.Exp, scale=-0.5).then_inc(rooted, 1)

            for n, (g, t) in enumerate(flat):
                if n >= 4:
                    act.wait_ge(summed, k.at(summed, n - 3))
                nc.scalar.activation(k.scr[:, n % 4, :], t[0], ACT.Square).then_inc(squared, 1)
                if g >= 1 and n == first[g]:
                    roots(g - 1)
            roots(len(groups) - 1)

        @block.tensor
        def _(pe):
            for n, (g, t) in enumerate(flat):
                if g >= 2 and n == first[g]:
                    pe.wait_ge(rooted, k.at(rooted, g - 1))
                pe.wait_ge(squared, k.at(squared, n + 1))
                nc.tensor.matmul(k.ps[:, g % 2, :], k.c("ones"), k.scr[:, n % 4, :], start=(n == first[g]),
                                 stop=(n == first[g + 1] - 1)).then_inc(summed, 1)

        @block.vector
        def _(dve):
            gated = 0
            for n, (g, (src, out, gain, gate)) in enumerate(flat):
                inv = k.scr[:, 8 + g % 2, :]
                dve.wait_ge(rooted, k.at(rooted, g + 1))
                if gate is None:
                    nc.vector.scalar_tensor_tensor(out, src, gain, inv, ALU.mult, ALU.mult)\
                        .then_inc(normed, 1)
                else:
                    nc.vector.scalar_tensor_tensor(out, src, gain, inv, ALU.mult, ALU.mult)\
                        .then_inc(k.flag("ungated"), 1)
                    gated += 1
                    dve.wait_ge(k.flag("ungated"), k.at(k.flag("ungated"), gated))
                    nc.vector.tensor_tensor(out, out, gate, ALU.mult).then_inc(normed, 1)
    k.flag("ungated")
    k.passed(squared=len(flat), summed=len(flat), rooted=len(groups), norm_step=len(groups),
             normed=len(flat), ungated=gates)


def layernorm_phase(k, gain, shift):
    nc = k.nc
    added, centred, squared, summed, rooted, normed, step, shifted = [k.flag(n) for n in (
        "added", "centred", "squared", "summed", "rooted", "normed", "norm_step", "shifted")]
    with nc.Block() as block:
        @block.tensor
        def _(pe):
            for n in range(KD):
                mm = nc.tensor.matmul(k.ps[:, 0, :], k.c("ones"), k.x[:, n, :], start=(n == 0), stop=(n == KD - 1))
            mm.then_inc(added, 1)
            for n in range(KD):
                pe.wait_ge(squared, k.at(squared, n + 1))
                nc.tensor.matmul(k.ps[:, 1, :], k.c("ones"), k.scr[:, n % 4, :], start=(n == 0),
                                 stop=(n == KD - 1)).then_inc(summed, 1)

        @block.vector
        def _(dve):
            dve.wait_ge(added, k.at(added, 1))
            for n in range(KD):
                nc.vector.scalar_tensor_tensor(k.x[:, n, :], k.ps[:, 0, :], -1.0 / D, k.x[:, n, :], ALU.mult,
                                               ALU.add).then_inc(centred, 1)
            dve.wait_ge(rooted, k.at(rooted, 1))
            for n in range(KD):
                nc.vector.scalar_tensor_tensor(k.x[:, n, :], k.x[:, n, :], k.v(gain, n), k.scr[:, 8, :],
                                               ALU.mult, ALU.mult).then_inc(normed, 1)

        @block.scalar
        def _(act):
            for n in range(KD):
                act.wait_ge(centred, k.at(centred, n + 1))
                if n >= 4:
                    act.wait_ge(summed, k.at(summed, n - 3))
                nc.scalar.activation(k.scr[:, n % 4, :], k.x[:, n, :], ACT.Square).then_inc(squared, 1)
            act.wait_ge(summed, k.at(summed, KD))
            nc.scalar.activation(k.scr[:, 8, :], k.ps[:, 1, :], ACT.Ln, bias=k.c("ln_eps"), scale=1.0 / D)\
                .then_inc(step, 1)
            act.wait_ge(step, k.at(step, 1))
            nc.scalar.activation(k.scr[:, 8, :], k.scr[:, 8, :], ACT.Exp, scale=-0.5).then_inc(rooted, 1)
            for n in range(KD):
                act.wait_ge(normed, k.at(normed, n + 1))
                nc.scalar.activation(k.x[:, n, :], k.x[:, n, :], ACT.Identity, bias=k.v(shift, n))\
                    .then_inc(shifted, 1)
    k.passed(added=1, centred=KD, squared=KD, summed=KD, rooted=1, normed=KD, norm_step=1, shifted=KD)


def glu_phase(k, up, down):
    nc = k.nc
    base = k.sums
    k.use([range(a, a + KD) for pair in up for a in pair] + [range(a, a + KF2) for a in down])
    sigmoid, hidden, resid = [k.flag(n) for n in ("silu_done", "hidden_ready", "resid_added")]
    with nc.Block() as block:
        @block.sync
        def _(sp):
            k.load_slabs(sp)

        @block.tensor
        def _(pe):
            for f, pair in enumerate(up):
                if f >= 2:
                    pe.wait_ge(hidden, k.at(hidden, f - 1))
                for b, at in enumerate(pair):
                    for c in range(KD):
                        k.need(pe, at + c)
                        mm = nc.tensor.matmul(k.ps[:, 2 * (f % 2) + b, :], k.wtile(at + c), k.x[:, c, :],
                                              start=(c == 0), stop=(c == KD - 1))
                    mm.then_inc(k.sums_done, 1)
            for j, at in enumerate(down):
                if j >= 2:
                    pe.wait_ge(resid, k.at(resid, j - 1))
                for c in range(KF2):
                    k.need(pe, at + c)
                    if j == 0:
                        pe.wait_ge(hidden, k.at(hidden, c + 1))
                    mm = nc.tensor.matmul(k.ps[:, 4 + j % 2, :], k.wtile(at + c), k.big[:, c, :],
                                          start=(c == 0), stop=(c == KF2 - 1))
                mm.then_inc(k.sums_done, 1)

        @block.scalar
        def _(act):
            for f in range(KF2):
                act.wait_ge(k.sums_done, base + 2 * f + 1)
                if f >= 2:
                    act.wait_ge(hidden, k.at(hidden, f - 1))
                nc.scalar.activation(k.scr[:, f % 2, :], k.ps[:, 2 * (f % 2), :], ACT.Silu)\
                    .then_inc(sigmoid, 1)

        @block.vector
        def _(dve):
            for f in range(KF2):
                dve.wait_ge(sigmoid, k.at(sigmoid, f + 1))
                dve.wait_ge(k.sums_done, base + 2 * f + 2)
                nc.vector.scalar_tensor_tensor(k.big[:, f, :], k.ps[:, 2 * (f % 2) + 1, :], 0.5,
                                               k.scr[:, f % 2, :], ALU.mult, ALU.mult).then_inc(hidden, 1)
            for j in range(KD):
                dve.wait_ge(k.sums_done, base + 2 * KF2 + j + 1)
                nc.vector.scalar_tensor_tensor(k.x[:, j, :], k.x[:, j, :], ALPHA, k.ps[:, 4 + j % 2, :],
                                               ALU.mult, ALU.add).then_inc(resid, 1)
    k.passed(silu_done=KF2, hidden_ready=KF2, resid_added=KD)


def relu2_phase(k, up, down):
    nc = k.nc
    base = k.sums
    n_up = len(up)
    k.use([range(a, a + KD) for a in up] + [range(a, a + n_up) for a in down])
    relu, hidden, resid = [k.flag(n) for n in ("relu_done", "hidden_ready", "resid_added")]
    with nc.Block() as block:
        @block.sync
        def _(sp):
            k.load_slabs(sp)

        @block.tensor
        def _(pe):
            for f, at in enumerate(up):
                if f >= 4:
                    pe.wait_ge(hidden, k.at(hidden, f - 3))
                for c in range(KD):
                    k.need(pe, at + c)
                    mm = nc.tensor.matmul(k.ps[:, f % 4, :], k.wtile(at + c), k.act[:, c, :],
                                          start=(c == 0), stop=(c == KD - 1))
                mm.then_inc(k.sums_done, 1)
            for j, at in enumerate(down):
                if j >= 2:
                    pe.wait_ge(resid, k.at(resid, j - 1))
                for c in range(n_up):
                    k.need(pe, at + c)
                    if j == 0:
                        pe.wait_ge(hidden, k.at(hidden, c + 1))
                    mm = nc.tensor.matmul(k.ps[:, 4 + j % 2, :], k.wtile(at + c), k.big[:, c, :],
                                          start=(c == 0), stop=(c == n_up - 1))
                mm.then_inc(k.sums_done, 1)

        @block.scalar
        def _(act):
            for f in range(n_up):
                act.wait_ge(k.sums_done, base + f + 1)
                if f >= 2:
                    act.wait_ge(hidden, k.at(hidden, f - 1))
                nc.scalar.activation(k.scr[:, f % 2, :], k.ps[:, f % 4, :], ACT.Relu).then_inc(relu, 1)

        @block.vector
        def _(dve):
            for f in range(n_up):
                dve.wait_ge(relu, k.at(relu, f + 1))
                nc.vector.tensor_tensor(k.big[:, f, :], k.ps[:, f % 4, :], k.scr[:, f % 2, :], ALU.mult)\
                    .then_inc(hidden, 1)
            for j in range(KD):
                dve.wait_ge(k.sums_done, base + n_up + j + 1)
                nc.vector.tensor_tensor(k.x[:, j, :], k.x[:, j, :], k.ps[:, 4 + j % 2, :], ALU.add)\
                    .then_inc(resid, 1)
    k.passed(relu_done=n_up, hidden_ready=n_up, resid_added=KD)


def project_phase(k, tiles, alpha, act):
    nc = k.nc
    base = k.sums
    k.use([range(a, a + KD) for a in tiles])
    resid = k.flag("resid_added")
    with nc.Block() as block:
        @block.sync
        def _(sp):
            k.load_slabs(sp)

        @block.tensor
        def _(pe):
            for j, at in enumerate(tiles):
                if j >= 4:
                    pe.wait_ge(resid, k.at(resid, j - 3))
                for c in range(KD):
                    k.need(pe, at + c)
                    mm = nc.tensor.matmul(k.ps[:, j % 4, :], k.wtile(at + c), act(c),
                                          start=(c == 0), stop=(c == KD - 1))
                mm.then_inc(k.sums_done, 1)

        @block.vector
        def _(dve):
            for j in range(len(tiles)):
                dve.wait_ge(k.sums_done, base + j + 1)
                nc.vector.scalar_tensor_tensor(k.x[:, j, :], k.x[:, j, :], alpha, k.ps[:, j % 4, :],
                                               ALU.mult, ALU.add).then_inc(resid, 1)
    k.passed(resid_added=len(tiles))


def merge_phase(k, tiles, y, out):
    nc = k.nc
    base = k.sums
    k.use([r for g, b in tiles for r in (range(g, g + KD), range(b, b + 4))])
    gate, merged, product = [k.flag(n) for n in ("gate_ready", "merged", "gated_product")]
    n_jobs = len(tiles)
    with nc.Block() as block:
        @block.sync
        def _(sp):
            k.load_slabs(sp)

        @block.tensor
        def _(pe):
            for j, (g, b) in enumerate(tiles):
                if j >= 2:
                    pe.wait_ge(product, k.at(product, j - 1))
                for c in range(KD):
                    k.need(pe, g + c)
                    mm = nc.tensor.matmul(k.ps[:, 2 * (j % 2), :], k.wtile(g + c), k.act[:, c, :],
                                          start=(c == 0), stop=(c == KD - 1))
                mm.then_inc(k.sums_done, 1)
                for c in range(4):
                    k.need(pe, b + c)
                    mm = nc.tensor.matmul(k.ps[:, 2 * (j % 2) + 1, :], k.wtile(b + c), y(j % 4, c),
                                          start=(c == 0), stop=(c == 3))
                mm.then_inc(k.sums_done, 1)

        @block.scalar
        def _(act):
            for j in range(n_jobs):
                act.wait_ge(k.sums_done, base + 2 * j + 1)
                if j >= 2:
                    act.wait_ge(product, k.at(product, j - 1))
                d, n = divmod(j, 4)
                nc.scalar.activation(k.scr[:, j % 2, :], k.ps[:, 2 * (j % 2), :], ACT.Sigmoid,
                                     bias=k.v("b_gates", 8 * n + d)).then_inc(gate, 1)

        @block.vector
        def _(dve):
            for j in range(n_jobs):
                d, n = divmod(j, 4)
                dve.wait_ge(gate, k.at(gate, j + 1))
                dve.wait_ge(k.sums_done, base + 2 * j + 2)
                to = out(d) if n == 0 else k.scr[:, 2 + j % 2, :]
                if n > 0 and j > 4:
                    dve.wait_ge(merged, k.at(merged, j - 1 - (j - 2) // 4 - 1))
                nc.vector.tensor_tensor(to, k.scr[:, j % 2, :], k.ps[:, 2 * (j % 2) + 1, :], ALU.mult)\
                    .then_inc(product, 1)
                if n > 0:
                    dve.wait_ge(product, k.at(product, j + 1))
                    if n > 1:
                        dve.wait_ge(merged, k.at(merged, 3 * d + n - 1))
                    nc.vector.tensor_tensor(out(d), out(d), to, ALU.add).then_inc(merged, 1)
    k.passed(gate_ready=n_jobs, gated_product=n_jobs, merged=3 * n_jobs // 4)


def mlstm_phase(k, q, key, v, f_row, i_row, f_fx, y):
    nc = k.nc
    names = ("soft", "log_f", "run_f", "u_ready", "m_ready", "m_sum", "stabil", "u_turned", "u_col", "fx_copied",
             "max_row", "scored", "arg_ready", "weight", "tri_done", "weighted", "head_summed", "em_row", "abs_den",
             "den_ready", "den_inv", "head_done", "unit_summed")
    s = {n: k.flag(n) for n in names}
    tmp, run_f, u, m, em = [k.scr[:, i, :] for i in range(5)]
    ucol = k.stat[:, 0, 0:16]
    units = [(h, b) for h in range(HEADS) for b in range(QB)]
    n = len(units)
    one = k.c("one").broadcast_to([P, T])
    one4 = k.c("one", 4).broadcast_to([4, T])
    with nc.Block() as block:
        @block.scalar
        def _(act):
            nc.scalar.activation(tmp, f_row, ACT.Abs).then_inc(s["soft"], 1)
            act.wait_ge(s["soft"], k.at(s["soft"], 1))
            nc.scalar.activation(tmp, tmp, ACT.Exp, scale=-1.0).then_inc(s["soft"], 1)
            act.wait_ge(s["soft"], k.at(s["soft"], 2))
            nc.scalar.activation(tmp, tmp, ACT.Ln, bias=1.0).then_inc(s["soft"], 1)
            act.wait_ge(s["m_sum"], k.at(s["m_sum"], 1))
            nc.scalar.activation(em[0:4], em[0:4], ACT.Exp, scale=-1.0).then_inc(s["stabil"], 1)
            act.wait_ge(s["u_turned"], k.at(s["u_turned"], 1))
            nc.scalar.activation(ucol, k.ps[:, 0, 0:16], ACT.Copy).then_inc(s["u_col"], 1)
            for i in range(n + 2):
                if i < n:
                    e = k.scr[:, 6 + i % 2, 0:T - P * units[i][1]]
                    act.wait_ge(s["arg_ready"], k.at(s["arg_ready"], i + 1))
                    nc.scalar.activation(e, e, ACT.Exp).then_inc(s["weight"], 1)
                if i >= 5 and (i - 5) % 4 == 0:
                    h = (i - 5) // 4
                    act.wait_ge(s["head_summed"], k.at(s["head_summed"], h + 1))
                    if h >= 1:
                        act.wait_ge(s["den_ready"], k.at(s["den_ready"], h))
                    nc.scalar.activation(k.scr[:, 10, :], k.ps[:, 6 + h % 2, :], ACT.Abs)\
                        .then_inc(s["abs_den"], 1)

        @block.tensor
        def _(pe):
            pe.wait_ge(s["u_ready"], k.at(s["u_ready"], 1))
            for b in range(QB):
                mm = nc.tensor.transpose(k.ps[:, 0, 4 * b:4 * b + 4], u[0:4, P * b:P * b + P], k.c("ident", 4)[:, 0:4])
            mm.then_inc(s["u_turned"], 1)
            pe.wait_ge(s["m_ready"], k.at(s["m_ready"], 1))
            pe.wait_ge(s["u_col"], k.at(s["u_col"], 1))
            pe.wait_ge(s["stabil"], k.at(s["stabil"], 1))
            for i in range(n + 1):
                if i < n:
                    h, b = units[i]
                    if b == 0:
                        if h >= 2:
                            pe.wait_ge(s["head_done"], k.at(s["head_done"], h - 1))
                        nc.tensor.matmul(k.ps[:, h % 2, :], k.c("negident", 4)[:, h:h + 1].broadcast_to([4, P]),
                                         m[0:4], start=True, stop=True).then_inc(s["max_row"], 1)
                    if i >= 2:
                        pe.wait_ge(s["weighted"], k.at(s["weighted"], i - 1))
                    nc.tensor.matmul(k.ps[:, 2 + i % 2, 0:T - P * b], key(h)[:, P * b:P * b + P], q(h)[:, P * b:T],
                                     start=True, stop=True).then_inc(s["scored"], 1)
                if i >= 1:
                    h, b = units[i - 1]
                    w = k.scr[:, 8 + (i - 1) % 2, 0:T - P * b]
                    pe.wait_ge(s["weighted"], k.at(s["weighted"], i))
                    if b == 0 and h >= 2:
                        pe.wait_ge(s["head_done"], k.at(s["head_done"], h - 1))
                    nc.tensor.matmul(k.ps[:, 4 + h % 2, P * b:T], v(b, h), w, start=(b == 0), stop=(b == QB - 1))
                    nc.tensor.matmul(k.ps[:, 6 + h % 2, P * b:T], k.c("ones"), w, start=(b == 0),
                                     stop=(b == QB - 1)).then_inc(s["unit_summed"], 1)
                    if b == QB - 1:
                        nc.tensor.matmul(k.ps[:, h % 2, :], k.c("ident", 4)[:, h:h + 1].broadcast_to([4, P]),
                                         em[0:4], start=True, stop=True).then_inc(s["head_summed"], 1)

        @block.vector
        def _(dve):
            dve.wait_ge(s["soft"], k.at(s["soft"], 3))
            nc.vector.scalar_tensor_tensor(tmp, f_row, 0.0, tmp, ALU.min, ALU.subtract).then_inc(s["log_f"], 1)
            dve.wait_ge(s["log_f"], k.at(s["log_f"], 1))
            nc.vector.tensor_tensor_scan(run_f, one, tmp, 0.0, ALU.mult, ALU.add).then_inc(s["run_f"], 1)
            dve.wait_ge(s["run_f"], k.at(s["run_f"], 1))
            nc.vector.tensor_copy(f_fx[0:4], run_f[32:36]).then_inc(s["fx_copied"], 1)
            nc.vector.tensor_tensor(u[0:4], i_row[0:4], run_f[0:4], ALU.subtract).then_inc(s["u_ready"], 1)
            dve.wait_ge(s["u_ready"], k.at(s["u_ready"], 1))
            nc.vector.tensor_tensor_scan(m[0:4], one4, u[0:4], 0.0, ALU.mult, ALU.max).then_inc(s["m_ready"], 1)
            dve.wait_ge(s["m_ready"], k.at(s["m_ready"], 1))
            nc.vector.tensor_tensor(em[0:4], run_f[0:4], m[0:4], ALU.add).then_inc(s["m_sum"], 1)
            dve.wait_ge(s["u_col"], k.at(s["u_col"], 1))

            def argument(i):
                h, b = units[i]
                if b == 0:
                    dve.wait_ge(s["max_row"], k.at(s["max_row"], h + 1))
                if i >= 2:
                    dve.wait_ge(s["weighted"], k.at(s["weighted"], i - 1))
                nc.vector.tensor_scalar(k.scr[:, 6 + i % 2, 0:T - P * b], k.ps[:, h % 2, P * b:T],
                                        ucol[:, 4 * b + h:4 * b + h + 1], 0.0, ALU.add, ALU.min)\
                    .then_inc(s["arg_ready"], 1)

            argument(0)
            for i in range(n + 2):
                if i + 1 < n:
                    argument(i + 1)
                if i < n:
                    h, b = units[i]
                    e = k.scr[:, 6 + i % 2, :]
                    dve.wait_ge(s["weight"], k.at(s["weight"], i + 1))
                    nc.vector.tensor_tensor(e[:, 0:P], e[:, 0:P], k.c("tri"), ALU.mult).then_inc(s["tri_done"], 1)
                    dve.wait_ge(s["tri_done"], k.at(s["tri_done"], i + 1))
                    dve.wait_ge(s["scored"], k.at(s["scored"], i + 1))
                    if i >= 2:
                        dve.wait_ge(s["unit_summed"], k.at(s["unit_summed"], i - 1))
                    nc.vector.scalar_tensor_tensor(k.scr[:, 8 + i % 2, 0:T - P * b],
                                                   k.ps[:, 2 + i % 2, 0:T - P * b], P ** -0.5,
                                                   e[:, 0:T - P * b], ALU.mult, ALU.mult)\
                        .then_inc(s["weighted"], 1)
                if i >= 5 and (i - 5) % 4 == 0:
                    h = (i - 5) // 4
                    den = k.scr[:, 11, :]
                    dve.wait_ge(s["abs_den"], k.at(s["abs_den"], h + 1))
                    nc.vector.tensor_tensor(den, k.scr[:, 10, :], k.ps[:, h % 2, :], ALU.max)\
                        .then_inc(s["den_ready"], 1)
                    dve.wait_ge(s["den_ready"], k.at(s["den_ready"], h + 1))
                    nc.vector.reciprocal(den, den).then_inc(s["den_inv"], 1)
                    dve.wait_ge(s["den_inv"], k.at(s["den_inv"], h + 1))
                    nc.vector.tensor_tensor(y(h), den, k.ps[:, 4 + h % 2, :], ALU.mult)\
                        .then_inc(s["head_done"], 1)
    k.passed(soft=3, log_f=1, run_f=1, u_ready=1, m_ready=1, m_sum=1, stabil=1, u_turned=1, u_col=1, fx_copied=1,
             max_row=HEADS, scored=n, arg_ready=n, weight=n, tri_done=n, weighted=n, head_summed=HEADS,
             abs_den=HEADS, den_ready=HEADS, den_inv=HEADS, head_done=HEADS, unit_summed=n)


class Unit:

    def __init__(self, scores, width, values, group, first, last, rows, out, scale, mask=None, keep=None, gate=None):
        self.scores, self.width, self.values = scores, width, values
        self.group, self.first, self.last, self.rows, self.out = group, first, last, rows, out
        self.scale, self.mask, self.keep, self.gate = scale, mask, keep, gate
        self.blocks = [(a, min(P, width - a)) for a in range(0, width, P)]


def attend(k, pe, u, n, units, probs, ready, turned, laid, unit_done, stored):
    nc = k.nc
    if 0 <= u < n:
        pe.wait_ge(ready, k.at(ready, u + 1))
        if u >= 2:
            pe.wait_ge(laid, k.at(laid, u - 1))
        for a, w in units[u].blocks:
            mm = nc.tensor.transpose(k.ps[0:w, 3 + u % 2, a:a + P], probs(u)[:, a:a + w], k.c("ident"))
        mm.then_inc(turned, 1)
    if 0 <= u - 1 < n:
        one = units[u - 1]
        pe.wait_ge(laid, k.at(laid, u))
        if one.first and one.group >= 3:
            pe.wait_ge(stored, k.at(stored, one.group - 2))
        lo, hi = one.rows
        for j, ((a, w), val) in enumerate(zip(one.blocks, one.values)):
            mm = nc.tensor.matmul(k.ps[lo:hi, 5 + one.group % 3, 0:P], val, k.scr[0:w, 6 + (u - 1) % 2, a:a + P],
                                  start=(one.first and j == 0), stop=(one.last and j == len(one.blocks) - 1))
        mm.then_inc(unit_done, 1)


def lay_and_store(k, act, u, n, units, turned, laid, unit_done, stored):
    nc = k.nc
    if 0 <= u < n:
        act.wait_ge(turned, k.at(turned, u + 1))
        if u >= 2:
            act.wait_ge(unit_done, k.at(unit_done, u - 1))
        rows = units[u].blocks[0][1]
        cols = P * len(units[u].blocks)
        nc.scalar.activation(k.scr[0:rows, 6 + u % 2, 0:cols], k.ps[0:rows, 3 + u % 2, 0:cols], ACT.Copy)\
            .then_inc(laid, 1)
    if 0 <= u - 2 < n and units[u - 2].last:
        one = units[u - 2]
        lo, hi = one.rows
        act.wait_ge(unit_done, k.at(unit_done, u - 1))
        nc.scalar.activation(one.out, k.ps[lo:hi, 5 + one.group % 3, 0:P], ACT.Copy).then_inc(stored, 1)


def attention_phase(k, units):
    nc = k.nc
    scored, masked, row_max, expd, row_inv, row_gate, probs_ready, turned, laid, unit_done, stored = [
        k.flag(n) for n in ("scored", "masked", "row_max", "probs_expd", "row_inv", "row_gate", "probs_ready",
                              "turned", "laid", "unit_done", "stored")]
    n = len(units)
    probs = lambda i: k.scr[:, i % 4, :]
    col = lambda kind, i: k.stat[:, kind, i:i + 1]
    gates = [sum(1 for u in units[:i + 1] if u.gate is not None) for i in range(n)]
    groups = sum(1 for u in units if u.last)
    assert n <= 64
    with nc.Block() as block:
        @block.tensor
        def _(pe):
            for i in range(n + 3):
                if i < n:
                    u = units[i]
                    if i >= 3:
                        pe.wait_ge(masked, k.at(masked, i - 2))
                    for j, (lhsT, rhs) in enumerate(u.scores):
                        mm = nc.tensor.matmul(k.ps[:, i % 3, 0:u.width], lhsT, rhs, start=(j == 0),
                                              stop=(j == len(u.scores) - 1))
                    mm.then_inc(scored, 1)
                attend(k, pe, i - 2, n, units, probs, probs_ready, turned, laid, unit_done, stored)

        @block.vector
        def _(dve):
            for i in range(n + 1):
                if i < n:
                    u = units[i]
                    s = probs(i)[:, 0:u.width]
                    dve.wait_ge(scored, k.at(scored, i + 1))
                    if i >= 4:
                        dve.wait_ge(turned, k.at(turned, i - 3))
                    nc.vector.scalar_tensor_tensor(s, k.ps[:, i % 3, 0:u.width], u.scale, u.mask, ALU.mult, ALU.add)\
                        .then_inc(masked, 1)
                    dve.wait_ge(masked, k.at(masked, i + 1))
                    nc.vector.tensor_reduce(col(0, i), s, AX, ALU.max, negate=True).then_inc(row_max, 1)
                if i >= 1:
                    u = units[i - 1]
                    p = probs(i - 1)[:, 0:u.width]
                    inv = col(1, i - 1)
                    dve.wait_ge(expd, k.at(expd, i))
                    nc.vector.reciprocal(inv, inv).then_inc(row_inv, 1)
                    dve.wait_ge(row_inv, k.at(row_inv, i))
                    if u.gate is not None:
                        nc.vector.tensor_tensor(inv, inv, u.gate, ALU.mult).then_inc(row_gate, 1)
                        dve.wait_ge(row_gate, k.at(row_gate, gates[i - 1]))
                    if u.keep is None:
                        nc.vector.tensor_scalar(p, p, inv, None, ALU.mult).then_inc(probs_ready, 1)
                    else:
                        nc.vector.scalar_tensor_tensor(p, p, inv, u.keep, ALU.mult, ALU.mult)\
                            .then_inc(probs_ready, 1)

        @block.scalar
        def _(act):
            for i in range(n + 4):
                if i < n:
                    p = probs(i)[:, 0:units[i].width]
                    act.wait_ge(row_max, k.at(row_max, i + 1))
                    nc.scalar.activation(p, p, ACT.Exp, bias=col(0, i), accum_out=col(1, i)).then_inc(expd, 1)
                lay_and_store(k, act, i - 2, n, units, turned, laid, unit_done, stored)
    k.passed(scored=n, masked=n, row_max=n, probs_expd=n, row_inv=n, row_gate=gates[-1], probs_ready=n, turned=n,
             laid=n, unit_done=n, stored=groups)


def stick_phase(k, units):
    nc = k.nc
    scored, masked, soft, logged, broken, rest, exponent, probs_ready, turned, laid, unit_done, stored = [
        k.flag(n) for n in ("scored", "masked", "soft", "logged", "broken", "rest", "exponent", "probs_ready",
                              "turned", "laid", "unit_done", "stored")]
    n = len(units)
    probs = lambda i: k.scr[:, i % 4, :]
    soft_at = lambda i: k.scr[:, 4 + i % 2, :]
    rest_at = lambda i: k.scr[:, 8 + i % 2, :]
    groups = sum(1 for u in units if u.last)
    with nc.Block() as block:
        @block.tensor
        def _(pe):
            for i in range(n + 4):
                if i < n:
                    u = units[i]
                    if i >= 3:
                        pe.wait_ge(masked, k.at(masked, i - 2))
                    nc.tensor.matmul(k.ps[:, i % 3, 0:u.width], u.scores[0][0], u.scores[0][1], start=True,
                                     stop=True).then_inc(scored, 1)
                attend(k, pe, i - 3, n, units, probs, probs_ready, turned, laid, unit_done, stored)

        @block.vector
        def _(dve):
            for i in range(n + 1):
                if i < n:
                    u = units[i]
                    dve.wait_ge(scored, k.at(scored, i + 1))
                    if i >= 4:
                        dve.wait_ge(turned, k.at(turned, i - 3))
                    nc.vector.scalar_tensor_tensor(probs(i)[:, 0:u.width], k.ps[:, i % 3, 0:u.width], u.scale,
                                                   u.mask, ALU.mult, ALU.add).then_inc(masked, 1)
                if i >= 1:
                    w = units[i - 1].width
                    z, l, r = [x(i - 1)[:, 0:w] for x in (probs, soft_at, rest_at)]
                    dve.wait_ge(logged, k.at(logged, i))
                    nc.vector.scalar_tensor_tensor(l, z, 0.0, l, ALU.max, ALU.add).then_inc(broken, 1)
                    dve.wait_ge(broken, k.at(broken, i))
                    nc.vector.tensor_tensor_scan(r[:, ::-1], k.c("one").broadcast_to([P, w]), l[:, ::-1], 0.0,
                                                 ALU.mult, ALU.add).then_inc(rest, 1)
                    dve.wait_ge(rest, k.at(rest, i))
                    nc.vector.tensor_tensor(z, z, r, ALU.subtract).then_inc(exponent, 1)

        @block.scalar
        def _(act):
            for i in range(n + 5):
                if i < n:
                    w = units[i].width
                    z, l = probs(i)[:, 0:w], soft_at(i)[:, 0:w]
                    act.wait_ge(masked, k.at(masked, i + 1))
                    if i >= 2:
                        act.wait_ge(rest, k.at(rest, i - 1))
                    nc.scalar.activation(l, z, ACT.Abs).then_inc(soft, 1)
                    act.wait_ge(soft, k.at(soft, 2 * i + 1))
                    nc.scalar.activation(l, l, ACT.Exp, scale=-1.0).then_inc(soft, 1)
                    act.wait_ge(soft, k.at(soft, 2 * i + 2))
                    nc.scalar.activation(l, l, ACT.Ln, bias=1.0).then_inc(logged, 1)
                if 1 <= i <= n:
                    p = probs(i - 1)[:, 0:units[i - 1].width]
                    act.wait_ge(exponent, k.at(exponent, i))
                    nc.scalar.activation(p, p, ACT.Exp).then_inc(probs_ready, 1)
                lay_and_store(k, act, i - 3, n, units, turned, laid, unit_done, stored)
    k.passed(scored=n, masked=n, soft=2 * n, logged=n, broken=n, rest=n, exponent=n, probs_ready=n, turned=n,
             laid=n, unit_done=n, stored=groups)


def conv_phase(k, padded, out):
    nc = k.nc
    edge, step = k.flag("edge"), k.flag("conv_step")
    with nc.Block() as block:
        @block.vector
        def _(dve):
            nc.vector.memset(padded[:, :, 0:3], 0.0).then_inc(edge, 1)
            dve.wait_ge(edge, k.at(edge, 1))
            done = 0
            for j in range(4):
                for t in range(4):
                    x = padded[:, j, t:t + T]
                    w = k.v("conv_w", 4 * t + j)
                    if t == 0:
                        nc.vector.tensor_scalar(out(j), x, w, k.v("conv_b", j), ALU.mult, ALU.add)\
                            .then_inc(step, 1)
                    else:
                        dve.wait_ge(step, k.at(step, done))
                        nc.vector.scalar_tensor_tensor(out(j), x, w, out(j), ALU.mult, ALU.add)\
                            .then_inc(step, 1)
                    done += 1
    k.passed(edge=1, conv_step=16)


def lru_phase(k, xc, r, i, ygate, u, sq, y):
    nc = k.nc
    s = {n: k.flag(n) for n in ("soft", "lam_min", "lam_ready", "tanh_done", "a_ready", "a_squared", "one_minus",
                                  "rooted", "gated_in", "u_ready", "scanned", "head_done")}
    tmp = k.v("tmp", 0, 4)
    with nc.Block() as block:
        @block.scalar
        def _(act):
            nc.scalar.activation(tmp, k.v("lam", 0, 4), ACT.Abs).then_inc(s["soft"], 1)
            act.wait_ge(s["soft"], k.at(s["soft"], 1))
            nc.scalar.activation(tmp, tmp, ACT.Exp, scale=-1.0).then_inc(s["soft"], 1)
            act.wait_ge(s["soft"], k.at(s["soft"], 2))
            nc.scalar.activation(tmp, tmp, ACT.Ln, bias=1.0).then_inc(s["soft"], 1)
            act.wait_ge(s["lam_ready"], k.at(s["lam_ready"], 1))
            for j in range(4):
                nc.scalar.activation(u(j), r(j), ACT.Tanh, scale=k.v("decay", j)).then_inc(s["tanh_done"], 1)
            for j in range(4):
                nc.scalar.activation(r(j), r(j), ACT.Exp, scale=k.v("decay", j)).then_inc(s["a_ready"], 1)
            for j in range(4):
                act.wait_ge(s["a_ready"], k.at(s["a_ready"], j + 1))
                nc.scalar.activation(sq(j), r(j), ACT.Square).then_inc(s["a_squared"], 1)
            for j in range(4):
                act.wait_ge(s["one_minus"], k.at(s["one_minus"], j + 1))
                nc.scalar.activation(u(j), u(j), ACT.Sqrt, scale=-1.0).then_inc(s["rooted"], 1)

        @block.vector
        def _(dve):
            dve.wait_ge(s["soft"], k.at(s["soft"], 3))
            nc.vector.scalar_tensor_tensor(tmp, k.v("lam", 0, 4), 0.0, tmp, ALU.min, ALU.subtract)\
                .then_inc(s["lam_min"], 1)
            dve.wait_ge(s["lam_min"], k.at(s["lam_min"], 1))
            nc.vector.tensor_scalar(k.v("decay", 0, 4), tmp, LRU_C, None, ALU.mult).then_inc(s["lam_ready"], 1)
            for j in range(4):
                dve.wait_ge(s["a_squared"], k.at(s["a_squared"], j + 1))
                nc.vector.scalar_tensor_tensor(u(j), sq(j), 1.0, u(j), ALU.add, ALU.mult)\
                    .then_inc(s["one_minus"], 1)
                nc.vector.tensor_tensor(i(j), i(j), xc(j), ALU.mult).then_inc(s["gated_in"], 1)
            for j in range(4):
                dve.wait_ge(s["rooted"], k.at(s["rooted"], j + 1))
                dve.wait_ge(s["gated_in"], k.at(s["gated_in"], j + 1))
                nc.vector.tensor_tensor(u(j), u(j), i(j), ALU.mult).then_inc(s["u_ready"], 1)
                dve.wait_ge(s["u_ready"], k.at(s["u_ready"], j + 1))
                nc.vector.tensor_tensor_scan(y(j), r(j), u(j), 0.0, ALU.mult, ALU.add).then_inc(s["scanned"], 1)
                dve.wait_ge(s["scanned"], k.at(s["scanned"], j + 1))
                nc.vector.tensor_tensor(y(j), y(j), ygate(j), ALU.mult).then_inc(s["head_done"], 1)
    k.passed(soft=3, lam_min=1, lam_ready=1, tanh_done=4, a_ready=4, a_squared=4, one_minus=4, rooted=4, gated_in=4,
             u_ready=4, scanned=4, head_done=4)


def gla_phase(k, q, key, v, z, bc, states, y):
    nc = k.nc
    s = {n: k.flag(n) for n in (
        "soft", "log_f", "run_f", "past", "to_end", "fwd_exp", "back_exp", "end_exp", "q_scaled", "k_scaled", "k_end",
        "end_turned", "end_laid", "added", "state_zero", "state_ready", "scored", "weighted", "unit_summed",
        "stored")}
    fwd = lambda p: k.scr[:, p, :]
    kt = lambda p: k.scr[:, 2 + p, :]
    ke = lambda p: k.scr[:, 4 + p, :]
    ke_tok = lambda p: k.scr[:, 6 + p, :]
    tmp = lambda p: k.scr[:, 10 + p, :]
    at = lambda i: k.scr[:, 8 + i % 2, 0:P]
    chunks = lambda x: x.rearrange("p (c t) -> p c t", t=CHUNK)
    units = [(h, tb) for h in range(HEADS) for tb in range(QB)]
    n = len(units)
    with nc.Block() as block:
        @block.scalar
        def _(act):
            for p in range(2):
                nc.scalar.activation(tmp(p), z(p), ACT.Abs).then_inc(s["soft"], 1)
                act.wait_ge(s["soft"], k.at(s["soft"], 3 * p + 1))
                nc.scalar.activation(tmp(p), tmp(p), ACT.Exp, scale=-1.0).then_inc(s["soft"], 1)
                act.wait_ge(s["soft"], k.at(s["soft"], 3 * p + 2))
                nc.scalar.activation(tmp(p), tmp(p), ACT.Ln, bias=1.0).then_inc(s["soft"], 1)
            for p in range(2):
                act.wait_ge(s["run_f"], k.at(s["run_f"], p + 1))
                nc.scalar.activation(fwd(p), bc(p), ACT.Exp, scale=1.0 / GLA_TAU).then_inc(s["fwd_exp"], 1)
                nc.scalar.activation(kt(p), bc(p), ACT.Exp, scale=-1.0 / GLA_TAU).then_inc(s["back_exp"], 1)
                act.wait_ge(s["to_end"], k.at(s["to_end"], p + 1))
                nc.scalar.activation(ke(p), ke(p), ACT.Exp, scale=1.0 / GLA_TAU).then_inc(s["end_exp"], 1)
            for p in range(2):
                act.wait_ge(s["end_turned"], k.at(s["end_turned"], p + 1))
                nc.scalar.activation(ke_tok(p), k.ps[:, p, :], ACT.Copy).then_inc(s["end_laid"], 1)
            for h in range(HEADS):
                act.wait_ge(s["unit_summed"], k.at(s["unit_summed"], QB * (h + 1)))
                nc.scalar.activation(y(h), k.ps[:, 4 + h, :], ACT.Copy).then_inc(s["stored"], 1)

        @block.vector
        def _(dve):
            nc.vector.memset(states(0, 0), 0.0).then_inc(s["state_zero"], 1)
            nc.vector.memset(states(1, 0), 0.0).then_inc(s["state_zero"], 1)
            for p in range(2):
                dve.wait_ge(s["soft"], k.at(s["soft"], 3 * p + 3))
                nc.vector.scalar_tensor_tensor(z(p), z(p), 0.0, tmp(p), ALU.min, ALU.subtract)\
                    .then_inc(s["log_f"], 1)
                dve.wait_ge(s["log_f"], k.at(s["log_f"], p + 1))
                nc.vector.tensor_tensor_scan(bc(p), k.c("goes_on"), z(p), 0.0, ALU.mult, ALU.add)\
                    .then_inc(s["run_f"], 1)
                dve.wait_ge(s["run_f"], k.at(s["run_f"], p + 1))
                nc.vector.tensor_tensor(chunks(ke(p)), chunks(bc(p))[:, :, CHUNK - 1:CHUNK].broadcast_to(
                    [P, NCHUNK, CHUNK]), chunks(bc(p)), ALU.subtract).then_inc(s["to_end"], 1)
            for p in range(2):
                dve.wait_ge(s["end_exp"], k.at(s["end_exp"], p + 1))
                nc.vector.tensor_tensor(ke(p), ke(p), key(p), ALU.mult).then_inc(s["k_end"], 1)
                nc.vector.tensor_tensor(kt(p), kt(p), key(p), ALU.mult).then_inc(s["k_scaled"], 1)
                nc.vector.scalar_tensor_tensor(q(p), q(p), CHUNK ** -0.5, fwd(p), ALU.mult, ALU.mult)\
                    .then_inc(s["q_scaled"], 1)
            dve.wait_ge(s["state_zero"], k.at(s["state_zero"], 2))
            for c in range(NCHUNK - 1):
                for p in range(2):
                    if c > 0:
                        dve.wait_ge(s["state_ready"], k.at(s["state_ready"], 2 * (c - 1) + p + 1))
                    dve.wait_ge(s["added"], k.at(s["added"], p + 1))
                    nc.vector.scalar_tensor_tensor(
                        states(p, c + 1), states(p, c), fwd(p)[:, CHUNK * (c + 1) - 1:CHUNK * (c + 1)],
                        k.ps[:, 2 * p + c % 2, P * (c // 2):P * (c // 2) + P], ALU.mult, ALU.add)\
                        .then_inc(s["state_ready"], 1)
            for i in range(n):
                dve.wait_ge(s["scored"], k.at(s["scored"], i + 1))
                if i >= 2:
                    dve.wait_ge(s["unit_summed"], k.at(s["unit_summed"], i - 1))
                nc.vector.tensor_tensor(at(i), k.ps[:, i % 2, 0:P], k.c("chunk_tri"), ALU.mult)\
                    .then_inc(s["weighted"], 1)

        @block.tensor
        def _(pe):
            for p in range(2):
                pe.wait_ge(s["k_end"], k.at(s["k_end"], p + 1))
                for tb in range(QB):
                    mm = nc.tensor.transpose(k.ps[:, p, P * tb:P * tb + P], ke(p)[:, P * tb:P * tb + P], k.c("ident"))
                mm.then_inc(s["end_turned"], 1)
            pe.wait_ge(s["end_laid"], k.at(s["end_laid"], 2))
            for p in range(2):
                for c in range(NCHUNK):
                    lo = CHUNK * (c % 2)
                    for hh in range(2):
                        mm = nc.tensor.matmul(
                            k.ps[64 * hh:64 * hh + 64, 2 * p + c % 2, P * (c // 2):P * (c // 2) + P],
                            ke_tok(p)[lo:lo + CHUNK, P * (c // 2) + 64 * hh:P * (c // 2) + 64 * hh + 64],
                            v(c // 2, 2 * p + hh)[lo:lo + CHUNK], start=True, stop=True)
                mm.then_inc(s["added"], 1)
            pe.wait_ge(s["k_scaled"], k.at(s["k_scaled"], 2))
            pe.wait_ge(s["q_scaled"], k.at(s["q_scaled"], 2))
            pe.wait_ge(s["state_ready"], k.at(s["state_ready"], 2 * (NCHUNK - 1)))
            for i in range(n + 1):
                if i < n:
                    h, tb = units[i]
                    p, lo = h // 2, 64 * (h % 2)
                    if i >= 2:
                        pe.wait_ge(s["weighted"], k.at(s["weighted"], i - 1))
                    nc.tensor.matmul(k.ps[:, i % 2, 0:P], kt(p)[lo:lo + 64, P * tb:P * tb + P],
                                     q(p)[lo:lo + 64, P * tb:P * tb + P], start=True, stop=True)\
                        .then_inc(s["scored"], 1)
                if i >= 1:
                    h, tb = units[i - 1]
                    p, lo = h // 2, 64 * (h % 2)
                    pe.wait_ge(s["weighted"], k.at(s["weighted"], i))
                    nc.tensor.matmul(k.ps[:, 4 + h, P * tb:P * tb + P], v(tb, h), at(i - 1), start=True, stop=False)
                    for c in (2 * tb, 2 * tb + 1):
                        mm = nc.tensor.matmul(k.ps[:, 4 + h, CHUNK * c:CHUNK * c + CHUNK],
                                              states(p, c)[lo:lo + 64], q(p)[lo:lo + 64, CHUNK * c:CHUNK * c + CHUNK],
                                              start=False, stop=(c % 2 == 1))
                    mm.then_inc(s["unit_summed"], 1)
    k.flag("past")
    k.passed(soft=6, log_f=2, run_f=2, to_end=2, fwd_exp=2, back_exp=2, end_exp=2, q_scaled=2, k_scaled=2, k_end=2,
             end_turned=2, end_laid=2, added=2, state_zero=2, state_ready=2 * (NCHUNK - 1), scored=n, weighted=n,
             unit_summed=n, stored=HEADS)


def compress_phase(k, kv, blk, w1, w2, hid, kc, vc, gates_in, gates):
    nc = k.nc
    base = k.sums
    k.use([range(w1, w1 + 16), range(w1, w1 + 16), [w2], [w2]])
    blocks, gelu, stored = k.flag("blocks_ready"), k.flag("gelu_done"), k.flag("stored")
    by_token = kv.rearrange("p (m s) -> p s m", s=CMP_STRIDE)
    with nc.Block() as block:
        @block.sync
        def _(sp):
            k.load_slabs(sp)

        @block.vector
        def _(dve):
            for a in range(2):
                pos = k.v("pos", CMP_STRIDE * a, CMP_STRIDE).unsqueeze(2).broadcast_to([P, CMP_STRIDE, NCMP])
                nc.vector.tensor_tensor(blk[:, CMP_STRIDE * a:CMP_STRIDE * (a + 1), :], by_token[:, :, a:a + NCMP], pos,
                                        ALU.add).then_inc(blocks, 1)

        @block.tensor
        def _(pe):
            pe.wait_ge(blocks, k.at(blocks, 2))
            for j, lo in enumerate((0, 64)):
                for l in range(CMP_LEN):
                    k.need(pe, w1 + l // 2)
                    mm = nc.tensor.matmul(k.ps[lo:lo + 64, j, 0:NCMP],
                                          k.wtile(w1 + l // 2)[lo:lo + 64, 64 * (l % 2):64 * (l % 2) + 64],
                                          blk[lo:lo + 64, l, :], start=(l == 0), stop=(l == CMP_LEN - 1))
                mm.then_inc(k.sums_done, 1)
            pe.wait_ge(gelu, k.at(gelu, 2))
            nc.tensor.matmul(k.ps[:, 2, 0:NCMP], k.wtile(w2)[0:64, :], hid[0:64, 0:NCMP], start=True, stop=True)\
                .then_inc(k.sums_done, 1)
            nc.tensor.matmul(k.ps[0:NCMP, 3, 0:64], hid[64:128, 0:NCMP], k.wtile(w2)[64:128, 0:64], start=True,
                             stop=True).then_inc(k.sums_done, 1)

        @block.scalar
        def _(act):
            nc.scalar.activation(gates, gates_in, ACT.Sigmoid).then_inc(stored, 1)
            for j, lo in enumerate((0, 64)):
                act.wait_ge(k.sums_done, base + j + 1)
                nc.scalar.activation(hid[lo:lo + 64, 0:NCMP], k.ps[lo:lo + 64, j, 0:NCMP], ACT.Gelu_apprx_tanh)\
                    .then_inc(gelu, 1)
            act.wait_ge(k.sums_done, base + 3)
            nc.scalar.activation(kc, k.ps[:, 2, 0:NCMP], ACT.Copy).then_inc(stored, 1)
            act.wait_ge(k.sums_done, base + 4)
            nc.scalar.activation(vc, k.ps[0:NCMP, 3, 0:64], ACT.Copy).then_inc(stored, 1)
    k.passed(blocks_ready=2, gelu_done=2, stored=3)


def select_phase(k, iq, ik, weight, select):
    nc = k.nc
    scored, relu, summed, top, taken, made = [k.flag(n) for n in (
        "scored", "relu_done", "index_added", "top8", "top8_taken", "select_made")]
    units = [(qb, h) for qb in range(1, QB) for h in range(IDX_HEADS)]
    rounds = TOPK // 8
    with nc.Block() as block:
        @block.tensor
        def _(pe):
            for i, (qb, h) in enumerate(units):
                lo = 32 * (h % 4)
                if i >= 4:
                    pe.wait_ge(relu, k.at(relu, i - 3))
                nc.tensor.matmul(k.ps[:, i % 4, 0:P * (qb + 1)], iq(h // 4)[lo:lo + 32, P * qb:P * qb + P],
                                 ik[lo:lo + 32, 0:P * (qb + 1)], start=True, stop=True,
                                 tile_position=(lo, 0)).then_inc(scored, 1)

        @block.scalar
        def _(act):
            for i, (qb, h) in enumerate(units):
                act.wait_ge(scored, k.at(scored, i + 1))
                if i >= 8:
                    act.wait_ge(summed, k.at(summed, i - 7 + (i - 8) // 8))
                nc.scalar.activation(k.scr[:, i % 8, 0:P * (qb + 1)], k.ps[:, i % 4, 0:P * (qb + 1)], ACT.Relu,
                                     scale=(IDX_HEADS * 32) ** -0.5).then_inc(relu, 1)

        @block.vector
        def _(dve):
            added = tops = 0
            for i, (qb, h) in enumerate(units):
                w = P * (qb + 1)
                s = select(qb)[:, 0:w]
                r = k.scr[:, i % 8, 0:w]
                dve.wait_ge(relu, k.at(relu, i + 1))
                if h == 0:
                    nc.vector.tensor_scalar(s, r, weight(qb, h), None, ALU.mult).then_inc(summed, 1)
                else:
                    dve.wait_ge(summed, k.at(summed, added))
                    nc.vector.scalar_tensor_tensor(s, r, weight(qb, h), s, ALU.mult, ALU.add)\
                        .then_inc(summed, 1)
                added += 1
                if h < IDX_HEADS - 1:
                    continue
                dve.wait_ge(summed, k.at(summed, added))
                nc.vector.tensor_tensor(s, s, k.c("causal")[:, T - w:T], ALU.add).then_inc(summed, 1)
                added += 1
                dve.wait_ge(summed, k.at(summed, added))
                for _ in range(rounds):
                    best = k.stat[:, 0, 0:8]
                    if tops:
                        dve.wait_ge(taken, k.at(taken, tops))
                    nc.vector.max(best, s).then_inc(top, 1)
                    tops += 1
                    dve.wait_ge(top, k.at(top, tops))
                    nc.vector.match_replace(s, best, s, TAKEN).then_inc(taken, 1)
                dve.wait_ge(taken, k.at(taken, tops))
                nc.vector.tensor_scalar(s, s, TAKEN / 2, NEG, ALU.is_ge, ALU.mult).then_inc(made, 1)
    k.passed(scored=len(units), relu_done=len(units), index_added=9 * (QB - 1), top8=rounds * (QB - 1),
             top8_taken=rounds * (QB - 1), select_made=QB - 1)


def copy_in_phase(k, sources):
    nc = k.nc
    here = k.flag("inputs_here")
    with nc.Block() as block:
        @block.sync
        def _(sp):
            for dst, src in sources:
                sp.dma_start(dst, src).then_inc(here, 16)
            sp.wait_ge(here, k.at(here, 16 * len(sources)))
            k.load_slabs(sp)
    k.passed(inputs_here=16 * len(sources))


def softmax_units(q, key, v, dims, width_of, masks, scale, group0, out, extra=None):
    units = []
    for h in range(HEADS):
        for qb in range(QB):
            w = P * (qb + 1)
            pairs = [(q(h)[:, P * qb:P * qb + P], key(h)[:, 0:w])] + (extra(h, w) if extra else [])
            lo = 64 * (h % 2) if dims == 64 else 0
            units.append(Unit(pairs, w, [v(kb, h) for kb in range(qb + 1)], group0 + QB * h + qb, True, True,
                              (lo, lo + dims), out(h)[lo:lo + dims, P * qb:P * qb + P], scale, mask=masks(qb)))
    return units


def token_job(k, act_tile, at, out, tb, bias=None, n=T, depth=KD, per=4):
    s = [(act_tile(c)[:, P * tb:P * tb + P], k.wtile(at + per * c, per)[:, 0:n], at + per * c) for c in range(depth)]
    if bias is not None:
        s.append((k.c("ones", 1), bias, None))
    return {"sum": s, "out": out, "n": n}


def feature_job(k, act_tile, at, out, depth=KD, **more):
    return {"sum": [(k.wtile(at + c), act_tile(c), at + c) for c in range(depth)], "out": out, **more}


def block_one(k, brow):
    nc, big, scr, w = k.nc, k.big, k.scr, WHERE
    k.vec_cols = VEC1
    act = lambda c: k.act[:, c, :]
    tile = lambda base: (lambda j: big[:, base + j, :])
    value = lambda base: (lambda tb, h: big[:, base + tb, P * h:P * h + P])
    small, i_row, f_fx = big[:, 40, :], big[:, 41, :], big[:, 42, :]
    y = lambda n, c: big[:, 12 + 4 * n + c, :]
    rms_phase(k, [[(k.x[:, c, :], act(c), k.v("norm1_g", c), None) for c in range(KD)]], "rms_eps", D)
    bias_rows = scr[0:1, 0:3, :]
    copy_in_phase(k, [(bias_rows, brow.rearrange("a (b c) -> a b c", c=T))])
    jobs = []
    for n, key in enumerate(("mv", "fv", "gv")):
        for tb in range(QB):
            jobs.append(token_job(k, act, w[key], big[:, 4 * n + tb, :], tb, bias=scr[0:1, n, :]))
    F = lambda key, j, out, **more: feature_job(k, act, w[key][j], out, bias=k.v("b_" + key, j), **more)
    jobs.append(feature_job(k, act, w["small"], small, bias=k.v("b_small")))
    jobs.append(feature_job(k, act, w["mi"], i_row, bias=k.v("b_mi")))
    for j in range(4):
        jobs.append(F("mq", j, big[:, 28 + j, :]))
    for j in range(4):
        jobs.append(F("mk", j, big[:, 32 + j, :]))
    for j in range(4):
        jobs.append(F("mo", j, big[:, 36 + j, :], func=ACT.Sigmoid))
    gemm_phase(k, jobs)
    mlstm_phase(k, tile(28), tile(32), value(0), small, i_row, f_fx, lambda h: y(0, h))
    rms_phase(k, [[(y(0, h), y(0, h), k.v("ml_g", h), big[:, 36 + h, :])] for h in range(4)], "rms_eps", P)
    gemm_phase(k, [F(key, j, big[:, b + j, :]) for key, b in (("fq", 28), ("fk", 32)) for j in range(4)])
    rms_phase(k, [[(big[:, b + h, :], big[:, b + h, :], k.v(g), None)] for b, g in ((28, "fxq_g"), (32, "fxk_g"))
                  for h in range(4)], "rms_eps", P)
    less_f = lambda h, n: [(k.c("negroot", 4)[:, h:h + 1].broadcast_to([4, P]), f_fx[0:4, 0:n])]
    attention_phase(k, softmax_units(tile(28), tile(32), value(4), P, None, lambda qb: k.c("causal")[:, T - P * (qb + 1):T],
                                     P ** -0.5, 0, lambda h: y(1, h), extra=less_f))
    padded = big[:, 28:33, :].rearrange("p a b -> p (a b)")[:, 0:4 * (T + 3)].rearrange("p (j t) -> p j t", j=4)
    gemm_phase(k, [F("rx", j, padded[:, j, 3:T + 3]) for j in range(4)]
               + [F("ry", j, big[:, 33 + j, :], func=ACT.Gelu_apprx_tanh) for j in range(4)])
    xc = lambda j: scr[:, j, :]
    conv_phase(k, padded, xc)
    gemm_phase(k, [feature_job(k, lambda c, j=j: xc(j), w[wk][j], scr[:, b + j, :], depth=1, bias=k.v(bk, j),
                               func=ACT.Sigmoid) for wk, bk, b in (("wa", "lru_ba", 4), ("wx", "lru_bx", 8))
                   for j in range(4)])
    lru_phase(k, xc, lambda j: scr[:, 4 + j, :], lambda j: scr[:, 8 + j, :], tile(33),
              lambda j: big[:, (37, 38, 39, 43)[j], :], tile(28), lambda j: y(2, j))
    gemm_phase(k, [feature_job(k, act, w[key][j], big[:, b + j, :], bias=b_ap(j), scale=sc)
                   for key, b, b_ap, sc in (("gq", 28, lambda j: k.v("b_gq", j), 1.0),
                                            ("gk", 30, lambda j: k.v("b_gk", j), 1.0)) for j in range(2)]
               + [F("gg", j, big[:, 32 + j, :], func=ACT.Silu) for j in range(4)]
               + [feature_job(k, lambda c: small, w["walpha"][j], big[:, 36 + j, :], depth=1,
                              bias=k.v("b_alpha", j)) for j in range(2)])
    states = big[:, 40:44, :].rearrange("p a b -> p (a b)").rearrange("p (q c n) -> p q c n", q=2, n=P)
    gla_phase(k, tile(28), tile(30), value(8), tile(36), tile(38), lambda p, c: states[:, p, c, :],
              lambda h: y(3, h))
    rms_phase(k, [[(y(3, h), y(3, h), k.v("gla_g", h), big[:, 32 + h, :])] for h in range(4)], "rms_eps", P)
    merged = lambda d: big[:, d, :]
    merge_phase(k, w["merge"], y, merged)
    project_phase(k, w["wo"], 1.0, merged)
    rms_phase(k, [[(k.x[:, c, :], act(c), k.v("norm2_g", c), None) for c in range(KD)]], "rms_eps", D)
    relu2_phase(k, w["up"], w["down"])


def layer(k, l, vec):
    nc, big, scr, w = k.nc, k.big, k.scr, WHERE["layers"][l]
    k.vec_cols = VEC2
    copy_in_phase(k, [(k.vec[:, 0:VEC2.n], vec)])
    x = lambda c: k.x[:, c, :]
    glu_phase(k, *w["ffn1"])
    layernorm_phase(k, "ln1_g", "ln1_b")
    tile = lambda i: big[:, i, :]
    v_tok = lambda tb: big[:, tb, :]
    v_mla = big[:, 4:6, :].rearrange("p a b -> p (a b)").rearrange("p (t n) -> p t n", n=256)
    jobs = [token_job(k, x, w["v"], v_tok(tb)[:, 0:468], tb, n=468) for tb in range(QB)]
    at = {"cq0": 6, "cq1": 7, "ckv": 8, "krope": 9, "kvcmp": 10, "iq0": 11, "iq1": 12, "ik": 13, "nq0": 14,
          "nq1": 15, "ks": 16, "kw": 17, "dq0": 18, "dq1": 19, "dk": 20, "sq0": 21, "sq1": 22, "sk0": 23, "sk1": 24}
    rope = {"krope": "mq", "kvcmp": "cmp", "iq0": "i4", "iq1": "i4", "ik": "i4", "nq0": "h2", "nq1": "h2",
            "ks": "h2", "kw": "h2", "dq0": "h2", "dq1": "h2", "dk": "h2"}
    jobs += [feature_job(k, x, w[key], tile(i), rope=rope.get(key)) for key, i in at.items()]
    gemm_phase(k, jobs)
    rms_phase(k, [[(tile(6 + j), tile(6 + j), k.v("q_g", j), None) for j in range(2)]], "rms_eps", 256)
    rms_phase(k, [[(tile(8), tile(8), k.v("kv_g"), None)]], "rms_eps", P)
    jobs = [feature_job(k, lambda c: tile(6 + c), w["uq"][h], tile(25 + h), depth=2, rope="mq") for h in range(HEADS)]
    for h in range(HEADS):
        job = feature_job(k, lambda c: tile(8), w["uk"][h], tile(29 + h), depth=1)
        job["sum"].append((k.c("ident"), tile(9), None))
        jobs.append(job)
    jobs += [token_job(k, lambda c: tile(8), w["uv"], v_mla[:, tb, :], tb, n=256, depth=1, per=2) for tb in range(QB)]
    gemm_phase(k, jobs)
    blk = big[:, 37:39, :].rearrange("p a b -> p (a b)")[:, 0:CMP_LEN * NCMP].rearrange("p (l n) -> p l n", n=NCMP)
    kc, vc, gates = tile(36)[:, 0:NCMP], tile(36)[0:NCMP, 64:128], tile(36)[:, 256:256 + 48].rearrange(
        "p (t g) -> p t g", g=12)
    compress_phase(k, tile(10), blk, w["c1"], w["c2"], tile(36)[:, 128:192], kc, vc,
                   big[:, 0:QB, GT0:GT0 + 12], gates)
    select = lambda qb: tile(32 + qb)
    select_phase(k, lambda j: tile(11 + j), tile(13), lambda qb, h: v_tok(qb)[:, IW0 + h:IW0 + h + 1], select)
    causal = lambda qb: k.c("causal")[:, T - P * (qb + 1):T]
    half = lambda t, h: t[64 * (h % 2):64 * (h % 2) + 64]
    ys = lambda n: (lambda h: k.act[:, 2 * n + h // 2, :])
    units = softmax_units(lambda h: tile(25 + h), lambda h: tile(29 + h),
                          lambda kb, h: v_mla[:, kb, 64 * h:64 * h + 64], 64, None, causal, 96 ** -0.5, 0, ys(0))
    attention_phase(k, units)
    units = []
    for h in range(HEADS):
        lo = 64 * (h % 2)
        q = half(tile(14 + h // 2), h)
        for qb in range(QB):
            wd = P * (qb + 1)
            more = dict(group=QB * h + qb, rows=(lo, lo + 64), scale=64 ** -0.5,
                        out=ys(1)(h)[lo:lo + 64, P * qb:P * qb + P])
            gate = lambda b: gates[:, qb, 4 * b + h:4 * b + h + 1]
            qs = q[:, P * qb:P * qb + P]
            at_cmp = slice(CONST.at["cmp_neg"][0] + NCMP * qb, CONST.at["cmp_neg"][0] + NCMP * (qb + 1))
            at_keep = slice(CONST.at["cmp_keep"][0] + NCMP * qb, CONST.at["cmp_keep"][0] + NCMP * (qb + 1))
            units.append(Unit([(qs, half(kc, h))], NCMP, [vc], first=True, last=False, gate=gate(0),
                              mask=k.const[:, at_cmp], keep=k.const[:, at_keep], **more))
            for b, (kt, col) in enumerate(((16, VS0), (17, VW0))):
                units.append(Unit([(qs, half(tile(kt), h)[:, 0:wd])], wd,
                                  [v_tok(kb)[:, col:col + 64] for kb in range(qb + 1)], first=False, last=(b == 1),
                                  gate=gate(b + 1), mask=causal(qb), **more))
    attention_phase(k, units)
    units = softmax_units(lambda h: half(tile(18 + h // 2), h), lambda h: half(tile(20), h),
                          lambda kb, h: v_tok(kb)[:, VD0:VD0 + 64], 64, None,
                          lambda qb: causal(0) if qb == 0 else select(qb)[:, 0:P * (qb + 1)], 64 ** -0.5, 0, ys(2))
    attention_phase(k, units)
    units = softmax_units(lambda h: half(tile(21 + h // 2), h), lambda h: half(tile(23 + h // 2), h),
                          lambda kb, h: v_tok(kb)[:, VB0 + 64 * h:VB0 + 64 * h + 64], 64, None,
                          lambda qb: k.c("strict")[:, T - P * (qb + 1):T], 64 ** -0.5, 0, ys(3))
    stick_phase(k, units)
    rms_phase(k, [[(k.act[:, 2 * g + j, :], k.act[:, 2 * g + j, :], k.v("group_g", 2 * g + j), None)
                   for j in range(2)] for g in range(4)], "rms_eps", 256)
    project_phase(k, w["wout"], ALPHA, lambda c: k.act[:, c, :])
    layernorm_phase(k, "ln2_g", "ln2_b")
    glu_phase(k, *w["ffn2"])
    layernorm_phase(k, "ln3_g", "ln3_b")


def build(nc, x, weights, const, vec1, brow, vec2, out):
    with ExitStack() as ctx:
        k = Core(nc, ctx, weights)
        copy_in_phase(k, [(k.x[:, :, :], x.rearrange("c p t -> p c t")), (k.const[:, :], const),
                          (k.vec[:, 0:VEC1.n], vec1)])

        block_one(k, brow)
        for l in range(LAYERS):
            layer(k, l, vec2[l])
        sent = k.flag("output_sent")
        with nc.Block() as block:
            @block.sync
            def _(sp):
                sp.dma_start(out.rearrange("c p t -> p c t"), k.x[:, :, :]).then_inc(sent, 16)
                sp.wait_ge(sent, 16)


def pack_weights(inputs):
    packed = np.zeros((len(STREAM.tiles), P, P), np.float32)
    for n, pieces in enumerate(STREAM.tiles):
        for name, lay, row, col, r0, c0, h, w in pieces or ():
            a = inputs[name][lay]
            if isinstance(row, tuple):
                a, row = a[row[0]], row[1]
            packed[n, r0:r0 + h, c0:c0 + w] = a[row:row + h, col:col + w]
    packed = packed.reshape(NSLABS, SLAB, P, P).transpose(0, 2, 1, 3)
    return np.ascontiguousarray(packed).reshape(NSLABS, P, SLAB * P)


def by_column(v):
    return np.asarray(v).reshape(-1, P).T


def pack_vec1(i):
    out = np.zeros((P, VEC1.n), np.float32)

    def put(name, a):
        at, n = VEC1.at[name]
        out[: a.shape[0], at:at + a.shape[1]] = a

    b = i["b_in"][0]
    put("norm1_g", by_column(i["norm1_g"][0]))
    put("norm2_g", by_column(i["norm2_g"][0]))
    for name, at, n in (("b_mq", MQ, 512), ("b_mk", MK, 512), ("b_mo", MO, 512), ("b_fq", FQ, 512),
                        ("b_fk", FK, 512), ("b_rx", RX, 512), ("b_ry", RY, 512), ("b_gq", GQ, 256),
                        ("b_gk", GK, 256), ("b_gg", GG, 512), ("b_gates", GATES, 4096)):
        put(name, by_column(b[at:at + n]))
    small = VEC1.at["b_small"][0]
    out[0:4, small] = b[MF:MF + 4]
    out[32:36, small] = b[FFG:FFG + 4]
    out[96:112, small] = b[GA:GA + 16]
    out[0:4, VEC1.at["b_mi"][0]] = b[MI:MI + 4]
    put("ml_g", by_column(i["ml_norm_g"][0]))
    put("gla_g", by_column(i["gla_norm_g"][0]))
    put("fxq_g", by_column(i["fx_qnorm_g"][0]))
    put("fxk_g", by_column(i["fx_knorm_g"][0]))
    put("conv_w", np.concatenate([by_column(i["lru_conv_w"][0][t]) for t in range(4)], 1))
    put("conv_b", by_column(i["lru_conv_b"][0]))
    put("lru_ba", by_column(i["lru_ba"][0]))
    put("lru_bx", by_column(i["lru_bx"][0]))
    put("lam", by_column(i["lru_lambda"][0]))
    put("b_alpha", by_column(i["gla_b_alpha"][0]))
    return out


def pack_vec2(i):
    out = np.zeros((LAYERS, P, VEC2.n), np.float32)
    for l in range(LAYERS):
        for name, key in (("ln1_g", "ln1_g_2"), ("ln1_b", "ln1_b_2"), ("q_g", "mla_q_norm_2"),
                          ("kv_g", "mla_kv_norm_2"), ("group_g", "group_norm_g_2"), ("ln2_g", "ln2_g_2"),
                          ("ln2_b", "ln2_b_2"), ("ln3_g", "ln3_g_2"), ("ln3_b", "ln3_b_2")):
            at, n = VEC2.at[name]
            out[l, :, at:at + n] = by_column(i[key][l])
        at, n = VEC2.at["pos"]
        out[l, 0:64, at:at + n] = i["nsa_cmp_pos_2"][l].T
        out[l, 64:128, at:at + n] = i["nsa_cmp_pos_2"][l].T
    return out


def arrays_of(inputs):
    i = {name: np.asarray(a) for name, a in inputs.items()}
    b = i["b_in"][0]
    return {
        "xT": np.ascontiguousarray(i["x"][0].T).reshape(KD, P, T),
        "weights": pack_weights(i),
        "consts": constants(),
        "vec1": pack_vec1(i),
        "brow": np.concatenate([b[c:c + 512] for c in (MV, FV, GV)])[None, :],
        "vec2": pack_vec2(i),
    }


def kernel(**inputs):
    import concourse.bacc as bacc
    from concourse.bass_utils import run_bass_kernel_spmd

    nc = bacc.Bacc("TRN2", target_bir_lowering=False, num_devices=1)
    arrays = arrays_of(inputs)
    aps = [nc.dram_tensor(name, a.shape, F32, kind="ExternalInput").ap() for name, a in arrays.items()]
    out = nc.dram_tensor("outT", (KD, P, T), F32, kind="ExternalOutput").ap()
    build(nc, *aps, out)
    r = run_bass_kernel_spmd(nc, [arrays], core_ids=[0])
    got = np.asarray(r.results[0]["outT"]).reshape(D, T)
    return np.ascontiguousarray(got.T)[None]
```

```python
from contextlib import ExitStack

import numpy as np

import concourse.bass as bass
from concourse import mybir

F32 = mybir.dt.float32
F32R = mybir.dt.float32r
ALU = mybir.AluOpType
ACT = mybir.ActivationFunctionType
AX = mybir.AxisListType.X

P = 128
T = 512
QB = T // P
D = 1024
KD = D // P
NEG = -1e30
TAKEN = -3e38

BW = 512
FF1 = 4096
HEADS = 4
GLA_TAU = 16.0
LRU_C = 8.0
CHUNK = 64
NCHUNK = T // CHUNK
RMS_EPS, LN_EPS = 1e-6, 1e-5
W1 = (512, 512, 512, 512, 4, 4, 512, 512, 512, 4, 512, 512, 256, 256, 512, 512, 16, 4096)
O1 = np.concatenate([[0], np.cumsum(W1)])
(MQ, MK, MV, MO, MI, MF, FQ, FK, FV, FFG, RX, RY, GQ, GK, GV, GG, GA, GATES) = [int(o) for o in O1[:-1]]

LAYERS = 2
FF2 = 2816
KF2 = FF2 // P
ALPHA = (2.0 * LAYERS) ** 0.25
W2 = (256, 128, 32, 256, 64, 64, 64, 64, 64, 64, 12, 256, 64, 64, 256, 32, 8, 256, 256, 256)
O2 = np.concatenate([[0], np.cumsum(W2)])
(CQ, CKV, KROPE, NQ, NKC, NVC, NKS, NVS, NKW, NVW, NGATE, DQ, DK, DV, IQ, IK, IW, SQ, SK, SV) = [
    int(o) for o in O2[:-1]]
NCMP, CMP_LEN, CMP_STRIDE = 31, 32, 16
TOPK = T // 4
IDX_HEADS = 8
TOP_STEPS = TOPK // 8
VS0, VW0, VD0, VB0, GT0, IW0 = 0, 64, 128, 192, 448, 460

SLAB = 8
RAW = 3
SPLIT = 3


class Stream:

    def __init__(self):
        self.tiles = []
        self.whole = set()

    def align(self, n):
        while len(self.tiles) % n:
            self.tiles.append(None)

    def add(self, pieces):
        at = len(self.tiles)
        self.tiles.extend(pieces)
        return at

    def columns(self, name, layer, depth, cols, row=0):
        at = len(self.tiles)
        for k in range(depth):
            self.tiles.append([(name, layer, row + k * P, m, 0, c, P, n) for c, m, n in cols])
        return at

    def wide(self, name, layer, depth, cols):
        at = len(self.tiles)
        assert at % SLAB == 0
        for k in range(depth):
            for q in range(T // P):
                lo, hi = q * P, (q + 1) * P
                self.tiles.append([(name, layer, k * P, m + max(c, lo) - c, 0, max(c, lo) - lo, P,
                                    min(c + n, hi) - max(c, lo)) for c, m, n in cols if max(c, lo) < min(c + n, hi)])
        return at

    def plain(self, at, n):
        assert at % SLAB == 0 and n % SLAB == 0
        self.whole.update(range(at // SLAB, (at + n) // SLAB))


def plan():
    s = Stream()
    w = {}
    one = lambda name, layer, depth, col, n: [
        s.columns(name, layer, depth, [(0, col + P * j, P)]) for j in range(n)]
    w["mv"], w["fv"], w["gv"] = [s.wide("w_in", 0, KD, [(0, c, BW)]) for c in (MV, FV, GV)]
    w["small"] = s.columns("w_in", 0, KD, [(0, MF, 4), (32, FFG, 4), (96, GA, 16)])
    w["mi"] = s.columns("w_in", 0, KD, [(0, MI, 4)])
    w["mq"] = one("w_in", 0, KD, MQ, 4)
    w["mk"] = one("w_in", 0, KD, MK, 4)
    w["mo"] = one("w_in", 0, KD, MO, 4)
    w["fq"] = one("w_in", 0, KD, FQ, 4)
    w["fk"] = one("w_in", 0, KD, FK, 4)
    w["rx"] = one("w_in", 0, KD, RX, 4)
    w["ry"] = one("w_in", 0, KD, RY, 4)
    for key, name in (("wa", "lru_wa"), ("wx", "lru_wx")):
        w[key] = [s.add([[(name, 0, (2 * j, 0), 0, 0, 0, 64, 64), (name, 0, (2 * j + 1, 0), 0, 64, 64, 64, 64)]])
                  for j in range(4)]
    s.plain(w["wa"][0], 8)
    w["gq"] = one("w_in", 0, KD, GQ, 2)
    w["gk"] = one("w_in", 0, KD, GK, 2)
    w["gg"] = one("w_in", 0, KD, GG, 4)
    w["walpha"] = [s.add([[("gla_w_alpha", 0, 0, P * j, 96, 0, 16, P)]]) for j in range(2)]
    s.align(SLAB)
    s.plain(w["walpha"][0], 8)
    w["merge"] = []
    for d in range(KD):
        for n in range(4):
            g = s.columns("w_in", 0, KD, [(0, GATES + D * n + P * d, P)])
            b = len(s.tiles)
            for k in range(4):
                s.tiles.append([("w_branch", 0, (n, k * P), P * d, 0, 0, P, P)])
            w["merge"].append((g, b))
    w["wo"] = one("w_o", 0, KD, 0, KD)
    w["ffn"] = []
    for half in range(2):
        at = half * FF1 // 2
        up = one("w_up", 0, KD, at, FF1 // 2 // P)
        w["ffn"].append((up, [s.columns("w_down", 0, FF1 // 2 // P, [(0, P * j, P)], row=at) for j in range(KD)]))
    s.align(SLAB)
    w["layers"] = []
    for l in range(LAYERS):
        v = {}

        def ffn(n):
            up = []
            for f in range(KF2):
                up.append(tuple(s.columns(f"ffn{n}_{m}_2", l, KD, [(0, P * f, P)]) for m in ("w1", "w3")))
            down = [s.columns(f"ffn{n}_w2_2", l, KF2, [(0, P * j, P)]) for j in range(KD)]
            return up, down

        v["ffn1"] = ffn(1)
        spans = [(VS0, NVS, 64), (VW0, NVW, 64), (VD0, DV, 64), (VB0, SV, 256), (GT0, NGATE, 12), (IW0, IW, 8)]
        v["v"] = s.wide("w_in_2", l, KD, spans)
        two = lambda c: [(0, c, 64), (64, c, 64)]
        for key, cols in (
            ("cq0", [(0, CQ, P)]), ("cq1", [(0, CQ + P, P)]), ("ckv", [(0, CKV, P)]),
            ("krope", [(64, KROPE, 32)]), ("kvcmp", [(0, NKC, 64), (64, NVC, 64)]),
            ("iq0", [(0, IQ, P)]), ("iq1", [(0, IQ + P, P)]), ("ik", [(32 * i, IK, 32) for i in range(4)]),
            ("nq0", [(0, NQ, P)]), ("nq1", [(0, NQ + P, P)]), ("ks", two(NKS)), ("kw", two(NKW)),
            ("dq0", [(0, DQ, P)]), ("dq1", [(0, DQ + P, P)]), ("dk", two(DK)),
            ("sq0", [(0, SQ, P)]), ("sq1", [(0, SQ + P, P)]), ("sk0", [(0, SK, P)]), ("sk1", [(0, SK + P, P)]),
        ):
            v[key] = s.columns("w_in_2", l, KD, cols)
        v["uq"] = [s.columns("mla_w_uq_2", l, 2, [(0, 96 * h, 96)]) for h in range(HEADS)]
        v["uk"] = [s.columns("mla_w_ukv_2", l, 1, [(0, 128 * h, 64)]) for h in range(HEADS)]
        v["uv"] = [s.add([[("mla_w_ukv_2", l, 0, 128 * (2 * i + j) + 64, 0, 64 * j, P, 64) for j in range(2)]])
                   for i in range(2)]
        s.align(SLAB)
        v["c1"] = s.add([[(f"nsa_cmp_w{m}1_2", l, 64 * (2 * i + j), 0, r, 64 * j, 64, 64)
                          for m, r in (("k", 0), ("v", 64)) for j in range(2)] for i in range(16)])
        v["c2"] = s.add([[("nsa_cmp_wk2_2", l, 0, 0, 0, 0, 64, 64), ("nsa_cmp_wk2_2", l, 0, 0, 0, 64, 64, 64),
                          ("nsa_cmp_wv2_2", l, 0, 0, 64, 0, 64, 64)]])
        s.align(SLAB)
        s.plain(v["uq"][0], len(s.tiles) - v["uq"][0])
        v["wout"] = [s.columns("w_out_2", l, KD, [(0, P * j, P)]) for j in range(KD)]
        v["ffn2"] = ffn(2)
        s.align(SLAB)
        w["layers"].append(v)
    s.align(SLAB)
    return s, w


STREAM, WHERE = plan()
NSLABS = len(STREAM.tiles) // SLAB
SPLITS = [n for n in range(NSLABS) if n not in STREAM.whole]
SPLIT_AT = {n: m for m, n in enumerate(SPLITS)}


class Columns:

    def __init__(self):
        self.at, self.n = {}, 0

    def add(self, name, n):
        self.at[name] = (self.n, n)
        self.n += n


CONST = Columns()
for _n, _w in (("ident", P), ("ones", P), ("negident", 4), ("negroot", 4), ("causal", T), ("strict", T), ("tri", P),
               ("chunk_tri", P), ("cmp_neg", QB * NCMP), ("cmp_keep", QB * NCMP), ("goes_on", T),
               ("rms_eps", 1), ("ln_eps", 1), ("one", 1)):
    CONST.add(_n, _w)

ROPE = Columns()
for _n in ("h2", "i4", "mq", "cmp"):
    ROPE.add("cos_" + _n, T)
    ROPE.add("sin_" + _n, T)
for _n in ("h2", "i4", "mq", "cmp"):
    ROPE.add("rot_" + _n, P)

VEC1 = Columns()
for _n, _w in (("norm1_g", 8), ("norm2_g", 8), ("b_mq", 4), ("b_mk", 4), ("b_mo", 4), ("b_fq", 4), ("b_fk", 4),
               ("b_rx", 4), ("b_ry", 4), ("b_gq", 2), ("b_gk", 2), ("b_gg", 4), ("b_small", 1), ("b_mi", 1),
               ("b_gates", 32), ("ml_g", 4), ("gla_g", 4), ("fxq_g", 1), ("fxk_g", 1), ("conv_w", 16),
               ("conv_b", 4), ("lru_ba", 4), ("lru_bx", 4), ("lam", 4), ("b_alpha", 2), ("decay", 4), ("tmp", 4)):
    VEC1.add(_n, _w)
VEC2 = Columns()
for _n, _w in (("ln1_g", 8), ("ln1_b", 8), ("q_g", 2), ("kv_g", 1), ("group_g", 8), ("ln2_g", 8), ("ln2_b", 8),
               ("ln3_g", 8), ("ln3_b", 8), ("pos", CMP_LEN)):
    VEC2.add(_n, _w)
NVEC = VEC1.n + LAYERS * VEC2.n
BROW = 3 * 512


def constants():
    c = np.zeros((P, CONST.n), np.float32)
    rope = np.zeros((P, ROPE.n), np.float32)

    def put(name, a):
        where, to = (ROPE, rope) if name in ROPE.at else (CONST, c)
        at, n = where.at[name]
        to[: a.shape[0], at:at + n] = a

    put("ident", np.eye(P))
    put("ones", np.ones((P, P)))
    put("negident", -np.eye(4))
    put("negroot", -np.eye(4) * np.sqrt(128.0))

    def rotation(spans):
        r = np.zeros((P, P))
        for a, n in spans:
            for i in range(n // 2):
                r[a + n // 2 + i, a + i] = -1
                r[a + i, a + n // 2 + i] = 1
        return r

    def tables(spans):
        cos, sin = np.ones((P, T)), np.zeros((P, T))
        for a, n in spans:
            inv = np.float32(10000.0) ** (-np.arange(0, n, 2, dtype=np.float32) / np.float32(n))
            ang = (np.arange(T, dtype=np.float32)[None, :] * inv.astype(np.float32)[:, None]).astype(np.float32)
            for half in range(2):
                cos[a + half * n // 2:a + (half + 1) * n // 2] = np.cos(ang.astype(np.float64))
                sin[a + half * n // 2:a + (half + 1) * n // 2] = np.sin(ang.astype(np.float64))
        return cos, sin

    for kind, spans in (("h2", [(0, 64), (64, 64)]), ("i4", [(32 * i, 32) for i in range(4)]),
                        ("mq", [(64, 32)]), ("cmp", [(0, 64)])):
        put("rot_" + kind, rotation(spans))
        cos, sin = tables(spans)
        put("cos_" + kind, cos)
        put("sin_" + kind, sin)
    i = np.arange(P)
    before = np.zeros((P, T - P))
    put("causal", np.concatenate([before, np.where(i[None, :] <= i[:, None], 0, NEG)], 1))
    put("strict", np.concatenate([before, np.where(i[None, :] < i[:, None], 0, NEG)], 1))
    put("tri", (i[:, None] <= i[None, :]).astype(float))
    put("chunk_tri", ((i[:, None] <= i[None, :]) & (i[:, None] // CHUNK == i[None, :] // CHUNK)).astype(float))
    ends = np.arange(NCMP) * CMP_STRIDE + CMP_LEN - 1
    seen = ends[None, None, :] <= (np.arange(QB)[None, :, None] * P + i[:, None, None])
    put("cmp_keep", seen.astype(float).reshape(P, -1))
    put("cmp_neg", np.where(seen, 0, NEG).reshape(P, -1))
    put("goes_on", np.tile((np.arange(T) % CHUNK != 0).astype(float), (P, 1)))
    put("rms_eps", np.full((P, 1), RMS_EPS))
    put("ln_eps", np.full((P, 1), LN_EPS))
    put("one", np.ones((P, 1)))
    return c, rope


class Signal:

    def __init__(self, sem):
        self, self.base = sem, 0


def wait(eng, signal, count):
    assert count >= 1
    eng.wait_ge(signal, signal.base + count)


class Core:

    def __init__(self, nc, ctx, weights):
        self.nc, self.ctx, self.weights = nc, ctx, weights
        at = [0]
        total = 4 * (T * (KD + 2 * KD + 44 + 12) + SLAB * P * (RAW + 2 * SPLIT)) // 4
        first = nc.sbuf_base + (-nc.sbuf_base) % 64
        ctx.enter_context(nc.sbuf_tensor("arena", [P, total + 16], F32))

        def place(name, shape, dt=F32, over=None):
            size = int(np.prod(shape[1:]))
            start = at[0] if over is None else over
            if over is None:
                at[0] += size
            assert at[0] <= total
            return nc.alloc_sbuf_tensor_at(name, shape, dt, offset=first + 4 * start)

        self.x = place("x_resid", [P, KD, T])
        self.in_hi = place("in_hi", [P, KD, T], F32R)
        self.act = place("act", [P, KD, T])
        self.in_lo = place("in_lo", [P, KD, T], F32R, over=at[0] - KD * T)
        self.big = place("big", [P, 44, T])
        self.parts = place("parts", [P, 44, T], F32R, over=at[0] - 44 * T)
        self.scr = place("scratch", [P, 12, T])
        self.raw = place("raw_slabs", [P, RAW, SLAB * P])
        self.w_hi = place("w_hi", [P, SPLIT, SLAB * P], F32R)
        self.w_lo = place("w_lo", [P, SPLIT, SLAB * P], F32R)
        sb = lambda name, shape: ctx.enter_context(nc.sbuf_tensor(name, shape, F32))
        self.const = sb("const_cols", [P, CONST.n])
        self.vec = sb("vector_cols", [P, NVEC])
        self.stat = sb("stats", [P, 2, 64])
        self.ps = ctx.enter_context(nc.psum_tensor("ps", [P, 8, T], F32))
        self.flags = {}
        self.base = {}
        self.slab_loaded = [ctx.enter_context(nc.semaphore(f"slab_loaded{i}")) for i in range(RAW)]
        self.hi_made, self.lo_made = self.flag("w_hi_made"), self.flag("w_lo_made")
        self.sums_done = self.flag("sums_done")
        self.loaded = 0
        self.high = self.low = 0
        self.last_sum = {}
        self.sums = 0
        self.seen_slab = -1
        self.vec_cols, self.vec_from = VEC1, 0

    def flag(self, name):
        if name not in self.flags:
            self.flags[name] = self.ctx.enter_context(self.nc.semaphore(name))
            self.base[name] = 0
        return self.flags[name]

    def at(self, flag, count):
        assert count >= 1
        return next(self.base[name] for name, f in self.flags.items() if f is flag) + count

    def passed(self, **counts):
        for name, n in counts.items():
            self.base[name] += n

    def c(self, name, rows=P):
        at, n = CONST.at[name]
        return self.const[0:rows, at:at + n]

    def rope(self, name):
        at, n = ROPE.at[name]
        return self.big[:, 33 + at // T, at % T:at % T + n]

    def v(self, name, j=0, n=1):
        at, _ = self.vec_cols.at[name]
        at += self.vec_from
        return self.vec[:, at + j:at + j + n]

    def raw_tile(self, i):
        slab, c = divmod(i, SLAB)
        return self.raw[:, slab % RAW, c * P:(c + 1) * P]

    def w_parts(self, i):
        slab, c = divmod(i, SLAB)
        at = SPLIT_AT[slab] % SPLIT
        return self.w_hi[:, at, c * P:(c + 1) * P], self.w_lo[:, at, c * P:(c + 1) * P]

    def wide_parts(self, i):
        slab, c = divmod(i, SLAB)
        at = SPLIT_AT[slab] % SPLIT
        return self.w_hi[:, at, c * P:(c + 4) * P], self.w_lo[:, at, c * P:(c + 4) * P]

    def products(self, i, x):
        (wh, wl), (xh, xl) = self.w_parts(i), x
        return [(wh, xh), (wh, xl), (wl, xh)]

    def use(self, jobs, by_slab=True):
        ends = []
        for tiles in jobs:
            tiles = list(tiles)
            for n, i in enumerate(tiles):
                if n == len(tiles) - 1 or (by_slab and i % SLAB == SLAB - 1):
                    self.sums += 1
                self.last_sum[i // SLAB] = self.sums + (0 if n == len(tiles) - 1 or i % SLAB == SLAB - 1 else 1)
            for i in tiles if not by_slab else ():
                self.last_sum[i // SLAB] = self.sums
            ends.append(self.sums)
        return ends

    def load_slabs(self, sp):
        last = max(self.last_sum) if self.last_sum else -1
        while self.loaded < min(NSLABS, last + 1 + RAW):
            n = self.loaded
            if n >= RAW and n - RAW in SPLIT_AT:
                sp.wait_ge(self.lo_made, SPLIT_AT[n - RAW] + 1)
            elif n >= RAW:
                sp.wait_ge(self.sums_done, self.last_sum[n - RAW])
            sp.dma_start(self.raw[:, n % RAW, :], self.weights[n]).then_inc(self.slab_loaded[n % RAW], 16)
            self.loaded += 1

    def high_slabs(self, act, i):
        last = max(self.last_sum)
        while self.high < len(SPLITS) and SPLITS[self.high] <= min(i // SLAB + SPLIT - 1, self.loaded - 1):
            m = self.high
            n = SPLITS[m]
            if m >= SPLIT and SPLITS[m - SPLIT] > last:
                break
            act.wait_ge(self.slab_loaded[n % RAW], 16 * (n // RAW + 1))
            if m >= SPLIT:
                act.wait_ge(self.sums_done, self.last_sum[SPLITS[m - SPLIT]])
            self.nc.scalar.activation(self.w_hi[:, m % SPLIT, :], self.raw[:, n % RAW, :], ACT.Copy)\
                .then_inc(self.hi_made, 1)
            self.high += 1

    def low_slabs(self, pool):
        while self.low < self.high:
            m = self.low
            n = SPLITS[m]
            pool.wait_ge(self.hi_made, m + 1)
            self.nc.gpsimd.tensor_tensor(self.w_lo[:, m % SPLIT, :], self.raw[:, n % RAW, :],
                                         self.w_hi[:, m % SPLIT, :].bitcast(F32), ALU.subtract)\
                .then_inc(self.lo_made, 1)
            self.low += 1

    def need(self, pe, i):
        slab = i // SLAB
        if self.seen_slab < slab:
            if slab in SPLIT_AT:
                pe.wait_ge(self.lo_made, SPLIT_AT[slab] + 1)
            else:
                pe.wait_ge(self.slab_loaded[slab % RAW], 16 * (slab // RAW + 1))
            self.seen_slab = slab


def add_up(k, pe, out, tiles, wait_tile=None):
    for c, (i, x) in enumerate(tiles):
        k.need(pe, i)
        if wait_tile:
            wait_tile(pe, c)
        last = c == len(tiles) - 1
        for m, (lhsT, rhs) in enumerate(k.products(i, x)):
            mm = k.nc.tensor.matmul(out, lhsT, rhs, start=(c == 0 and m == 0), stop=(last and m == 2))
        if last or i % SLAB == SLAB - 1:
            mm.then_inc(k.sums_done, 1)


def tiles_of(job):
    return [i for _, i, *_ in job["sum"] if i is not None]


def gemm_phase(k, jobs):
    nc = k.nc
    ends = k.use([tiles_of(j) for j in jobs], by_slab=False)
    taken, rotated, joined, part = [k.flag(n) for n in ("taken", "rotated", "joined", "rope_part")]
    ropes = [j for j, job in enumerate(jobs) if job.get("rope")]

    with nc.Block() as block:
        @block.sync
        def _(sp):
            k.load_slabs(sp)

        @block.tensor
        def _(pe):

            def rotate(r):
                job = jobs[ropes[r]]
                pe.wait_ge(taken, k.at(taken, ropes[r] + 1))
                if r >= 2:
                    pe.wait_ge(joined, k.at(joined, r - 1))
                nc.tensor.matmul(k.ps[:, 4 + r % 2, :], k.rope("rot_" + job["rope"]), job["out"],
                                 start=True, stop=True).then_inc(rotated, 1)

            for j, job in enumerate(jobs):
                if j >= 4:
                    pe.wait_ge(taken, k.at(taken, j - 3))
                for part, i, cols, start, stop in job["sum"]:
                    if i is not None:
                        k.need(pe, i)
                    for m, (lhsT, rhs) in enumerate(part):
                        mm = nc.tensor.matmul(k.ps[:, j % 4, cols], lhsT, rhs, start=(start and m == 0),
                                              stop=(stop and m == len(part) - 1))
                mm.then_inc(k.sums_done, 1)
                if j - 1 in ropes:
                    rotate(ropes.index(j - 1))
            if len(jobs) - 1 in ropes:
                rotate(len(ropes) - 1)

        @block.scalar
        def _(act):
            for j, job in enumerate(jobs):
                k.high_slabs(act, max(tiles_of(job)))
                act.wait_ge(k.sums_done, ends[j])
                nc.scalar.activation(job["out"], job.get("view", lambda bank: bank)(k.ps[:, j % 4, :]),
                                     job.get("func", ACT.Identity), bias=job.get("bias", 0.0),
                                     scale=job.get("scale", 1.0)).then_inc(taken, 1)

        if ropes:
            @block.vector
            def _(dve):
                for r, j in enumerate(ropes):
                    job = jobs[j]
                    turned = k.scr[:, 10 + r % 2, :]
                    dve.wait_ge(rotated, k.at(rotated, r + 1))
                    nc.vector.tensor_tensor(turned, k.ps[:, 4 + r % 2, :], k.rope("sin_" + job["rope"]),
                                            ALU.mult).then_inc(part, 1)
                    nc.vector.tensor_tensor(job["out"], job["out"], k.rope("cos_" + job["rope"]),
                                            ALU.mult).then_inc(part, 1)
                    dve.wait_ge(part, k.at(part, 2 * r + 2))
                    nc.vector.tensor_tensor(job["out"], job["out"], turned, ALU.add).then_inc(joined, 1)

        @block.gpsimd
        def _(pool):
            k.low_slabs(pool)
    k.passed(taken=len(jobs), rotated=len(ropes), joined=len(ropes), rope_part=2 * len(ropes))


def token_phase(k, x, jobs, norm, loads=()):
    nc = k.nc
    depth = KD
    ends = k.use([range(at, at + 4 * depth) for at, _, _ in jobs])
    taken, here = k.flag("taken"), k.flag("inputs_here")
    with nc.Block() as block:
        @block.sync
        def _(sp):
            for dst, src in loads:
                sp.dma_start(dst, src).then_inc(here, 16)
            k.load_slabs(sp)
            if loads:
                sp.wait_ge(here, k.at(here, 16 * len(loads)))

        @block.tensor
        def _(pe):
            norm.tensor(pe)
            for j, (at, _, _) in enumerate(jobs):
                if j >= 2:
                    pe.wait_ge(taken, k.at(taken, QB * (j - 1)))
                for c in range(depth):
                    i = at + 4 * c
                    k.need(pe, i)
                    if j == 0:
                        norm.wait_tile(pe, c)
                    xh, xl = x(c)
                    wh, wl = k.wide_parts(i)
                    for tb in range(QB):
                        block = slice(P * tb, P * tb + P)
                        for m, (lhsT, rhs) in enumerate(((xh, wh), (xh, wl), (xl, wh))):
                            mm = nc.tensor.matmul(k.ps[:, QB * (j % 2) + tb, :], lhsT[:, block], rhs,
                                                  start=(c == 0 and m == 0), stop=(c == depth - 1 and m == 2))
                    if (i + 3) % SLAB == SLAB - 1:
                        mm.then_inc(k.sums_done, 1)

        @block.scalar
        def _(act):
            norm.scalar(act)
            for j, (at, _, _) in enumerate(jobs):
                k.high_slabs(act, at + 4 * depth - 1)

        @block.vector
        def _(dve):
            norm.vector(dve)
            for j, (_, out, bias) in enumerate(jobs):
                dve.wait_ge(k.sums_done, ends[j])
                for tb in range(QB):
                    bank = k.ps[:, QB * (j % 2) + tb, :]
                    if bias is None:
                        nc.vector.tensor_copy(out(tb), bank).then_inc(taken, 1)
                    else:
                        nc.vector.tensor_tensor(out(tb), bank, bias, ALU.add).then_inc(taken, 1)

        @block.gpsimd
        def _(pool):
            k.low_slabs(pool)
    norm.passed()
    k.passed(taken=QB * len(jobs), inputs_here=16 * len(loads))


class RmsNorm:

    BATCH = 4

    def __init__(self, k, groups, eps, width, parts=()):
        self.k, self.groups, self.eps, self.width, self.parts = k, groups, eps, width, parts
        self.flat = [(g, t) for g, group in enumerate(groups) for t in group]
        self.first = [sum(len(x) for x in groups[:g]) for g in range(len(groups) + 1)]
        self.squared, self.summed, self.logged, self.rooted, self.ungated, self.normed, self.hi, self.lo = [
            k.flag(n) for n in ("squared", "summed", "norm_logged", "rooted", "ungated", "normed", "norm_hi", "norm_lo")]

    def inv(self, g):
        return self.k.scr[:, 8 + g % self.BATCH, :]

    def tensor(self, pe):
        k, first = self.k, self.first
        for n, (g, t) in enumerate(self.flat):
            if g >= self.BATCH and n == first[g]:
                pe.wait_ge(self.rooted, k.at(self.rooted, g - self.BATCH + 1))
            pe.wait_ge(self.squared, k.at(self.squared, n + 1))
            k.nc.tensor.matmul(k.ps[:, g % self.BATCH, :], k.c("ones"), k.scr[:, n % 4, :], start=(n == first[g]),
                               stop=(n == first[g + 1] - 1)).then_inc(self.summed, 1)

    def wait_tile(self, pe, c):
        pe.wait_ge(self.lo, self.k.at(self.lo, c + 1))

    def scalar(self, act):
        k, first, nc = self.k, self.first, self.k.nc
        for b in range(0, len(self.groups), self.BATCH):
            batch = range(b, min(b + self.BATCH, len(self.groups)))
            for n in range(first[b], first[batch[-1] + 1]):
                if n >= 4:
                    act.wait_ge(self.summed, k.at(self.summed, n - 3))
                nc.scalar.activation(k.scr[:, n % 4, :], self.flat[n][1][0], ACT.Square).then_inc(self.squared, 1)
            for g in batch:
                act.wait_ge(self.summed, k.at(self.summed, first[g + 1]))
                if g >= self.BATCH:
                    act.wait_ge(self.normed, k.at(self.normed, first[g - self.BATCH + 1]))
                nc.scalar.activation(self.inv(g), k.ps[:, g % self.BATCH, :], ACT.Ln, bias=k.c(self.eps),
                                     scale=1.0 / self.width).then_inc(self.logged, 1)
            for g in batch:
                act.wait_ge(self.logged, k.at(self.logged, g + 1))
                nc.scalar.activation(self.inv(g), self.inv(g), ACT.Exp, scale=-0.5).then_inc(self.rooted, 1)
        for n, (hi, _) in enumerate(self.parts):
            act.wait_ge(self.normed, k.at(self.normed, n + 1))
            nc.scalar.activation(hi, self.flat[n][1][1], ACT.Copy).then_inc(self.hi, 1)

    def vector(self, dve):
        k, nc = self.k, self.k.nc
        gated = 0
        for n in range(len(self.flat) + 1):
            if n < len(self.flat):
                g, (src, out, gain, gate) = self.flat[n]
                dve.wait_ge(self.rooted, k.at(self.rooted, g + 1))
                if gate is None:
                    nc.vector.scalar_tensor_tensor(out, src, gain, self.inv(g), ALU.mult, ALU.mult)\
                        .then_inc(self.normed, 1)
                else:
                    nc.vector.scalar_tensor_tensor(out, src, gain, self.inv(g), ALU.mult, ALU.mult)\
                        .then_inc(self.ungated, 1)
                    gated += 1
                    dve.wait_ge(self.ungated, k.at(self.ungated, gated))
                    nc.vector.tensor_tensor(out, out, gate, ALU.mult).then_inc(self.normed, 1)
            if self.parts and n >= 1:
                hi, lo = self.parts[n - 1]
                dve.wait_ge(self.hi, k.at(self.hi, n))
                nc.vector.tensor_tensor(lo, self.flat[n - 1][1][1], hi.bitcast(F32), ALU.subtract).then_inc(self.lo, 1)

    def passed(self):
        n, g = len(self.flat), len(self.groups)
        self.k.passed(squared=n, summed=n, norm_logged=g, rooted=g, normed=n, norm_hi=len(self.parts),
                      norm_lo=len(self.parts), ungated=sum(1 for _, t in self.flat if t[3] is not None))


def rms_phase(k, groups, eps, width):
    norm = RmsNorm(k, groups, eps, width)
    with k.nc.Block() as block:
        @block.scalar
        def _(act):
            norm.scalar(act)

        @block.tensor
        def _(pe):
            norm.tensor(pe)

        @block.vector
        def _(dve):
            norm.vector(dve)
    norm.passed()


class LayerNorm:

    def __init__(self, k, gain, shift, split=True):
        self.k, self.gain, self.shift, self.split = k, gain, shift, split
        self.cols = k.vec_cols
        self.added, self.centred, self.squared, self.summed, self.logged, self.rooted, self.normed, self.hi, \
            self.lo, self.shifted = [k.flag(n) for n in (
                "added", "centred", "squared", "summed", "norm_logged", "rooted", "normed", "norm_hi", "norm_lo",
                "shifted")]
        self.gain_at = [k.v(gain, n) for n in range(KD)]
        self.shift_at = [k.v(shift, n) for n in range(KD)]

    def tensor(self, pe):
        k, nc = self.k, self.k.nc
        for n in range(KD):
            mm = nc.tensor.matmul(k.ps[:, 0, :], k.c("ones"), k.x[:, n, :], start=(n == 0), stop=(n == KD - 1))
        mm.then_inc(self.added, 1)
        for n in range(KD):
            pe.wait_ge(self.squared, k.at(self.squared, n + 1))
            nc.tensor.matmul(k.ps[:, 1, :], k.c("ones"), k.scr[:, n % 4, :], start=(n == 0),
                             stop=(n == KD - 1)).then_inc(self.summed, 1)

    def wait_tile(self, pe, c):
        pe.wait_ge(self.lo, self.k.at(self.lo, c + 1))

    def vector(self, dve):
        k, nc = self.k, self.k.nc
        dve.wait_ge(self.added, k.at(self.added, 1))
        for n in range(KD):
            nc.vector.scalar_tensor_tensor(k.x[:, n, :], k.ps[:, 0, :], -1.0 / D, k.x[:, n, :], ALU.mult,
                                           ALU.add).then_inc(self.centred, 1)
        dve.wait_ge(self.rooted, k.at(self.rooted, 1))
        for n in range(KD + 1):
            if n < KD:
                nc.vector.scalar_tensor_tensor(k.x[:, n, :], k.x[:, n, :], self.gain_at[n], k.scr[:, 8, :],
                                               ALU.mult, ALU.mult).then_inc(self.normed, 1)
            if self.split and n >= 1:
                dve.wait_ge(self.hi, k.at(self.hi, n))
                nc.vector.scalar_tensor_tensor(k.in_lo[:, n - 1, :], k.x[:, n - 1, :], self.shift_at[n - 1],
                                               k.in_hi[:, n - 1, :].bitcast(F32), ALU.add, ALU.subtract)\
                    .then_inc(self.lo, 1)

    def scalar(self, act):
        k, nc = self.k, self.k.nc
        for n in range(KD):
            act.wait_ge(self.centred, k.at(self.centred, n + 1))
            if n >= 4:
                act.wait_ge(self.summed, k.at(self.summed, n - 3))
            nc.scalar.activation(k.scr[:, n % 4, :], k.x[:, n, :], ACT.Square).then_inc(self.squared, 1)
        act.wait_ge(self.summed, k.at(self.summed, KD))
        nc.scalar.activation(k.scr[:, 8, :], k.ps[:, 1, :], ACT.Ln, bias=k.c("ln_eps"), scale=1.0 / D)\
            .then_inc(self.logged, 1)
        act.wait_ge(self.logged, k.at(self.logged, 1))
        nc.scalar.activation(k.scr[:, 8, :], k.scr[:, 8, :], ACT.Exp, scale=-0.5).then_inc(self.rooted, 1)
        for n in range(KD) if self.split else ():
            act.wait_ge(self.normed, k.at(self.normed, n + 1))
            nc.scalar.activation(k.in_hi[:, n, :], k.x[:, n, :], ACT.Identity, bias=self.shift_at[n])\
                .then_inc(self.hi, 1)
        for n in range(KD):
            if self.split:
                act.wait_ge(self.lo, k.at(self.lo, n + 1))
            else:
                act.wait_ge(self.normed, k.at(self.normed, n + 1))
            nc.scalar.activation(k.x[:, n, :], k.x[:, n, :], ACT.Identity, bias=self.shift_at[n])\
                .then_inc(self.shifted, 1)

    def passed(self):
        parts = KD if self.split else 0
        self.k.passed(norm_hi=parts, norm_lo=parts, added=1, centred=KD, squared=KD, summed=KD, rooted=1, normed=KD,
                      norm_logged=1, shifted=KD)


def output_phase(k, gain, shift, out):
    norm = LayerNorm(k, gain, shift, split=False)
    sent = k.flag("output_sent")
    with k.nc.Block() as block:
        @block.scalar
        def _(act):
            norm.scalar(act)

        @block.tensor
        def _(pe):
            norm.tensor(pe)

        @block.vector
        def _(dve):
            norm.vector(dve)

        @block.sync
        def _(sp):
            for n in range(KD):
                sp.wait_ge(norm.shifted, k.at(norm.shifted, n + 1))
                sp.dma_start(out[n], k.x[:, n, :]).then_inc(sent, 16)
            sp.wait_ge(sent, k.at(sent, 16 * KD))
    norm.passed()


def glu_phase(k, up, down, norm=None):
    nc = k.nc
    ends = k.use([range(a, a + KD) for pair in up for a in pair] + [range(a, a + KF2) for a in down])
    silu, hidden, hi_ready, lo_ready, resid = [k.flag(n) for n in (
        "silu_done", "hidden_made", "hi_ready", "lo_ready", "resid_added")]
    made = lambda f: k.big[:, KF2 + f, :]
    hi, lo = lambda f: k.parts[:, f, :], lambda f: k.parts[:, KF2 + f, :]
    with nc.Block() as block:
        @block.sync
        def _(sp):
            k.load_slabs(sp)

        @block.tensor
        def _(pe):
            def hidden_tile(pe, c):
                pe.wait_ge(lo_ready, k.at(lo_ready, c + 1))

            if norm:
                norm.tensor(pe)
            x = lambda c: (k.in_hi[:, c, :], k.in_lo[:, c, :])
            for f, pair in enumerate(up):
                if f >= 2:
                    pe.wait_ge(hidden, k.at(hidden, f - 1))
                for b, at in enumerate(pair):
                    add_up(k, pe, k.ps[:, 2 * (f % 2) + b, :], [(at + c, x(c)) for c in range(KD)],
                           norm.wait_tile if norm and f == b == 0 else None)
            for j, at in enumerate(down):
                if j >= 2:
                    pe.wait_ge(resid, k.at(resid, j - 1))
                add_up(k, pe, k.ps[:, 4 + j % 2, :], [(at + c, (hi(c), lo(c))) for c in range(KF2)],
                       hidden_tile if j == 0 else None)

        @block.scalar
        def _(act):
            if norm:
                norm.scalar(act)
            for f in range(KF2 + 1):
                if f < KF2:
                    k.high_slabs(act, up[f][1])
                    act.wait_ge(k.sums_done, ends[2 * f])
                    if f >= 2:
                        act.wait_ge(hidden, k.at(hidden, f - 1))
                    nc.scalar.activation(k.scr[:, f % 2, :], k.ps[:, 2 * (f % 2), :], ACT.Silu).then_inc(silu, 1)
                if f >= 1:
                    act.wait_ge(hidden, k.at(hidden, f))
                    nc.scalar.activation(hi(f - 1), made(f - 1), ACT.Copy).then_inc(hi_ready, 1)
            k.high_slabs(act, down[-1] + KF2 - 1)

        @block.vector
        def _(dve):
            if norm:
                norm.vector(dve)
            for f in range(KF2 + 1):
                if f < KF2:
                    dve.wait_ge(silu, k.at(silu, f + 1))
                    dve.wait_ge(k.sums_done, ends[2 * f + 1])
                    nc.vector.scalar_tensor_tensor(made(f), k.ps[:, 2 * (f % 2) + 1, :], 0.5, k.scr[:, f % 2, :],
                                                   ALU.mult, ALU.mult).then_inc(hidden, 1)
                if f >= 1:
                    dve.wait_ge(hi_ready, k.at(hi_ready, f))
                    nc.vector.tensor_tensor(lo(f - 1), made(f - 1), hi(f - 1).bitcast(F32), ALU.subtract)\
                        .then_inc(lo_ready, 1)
            for j in range(KD):
                dve.wait_ge(k.sums_done, ends[2 * KF2 + j])
                nc.vector.scalar_tensor_tensor(k.x[:, j, :], k.x[:, j, :], ALPHA, k.ps[:, 4 + j % 2, :],
                                               ALU.mult, ALU.add).then_inc(resid, 1)

        @block.gpsimd
        def _(pool):
            k.low_slabs(pool)
    if norm:
        norm.passed()
    k.passed(silu_done=KF2, hidden_made=KF2, hi_ready=KF2, lo_ready=KF2, resid_added=KD)


def relu2_phase(k, up, down, norm=None):
    nc = k.nc
    n = len(up)
    ends = k.use([range(a, a + KD) for a in up] + [range(a, a + n) for a in down])
    relu, hidden, hi_ready, lo_ready, resid = [k.flag(x) for x in (
        "relu_done", "hidden_made", "hi_ready", "lo_ready", "resid_added")]
    made = lambda f: k.big[:, n + f, :]
    hi, lo = lambda f: k.parts[:, f, :], lambda f: k.parts[:, n + f, :]
    with nc.Block() as block:
        @block.sync
        def _(sp):
            k.load_slabs(sp)

        @block.tensor
        def _(pe):
            def hidden_tile(pe, c):
                pe.wait_ge(lo_ready, k.at(lo_ready, c + 1))

            if norm:
                norm.tensor(pe)
            for f, at in enumerate(up):
                if f >= 4:
                    pe.wait_ge(hidden, k.at(hidden, f - 3))
                add_up(k, pe, k.ps[:, f % 4, :], [(at + c, (k.in_hi[:, c, :], k.in_lo[:, c, :])) for c in range(KD)],
                       norm.wait_tile if norm and f == 0 else None)
            for j, at in enumerate(down):
                if j >= 2:
                    pe.wait_ge(resid, k.at(resid, j - 1))
                add_up(k, pe, k.ps[:, 4 + j % 2, :], [(at + c, (hi(c), lo(c))) for c in range(n)],
                       hidden_tile if j == 0 else None)

        @block.scalar
        def _(act):
            if norm:
                norm.scalar(act)
            for f in range(n + 1):
                if f < n:
                    k.high_slabs(act, up[f])
                    act.wait_ge(k.sums_done, ends[f])
                    if f >= 2:
                        act.wait_ge(hidden, k.at(hidden, f - 1))
                    nc.scalar.activation(k.scr[:, f % 2, :], k.ps[:, f % 4, :], ACT.Relu).then_inc(relu, 1)
                if f >= 1:
                    act.wait_ge(hidden, k.at(hidden, f))
                    nc.scalar.activation(hi(f - 1), made(f - 1), ACT.Copy).then_inc(hi_ready, 1)
            k.high_slabs(act, down[-1] + n - 1)

        @block.vector
        def _(dve):
            if norm:
                norm.vector(dve)
            for f in range(n + 1):
                if f < n:
                    dve.wait_ge(relu, k.at(relu, f + 1))
                    nc.vector.tensor_tensor(made(f), k.ps[:, f % 4, :], k.scr[:, f % 2, :], ALU.mult)\
                        .then_inc(hidden, 1)
                if f >= 1:
                    dve.wait_ge(hi_ready, k.at(hi_ready, f))
                    nc.vector.tensor_tensor(lo(f - 1), made(f - 1), hi(f - 1).bitcast(F32), ALU.subtract)\
                        .then_inc(lo_ready, 1)
            for j in range(KD):
                dve.wait_ge(k.sums_done, ends[n + j])
                nc.vector.tensor_tensor(k.x[:, j, :], k.x[:, j, :], k.ps[:, 4 + j % 2, :], ALU.add)\
                    .then_inc(resid, 1)

        @block.gpsimd
        def _(pool):
            k.low_slabs(pool)
    if norm:
        norm.passed()
    k.passed(relu_done=n, hidden_made=n, hi_ready=n, lo_ready=n, resid_added=KD)


def split_phase(k, items):
    nc = k.nc
    hi_ready, lo_ready = k.flag("hi_ready"), k.flag("lo_ready")
    with nc.Block() as block:
        @block.scalar
        def _(act):
            for t, hi, _ in items:
                nc.scalar.activation(hi, t, ACT.Copy).then_inc(hi_ready, 1)

        @block.vector
        def _(dve):
            for n, (t, hi, lo) in enumerate(items):
                dve.wait_ge(hi_ready, k.at(hi_ready, n + 1))
                nc.vector.tensor_tensor(lo, t, hi.bitcast(F32), ALU.subtract).then_inc(lo_ready, 1)
    k.passed(hi_ready=len(items), lo_ready=len(items))


def project_phase(k, tiles, alpha, parts, norm=None):
    nc = k.nc
    ends = k.use([range(a, a + KD) for a in tiles])
    resid = k.flag("resid_added")
    with nc.Block() as block:
        @block.sync
        def _(sp):
            k.load_slabs(sp)

        @block.tensor
        def _(pe):
            if norm:
                norm.tensor(pe)
            for j, at in enumerate(tiles):
                if j >= 4:
                    pe.wait_ge(resid, k.at(resid, j - 3))
                add_up(k, pe, k.ps[:, j % 4, :], [(at + c, parts(c)) for c in range(KD)],
                       norm.wait_tile if norm and j == 0 else None)

        @block.scalar
        def _(act):
            if norm:
                norm.scalar(act)
            k.high_slabs(act, tiles[-1] + KD - 1)

        @block.vector
        def _(dve):
            if norm:
                norm.vector(dve)
            for j in range(len(tiles)):
                dve.wait_ge(k.sums_done, ends[j])
                nc.vector.scalar_tensor_tensor(k.x[:, j, :], k.x[:, j, :], alpha, k.ps[:, j % 4, :],
                                               ALU.mult, ALU.add).then_inc(resid, 1)

        @block.gpsimd
        def _(pool):
            k.low_slabs(pool)
    if norm:
        norm.passed()
    k.passed(resid_added=len(tiles))


def merge_phase(k, tiles, y, out):
    nc = k.nc
    ends = k.use([r for g, b in tiles for r in (range(g, g + KD), range(b, b + 4))])
    gate, merged, product = [k.flag(n) for n in ("gate_ready", "merged", "gated_product")]
    n_jobs = len(tiles)
    with nc.Block() as block:
        @block.sync
        def _(sp):
            k.load_slabs(sp)

        @block.tensor
        def _(pe):
            for j, (g, b) in enumerate(tiles):
                if j >= 2:
                    pe.wait_ge(product, k.at(product, j - 1))
                add_up(k, pe, k.ps[:, 2 * (j % 2), :], [(g + c, (k.in_hi[:, c, :], k.in_lo[:, c, :]))
                                                        for c in range(KD)])
                add_up(k, pe, k.ps[:, 2 * (j % 2) + 1, :], [(b + c, y(j % 4, c)) for c in range(4)])

        @block.scalar
        def _(act):
            for j in range(n_jobs):
                k.high_slabs(act, tiles[j][1] + 3)
                act.wait_ge(k.sums_done, ends[2 * j])
                if j >= 2:
                    act.wait_ge(product, k.at(product, j - 1))
                d, n = divmod(j, 4)
                nc.scalar.activation(k.scr[:, j % 2, :], k.ps[:, 2 * (j % 2), :], ACT.Sigmoid,
                                     bias=k.v("b_gates", 8 * n + d)).then_inc(gate, 1)

        @block.vector
        def _(dve):
            for j in range(n_jobs):
                d, n = divmod(j, 4)
                dve.wait_ge(gate, k.at(gate, j + 1))
                dve.wait_ge(k.sums_done, ends[2 * j + 1])
                to = out(d) if n == 0 else k.scr[:, 2 + j % 2, :]
                if n > 0 and j > 4:
                    dve.wait_ge(merged, k.at(merged, j - 1 - (j - 2) // 4 - 1))
                nc.vector.tensor_tensor(to, k.scr[:, j % 2, :], k.ps[:, 2 * (j % 2) + 1, :], ALU.mult)\
                    .then_inc(product, 1)
                if n > 0:
                    dve.wait_ge(product, k.at(product, j + 1))
                    if n > 1:
                        dve.wait_ge(merged, k.at(merged, 3 * d + n - 1))
                    nc.vector.tensor_tensor(out(d), out(d), to, ALU.add).then_inc(merged, 1)

        @block.gpsimd
        def _(pool):
            k.low_slabs(pool)
    k.passed(gate_ready=n_jobs, gated_product=n_jobs, merged=3 * n_jobs // 4)


def mlstm_phase(k, q, key, v, f_row, i_row, f_fx, y):
    nc = k.nc
    names = ("soft", "log_f", "run_f", "u_ready", "m_ready", "m_sum", "stabil", "u_turned", "u_col", "fx_copied",
             "max_row", "scored", "arg_ready", "weight", "tri_done", "weighted", "head_summed", "em_row", "abs_den",
             "den_ready", "den_inv", "head_done", "unit_summed")
    s = {n: k.flag(n) for n in names}
    tmp, run_f, u, m, em = [k.scr[:, i, :] for i in range(5)]
    ucol = k.stat[:, 0, 0:16]
    units = [(h, b) for h in range(HEADS) for b in range(QB)]
    n = len(units)
    one = k.c("one").broadcast_to([P, T])
    one4 = k.c("one", 4).broadcast_to([4, T])
    with nc.Block() as block:
        @block.scalar
        def _(act):
            nc.scalar.activation(tmp, f_row, ACT.Abs).then_inc(s["soft"], 1)
            act.wait_ge(s["soft"], k.at(s["soft"], 1))
            nc.scalar.activation(tmp, tmp, ACT.Exp, scale=-1.0).then_inc(s["soft"], 1)
            act.wait_ge(s["soft"], k.at(s["soft"], 2))
            nc.scalar.activation(tmp, tmp, ACT.Ln, bias=1.0).then_inc(s["soft"], 1)
            act.wait_ge(s["m_sum"], k.at(s["m_sum"], 1))
            nc.scalar.activation(em[0:4], em[0:4], ACT.Exp, scale=-1.0).then_inc(s["stabil"], 1)
            act.wait_ge(s["u_turned"], k.at(s["u_turned"], 1))
            nc.scalar.activation(ucol, k.ps[:, 0, 0:16], ACT.Copy).then_inc(s["u_col"], 1)
            for i in range(n + 2):
                if i < n:
                    e = k.scr[:, 6 + i % 2, 0:T - P * units[i][1]]
                    act.wait_ge(s["arg_ready"], k.at(s["arg_ready"], i + 1))
                    nc.scalar.activation(e, e, ACT.Exp).then_inc(s["weight"], 1)
                if i >= 5 and (i - 5) % 4 == 0:
                    h = (i - 5) // 4
                    act.wait_ge(s["head_summed"], k.at(s["head_summed"], h + 1))
                    if h >= 1:
                        act.wait_ge(s["den_ready"], k.at(s["den_ready"], h))
                    nc.scalar.activation(k.scr[:, 10, :], k.ps[:, 6 + h % 2, :], ACT.Abs)\
                        .then_inc(s["abs_den"], 1)

        @block.tensor
        def _(pe):
            pe.wait_ge(s["u_ready"], k.at(s["u_ready"], 1))
            for b in range(QB):
                mm = nc.tensor.transpose(k.ps[:, 0, 4 * b:4 * b + 4], u[0:4, P * b:P * b + P], k.c("ident", 4)[:, 0:4])
            mm.then_inc(s["u_turned"], 1)
            pe.wait_ge(s["m_ready"], k.at(s["m_ready"], 1))
            pe.wait_ge(s["u_col"], k.at(s["u_col"], 1))
            pe.wait_ge(s["stabil"], k.at(s["stabil"], 1))
            for i in range(n + 1):
                if i < n:
                    h, b = units[i]
                    if b == 0:
                        if h >= 2:
                            pe.wait_ge(s["head_done"], k.at(s["head_done"], h - 1))
                        nc.tensor.matmul(k.ps[:, h % 2, :], k.c("negident", 4)[:, h:h + 1].broadcast_to([4, P]),
                                         m[0:4], start=True, stop=True).then_inc(s["max_row"], 1)
                    if i >= 2:
                        pe.wait_ge(s["weighted"], k.at(s["weighted"], i - 1))
                    nc.tensor.matmul(k.ps[:, 2 + i % 2, 0:T - P * b], key(h)[:, P * b:P * b + P], q(h)[:, P * b:T],
                                     start=True, stop=True).then_inc(s["scored"], 1)
                if i >= 1:
                    h, b = units[i - 1]
                    w = k.scr[:, 8 + (i - 1) % 2, 0:T - P * b]
                    pe.wait_ge(s["weighted"], k.at(s["weighted"], i))
                    if b == 0 and h >= 2:
                        pe.wait_ge(s["head_done"], k.at(s["head_done"], h - 1))
                    nc.tensor.matmul(k.ps[:, 4 + h % 2, P * b:T], v(b, h), w, start=(b == 0), stop=(b == QB - 1))
                    nc.tensor.matmul(k.ps[:, 6 + h % 2, P * b:T], k.c("ones"), w, start=(b == 0),
                                     stop=(b == QB - 1)).then_inc(s["unit_summed"], 1)
                    if b == QB - 1:
                        nc.tensor.matmul(k.ps[:, h % 2, :], k.c("ident", 4)[:, h:h + 1].broadcast_to([4, P]),
                                         em[0:4], start=True, stop=True).then_inc(s["head_summed"], 1)

        @block.vector
        def _(dve):
            dve.wait_ge(s["soft"], k.at(s["soft"], 3))
            nc.vector.scalar_tensor_tensor(tmp, f_row, 0.0, tmp, ALU.min, ALU.subtract).then_inc(s["log_f"], 1)
            dve.wait_ge(s["log_f"], k.at(s["log_f"], 1))
            nc.vector.tensor_tensor_scan(run_f, one, tmp, 0.0, ALU.mult, ALU.add).then_inc(s["run_f"], 1)
            dve.wait_ge(s["run_f"], k.at(s["run_f"], 1))
            nc.vector.tensor_copy(f_fx[0:4], run_f[32:36]).then_inc(s["fx_copied"], 1)
            nc.vector.tensor_tensor(u[0:4], i_row[0:4], run_f[0:4], ALU.subtract).then_inc(s["u_ready"], 1)
            dve.wait_ge(s["u_ready"], k.at(s["u_ready"], 1))
            nc.vector.tensor_tensor_scan(m[0:4], one4, u[0:4], 0.0, ALU.mult, ALU.max).then_inc(s["m_ready"], 1)
            dve.wait_ge(s["m_ready"], k.at(s["m_ready"], 1))
            nc.vector.tensor_tensor(em[0:4], run_f[0:4], m[0:4], ALU.add).then_inc(s["m_sum"], 1)
            dve.wait_ge(s["u_col"], k.at(s["u_col"], 1))

            def argument(i):
                h, b = units[i]
                if b == 0:
                    dve.wait_ge(s["max_row"], k.at(s["max_row"], h + 1))
                if i >= 2:
                    dve.wait_ge(s["weighted"], k.at(s["weighted"], i - 1))
                nc.vector.tensor_scalar(k.scr[:, 6 + i % 2, 0:T - P * b], k.ps[:, h % 2, P * b:T],
                                        ucol[:, 4 * b + h:4 * b + h + 1], 0.0, ALU.add, ALU.min)\
                    .then_inc(s["arg_ready"], 1)

            argument(0)
            for i in range(n + 2):
                if i + 1 < n:
                    argument(i + 1)
                if i < n:
                    h, b = units[i]
                    e = k.scr[:, 6 + i % 2, :]
                    dve.wait_ge(s["weight"], k.at(s["weight"], i + 1))
                    nc.vector.tensor_tensor(e[:, 0:P], e[:, 0:P], k.c("tri"), ALU.mult).then_inc(s["tri_done"], 1)
                    dve.wait_ge(s["tri_done"], k.at(s["tri_done"], i + 1))
                    dve.wait_ge(s["scored"], k.at(s["scored"], i + 1))
                    if i >= 2:
                        dve.wait_ge(s["unit_summed"], k.at(s["unit_summed"], i - 1))
                    nc.vector.scalar_tensor_tensor(k.scr[:, 8 + i % 2, 0:T - P * b],
                                                   k.ps[:, 2 + i % 2, 0:T - P * b], P ** -0.5,
                                                   e[:, 0:T - P * b], ALU.mult, ALU.mult)\
                        .then_inc(s["weighted"], 1)
                if i >= 5 and (i - 5) % 4 == 0:
                    h = (i - 5) // 4
                    den = k.scr[:, 11, :]
                    dve.wait_ge(s["abs_den"], k.at(s["abs_den"], h + 1))
                    nc.vector.tensor_tensor(den, k.scr[:, 10, :], k.ps[:, h % 2, :], ALU.max)\
                        .then_inc(s["den_ready"], 1)
                    dve.wait_ge(s["den_ready"], k.at(s["den_ready"], h + 1))
                    nc.vector.reciprocal(den, den).then_inc(s["den_inv"], 1)
                    dve.wait_ge(s["den_inv"], k.at(s["den_inv"], h + 1))
                    nc.vector.tensor_tensor(y(h), den, k.ps[:, 4 + h % 2, :], ALU.mult)\
                        .then_inc(s["head_done"], 1)
    k.passed(soft=3, log_f=1, run_f=1, u_ready=1, m_ready=1, m_sum=1, stabil=1, u_turned=1, u_col=1, fx_copied=1,
             max_row=HEADS, scored=n, arg_ready=n, weight=n, tri_done=n, weighted=n, head_summed=HEADS,
             abs_den=HEADS, den_ready=HEADS, den_inv=HEADS, head_done=HEADS, unit_summed=n)


class Unit:

    def __init__(self, scores, width, values, group, first, last, rows, out, scale, mask=None, keep=None, gate=None):
        self.scores, self.width, self.values = scores, width, values
        self.group, self.first, self.last, self.rows, self.out = group, first, last, rows, out
        self.scale, self.mask, self.keep, self.gate = scale, mask, keep, gate
        self.blocks = [(a, min(P, width - a)) for a in range(0, width, P)]


def attend(k, pe, u, n, units, probs, ready, turned, laid, unit_done, stored):
    nc = k.nc
    if 0 <= u < n:
        pe.wait_ge(ready, k.at(ready, u + 1))
        if u >= 2:
            pe.wait_ge(laid, k.at(laid, u - 1))
        for a, w in units[u].blocks:
            mm = nc.tensor.transpose(k.ps[0:w, 3 + u % 2, a:a + P], probs(u)[:, a:a + w], k.c("ident"))
        mm.then_inc(turned, 1)
    if 0 <= u - 1 < n:
        one = units[u - 1]
        pe.wait_ge(laid, k.at(laid, u))
        if one.first and one.group >= 3:
            pe.wait_ge(stored, k.at(stored, one.group - 2))
        lo, hi = one.rows
        for j, ((a, w), val) in enumerate(zip(one.blocks, one.values)):
            mm = nc.tensor.matmul(k.ps[lo:hi, 5 + one.group % 3, 0:P], val, k.scr[0:w, 6 + (u - 1) % 2, a:a + P],
                                  start=(one.first and j == 0), stop=(one.last and j == len(one.blocks) - 1))
        mm.then_inc(unit_done, 1)


def lay_and_store(k, act, u, n, units, turned, laid, unit_done, stored):
    nc = k.nc
    if 0 <= u < n:
        act.wait_ge(turned, k.at(turned, u + 1))
        if u >= 2:
            act.wait_ge(unit_done, k.at(unit_done, u - 1))
        rows = units[u].blocks[0][1]
        cols = P * len(units[u].blocks)
        nc.scalar.activation(k.scr[0:rows, 6 + u % 2, 0:cols], k.ps[0:rows, 3 + u % 2, 0:cols], ACT.Copy)\
            .then_inc(laid, 1)
    if 0 <= u - 2 < n and units[u - 2].last:
        one = units[u - 2]
        lo, hi = one.rows
        act.wait_ge(unit_done, k.at(unit_done, u - 1))
        nc.scalar.activation(one.out, k.ps[lo:hi, 5 + one.group % 3, 0:P], ACT.Copy).then_inc(stored, 1)


def attention_phase(k, units):
    nc = k.nc
    scored, masked, row_max, expd, row_inv, row_gate, probs_ready, turned, laid, unit_done, stored = [
        k.flag(n) for n in ("scored", "masked", "row_max", "probs_expd", "row_inv", "row_gate", "probs_ready",
                              "turned", "laid", "unit_done", "stored")]
    n = len(units)
    ring, lag = 6, 3
    probs = lambda i: k.scr[:, i % ring, :]
    col = lambda kind, i: k.stat[:, kind, i:i + 1]
    gates = [sum(1 for u in units[:i + 1] if u.gate is not None) for i in range(n)]
    groups = sum(1 for u in units if u.last)
    assert n <= 64
    with nc.Block() as block:
        @block.tensor
        def _(pe):
            for i in range(n + lag + 1):
                if i < n:
                    u = units[i]
                    if i >= 3:
                        pe.wait_ge(masked, k.at(masked, i - 2))
                    for j, (lhsT, rhs) in enumerate(u.scores):
                        mm = nc.tensor.matmul(k.ps[:, i % 3, 0:u.width], lhsT, rhs, start=(j == 0),
                                              stop=(j == len(u.scores) - 1))
                    mm.then_inc(scored, 1)
                attend(k, pe, i - lag, n, units, probs, probs_ready, turned, laid, unit_done, stored)

        @block.vector
        def _(dve):
            for i in range(n + 1):
                if i < n:
                    u = units[i]
                    s = probs(i)[:, 0:u.width]
                    dve.wait_ge(scored, k.at(scored, i + 1))
                    if i >= ring:
                        dve.wait_ge(turned, k.at(turned, i - ring + 1))
                    nc.vector.scalar_tensor_tensor(s, k.ps[:, i % 3, 0:u.width], u.scale, u.mask, ALU.mult, ALU.add)\
                        .then_inc(masked, 1)
                    dve.wait_ge(masked, k.at(masked, i + 1))
                    nc.vector.tensor_reduce(col(0, i), s, AX, ALU.max, negate=True).then_inc(row_max, 1)
                if i >= 1:
                    u = units[i - 1]
                    p = probs(i - 1)[:, 0:u.width]
                    inv = col(1, i - 1)
                    dve.wait_ge(expd, k.at(expd, i))
                    nc.vector.reciprocal(inv, inv).then_inc(row_inv, 1)
                    dve.wait_ge(row_inv, k.at(row_inv, i))
                    if u.gate is not None:
                        nc.vector.tensor_tensor(inv, inv, u.gate, ALU.mult).then_inc(row_gate, 1)
                        dve.wait_ge(row_gate, k.at(row_gate, gates[i - 1]))
                    if u.keep is None:
                        nc.vector.tensor_scalar(p, p, inv, None, ALU.mult).then_inc(probs_ready, 1)
                    else:
                        nc.vector.scalar_tensor_tensor(p, p, inv, u.keep, ALU.mult, ALU.mult)\
                            .then_inc(probs_ready, 1)

        @block.scalar
        def _(act):
            for i in range(n + lag + 2):
                if i < n:
                    p = probs(i)[:, 0:units[i].width]
                    act.wait_ge(row_max, k.at(row_max, i + 1))
                    nc.scalar.activation(p, p, ACT.Exp, bias=col(0, i), accum_out=col(1, i)).then_inc(expd, 1)
                lay_and_store(k, act, i - lag, n, units, turned, laid, unit_done, stored)
    k.passed(scored=n, masked=n, row_max=n, probs_expd=n, row_inv=n, row_gate=gates[-1], probs_ready=n, turned=n,
             laid=n, unit_done=n, stored=groups)


def stick_phase(k, units, probs, soft_at, index):
    nc = k.nc
    scored, masked, soft, logged, broken, rest, exponent, probs_ready, turned, laid, unit_done, stored = [
        k.flag(n) for n in ("scored", "masked", "soft", "logged", "broken", "rest", "exponent", "probs_ready",
                              "turned", "laid", "unit_done", "stored")]
    n, batch = len(units), 4
    ring = 3 * batch
    batches = n // batch
    steps = TOP_STEPS * (QB - 1)
    rest_at = lambda i: k.scr[:, 8 + i % 2, :]
    groups = sum(1 for u in units if u.last)
    with nc.Block() as block:
        @block.tensor
        def _(pe):
            for i in range(n + 2 * batch + 1):
                if i < n:
                    u = units[i]
                    if i >= 3:
                        pe.wait_ge(masked, k.at(masked, i - 2))
                    nc.tensor.matmul(k.ps[:, i % 3, 0:u.width], u.scores[0][0], u.scores[0][1], start=True,
                                     stop=True).then_inc(scored, 1)
                attend(k, pe, i - 2 * batch, n, units, probs, probs_ready, turned, laid, unit_done, stored)

        @block.vector
        def _(dve):
            for g in range(batches + 1):
                for i in range(batch * g, batch * (g + 1)) if g < batches else ():
                    u = units[i]
                    dve.wait_ge(scored, k.at(scored, i + 1))
                    if i >= ring:
                        dve.wait_ge(turned, k.at(turned, i - ring + 1))
                    nc.vector.scalar_tensor_tensor(probs(i)[:, 0:u.width], k.ps[:, i % 3, 0:u.width], u.scale,
                                                   u.mask, ALU.mult, ALU.add).then_inc(masked, 1)
                take_top(k, dve, index, range(steps * g // (batches + 1), steps * (g + 1) // (batches + 1)))
                for i in range(batch * (g - 1), batch * g) if g >= 1 else ():
                    w = units[i].width
                    z, l, r = [x(i)[:, 0:w] for x in (probs, soft_at, rest_at)]
                    dve.wait_ge(logged, k.at(logged, i + 1))
                    nc.vector.scalar_tensor_tensor(l, z, 0.0, l, ALU.max, ALU.add).then_inc(broken, 1)
                    dve.wait_ge(broken, k.at(broken, i + 1))
                    nc.vector.tensor_tensor_scan(r[:, ::-1], k.c("one").broadcast_to([P, w]), l[:, ::-1], 0.0,
                                                 ALU.mult, ALU.add).then_inc(rest, 1)
                    dve.wait_ge(rest, k.at(rest, i + 1))
                    nc.vector.tensor_tensor(z, z, r, ALU.subtract).then_inc(exponent, 1)

        @block.scalar
        def _(act):
            for g in range(batches + 2):
                new = range(batch * g, batch * (g + 1)) if g < batches else ()
                old = range(batch * (g - 1), batch * g) if 1 <= g <= batches else ()
                for i in new:
                    z, l = probs(i)[:, 0:units[i].width], soft_at(i)[:, 0:units[i].width]
                    act.wait_ge(masked, k.at(masked, i + 1))
                    if i >= batch:
                        act.wait_ge(rest, k.at(rest, i - batch + 1))
                    nc.scalar.activation(l, z, ACT.Abs).then_inc(soft, 1)
                    act.wait_ge(soft, k.at(soft, 2 * i + 1))
                    nc.scalar.activation(l, l, ACT.Exp, scale=-1.0).then_inc(soft, 1)
                for i in old:
                    p = probs(i)[:, 0:units[i].width]
                    act.wait_ge(exponent, k.at(exponent, i + 1))
                    nc.scalar.activation(p, p, ACT.Exp).then_inc(probs_ready, 1)
                for j in range(batch):
                    if new:
                        i = new[j]
                        l = soft_at(i)[:, 0:units[i].width]
                        act.wait_ge(soft, k.at(soft, 2 * i + 2))
                        nc.scalar.activation(l, l, ACT.Ln, bias=1.0).then_inc(logged, 1)
                    if g >= 1:
                        lay_and_store(k, act, batch * (g - 1) + j, n, units, turned, laid, unit_done, stored)
    k.passed(scored=n, masked=n, soft=2 * n, logged=n, broken=n, rest=n, exponent=n, probs_ready=n, turned=n,
             laid=n, unit_done=n, stored=groups, top8=steps, top8_taken=steps, select_made=QB - 1)


def conv_phase(k, padded, out):
    nc = k.nc
    edge, step = k.flag("edge"), k.flag("conv_step")
    with nc.Block() as block:
        @block.vector
        def _(dve):
            nc.vector.memset(padded[:, :, 0:3], 0.0).then_inc(edge, 1)
            dve.wait_ge(edge, k.at(edge, 1))
            done = 0
            for j in range(4):
                for t in range(4):
                    x = padded[:, j, t:t + T]
                    w = k.v("conv_w", 4 * t + j)
                    if t == 0:
                        nc.vector.tensor_scalar(out(j), x, w, k.v("conv_b", j), ALU.mult, ALU.add)\
                            .then_inc(step, 1)
                    else:
                        dve.wait_ge(step, k.at(step, done))
                        nc.vector.scalar_tensor_tensor(out(j), x, w, out(j), ALU.mult, ALU.add)\
                            .then_inc(step, 1)
                    done += 1
    k.passed(edge=1, conv_step=16)


def lru_phase(k, xc, r, i, ygate, u, sq, y):
    nc = k.nc
    s = {n: k.flag(n) for n in ("soft", "lam_min", "lam_ready", "tanh_done", "a_ready", "a_squared", "one_minus",
                                  "rooted", "gated_in", "u_ready", "scanned", "head_done")}
    tmp = k.v("tmp", 0, 4)
    with nc.Block() as block:
        @block.scalar
        def _(act):
            nc.scalar.activation(tmp, k.v("lam", 0, 4), ACT.Abs).then_inc(s["soft"], 1)
            act.wait_ge(s["soft"], k.at(s["soft"], 1))
            nc.scalar.activation(tmp, tmp, ACT.Exp, scale=-1.0).then_inc(s["soft"], 1)
            act.wait_ge(s["soft"], k.at(s["soft"], 2))
            nc.scalar.activation(tmp, tmp, ACT.Ln, bias=1.0).then_inc(s["soft"], 1)
            act.wait_ge(s["lam_ready"], k.at(s["lam_ready"], 1))
            for j in range(4):
                nc.scalar.activation(u(j), r(j), ACT.Tanh, scale=k.v("decay", j)).then_inc(s["tanh_done"], 1)
            for j in range(4):
                nc.scalar.activation(r(j), r(j), ACT.Exp, scale=k.v("decay", j)).then_inc(s["a_ready"], 1)
            for j in range(4):
                act.wait_ge(s["a_ready"], k.at(s["a_ready"], j + 1))
                nc.scalar.activation(sq(j), r(j), ACT.Square).then_inc(s["a_squared"], 1)
            for j in range(4):
                act.wait_ge(s["one_minus"], k.at(s["one_minus"], j + 1))
                nc.scalar.activation(u(j), u(j), ACT.Sqrt, scale=-1.0).then_inc(s["rooted"], 1)

        @block.vector
        def _(dve):
            dve.wait_ge(s["soft"], k.at(s["soft"], 3))
            nc.vector.scalar_tensor_tensor(tmp, k.v("lam", 0, 4), 0.0, tmp, ALU.min, ALU.subtract)\
                .then_inc(s["lam_min"], 1)
            dve.wait_ge(s["lam_min"], k.at(s["lam_min"], 1))
            nc.vector.tensor_scalar(k.v("decay", 0, 4), tmp, LRU_C, None, ALU.mult).then_inc(s["lam_ready"], 1)
            for j in range(4):
                dve.wait_ge(s["a_squared"], k.at(s["a_squared"], j + 1))
                nc.vector.scalar_tensor_tensor(u(j), sq(j), 1.0, u(j), ALU.add, ALU.mult)\
                    .then_inc(s["one_minus"], 1)
                nc.vector.tensor_tensor(i(j), i(j), xc(j), ALU.mult).then_inc(s["gated_in"], 1)
            for j in range(4):
                dve.wait_ge(s["rooted"], k.at(s["rooted"], j + 1))
                dve.wait_ge(s["gated_in"], k.at(s["gated_in"], j + 1))
                nc.vector.tensor_tensor(u(j), u(j), i(j), ALU.mult).then_inc(s["u_ready"], 1)
                dve.wait_ge(s["u_ready"], k.at(s["u_ready"], j + 1))
                nc.vector.tensor_tensor_scan(y(j), r(j), u(j), 0.0, ALU.mult, ALU.add).then_inc(s["scanned"], 1)
                dve.wait_ge(s["scanned"], k.at(s["scanned"], j + 1))
                nc.vector.tensor_tensor(y(j), y(j), ygate(j), ALU.mult).then_inc(s["head_done"], 1)
    k.passed(soft=3, lam_min=1, lam_ready=1, tanh_done=4, a_ready=4, a_squared=4, one_minus=4, rooted=4, gated_in=4,
             u_ready=4, scanned=4, head_done=4)


def gla_phase(k, q, key, v, z, bc, states, y):
    nc = k.nc
    s = {n: k.flag(n) for n in (
        "soft", "log_f", "run_f", "to_end", "fwd_exp", "back_exp", "end_exp", "q_scaled", "k_scaled", "k_end",
        "end_turned", "end_laid", "added", "state_zero", "state_ready", "scored", "weighted", "unit_summed",
        "stored")}
    fwd = lambda p: k.scr[:, p, :]
    kt = lambda p: k.scr[:, 2 + p, :]
    ke = lambda p: k.scr[:, 4 + p, :]
    ke_tok = lambda p: k.scr[:, 6 + p, :]
    tmp = lambda p: k.scr[:, 10 + p, :]
    at = lambda i: k.scr[:, 8 + i % 2, 0:P]
    chunks = lambda x: x.rearrange("p (c t) -> p c t", t=CHUNK)
    units = [(h, tb) for h in range(HEADS) for tb in range(QB)]
    n = len(units)
    with nc.Block() as block:
        @block.scalar
        def _(act):
            for p in range(2):
                nc.scalar.activation(tmp(p), z(p), ACT.Abs).then_inc(s["soft"], 1)
                act.wait_ge(s["soft"], k.at(s["soft"], 3 * p + 1))
                nc.scalar.activation(tmp(p), tmp(p), ACT.Exp, scale=-1.0).then_inc(s["soft"], 1)
                act.wait_ge(s["soft"], k.at(s["soft"], 3 * p + 2))
                nc.scalar.activation(tmp(p), tmp(p), ACT.Ln, bias=1.0).then_inc(s["soft"], 1)
            for p in range(2):
                act.wait_ge(s["run_f"], k.at(s["run_f"], p + 1))
                nc.scalar.activation(fwd(p), bc(p), ACT.Exp, scale=1.0 / GLA_TAU).then_inc(s["fwd_exp"], 1)
                nc.scalar.activation(kt(p), bc(p), ACT.Exp, scale=-1.0 / GLA_TAU).then_inc(s["back_exp"], 1)
                act.wait_ge(s["to_end"], k.at(s["to_end"], p + 1))
                nc.scalar.activation(ke(p), ke(p), ACT.Exp, scale=1.0 / GLA_TAU).then_inc(s["end_exp"], 1)
            for p in range(2):
                act.wait_ge(s["end_turned"], k.at(s["end_turned"], p + 1))
                nc.scalar.activation(ke_tok(p), k.ps[:, p, :], ACT.Copy).then_inc(s["end_laid"], 1)
            for h in range(HEADS):
                act.wait_ge(s["unit_summed"], k.at(s["unit_summed"], QB * (h + 1)))
                nc.scalar.activation(y(h), k.ps[:, 4 + h, :], ACT.Copy).then_inc(s["stored"], 1)

        @block.vector
        def _(dve):
            nc.vector.memset(states(0, 0), 0.0).then_inc(s["state_zero"], 1)
            nc.vector.memset(states(1, 0), 0.0).then_inc(s["state_zero"], 1)
            for p in range(2):
                dve.wait_ge(s["soft"], k.at(s["soft"], 3 * p + 3))
                nc.vector.scalar_tensor_tensor(z(p), z(p), 0.0, tmp(p), ALU.min, ALU.subtract)\
                    .then_inc(s["log_f"], 1)
                dve.wait_ge(s["log_f"], k.at(s["log_f"], p + 1))
                nc.vector.tensor_tensor_scan(bc(p), k.c("goes_on"), z(p), 0.0, ALU.mult, ALU.add)\
                    .then_inc(s["run_f"], 1)
                dve.wait_ge(s["run_f"], k.at(s["run_f"], p + 1))
                nc.vector.tensor_tensor(chunks(ke(p)), chunks(bc(p))[:, :, CHUNK - 1:CHUNK].broadcast_to(
                    [P, NCHUNK, CHUNK]), chunks(bc(p)), ALU.subtract).then_inc(s["to_end"], 1)
            for p in range(2):
                dve.wait_ge(s["end_exp"], k.at(s["end_exp"], p + 1))
                nc.vector.tensor_tensor(ke(p), ke(p), key(p), ALU.mult).then_inc(s["k_end"], 1)
                nc.vector.tensor_tensor(kt(p), kt(p), key(p), ALU.mult).then_inc(s["k_scaled"], 1)
                nc.vector.scalar_tensor_tensor(q(p), q(p), CHUNK ** -0.5, fwd(p), ALU.mult, ALU.mult)\
                    .then_inc(s["q_scaled"], 1)
            dve.wait_ge(s["state_zero"], k.at(s["state_zero"], 2))
            for c in range(NCHUNK - 1):
                for p in range(2):
                    if c > 0:
                        dve.wait_ge(s["state_ready"], k.at(s["state_ready"], 2 * (c - 1) + p + 1))
                    dve.wait_ge(s["added"], k.at(s["added"], p + 1))
                    nc.vector.scalar_tensor_tensor(
                        states(p, c + 1), states(p, c), fwd(p)[:, CHUNK * (c + 1) - 1:CHUNK * (c + 1)],
                        k.ps[:, 2 * p + c % 2, P * (c // 2):P * (c // 2) + P], ALU.mult, ALU.add)\
                        .then_inc(s["state_ready"], 1)
            for i in range(n):
                dve.wait_ge(s["scored"], k.at(s["scored"], i + 1))
                if i >= 2:
                    dve.wait_ge(s["unit_summed"], k.at(s["unit_summed"], i - 1))
                nc.vector.tensor_tensor(at(i), k.ps[:, i % 2, 0:P], k.c("chunk_tri"), ALU.mult)\
                    .then_inc(s["weighted"], 1)

        @block.tensor
        def _(pe):
            for p in range(2):
                pe.wait_ge(s["k_end"], k.at(s["k_end"], p + 1))
                for tb in range(QB):
                    mm = nc.tensor.transpose(k.ps[:, p, P * tb:P * tb + P], ke(p)[:, P * tb:P * tb + P], k.c("ident"))
                mm.then_inc(s["end_turned"], 1)
            pe.wait_ge(s["end_laid"], k.at(s["end_laid"], 2))
            for p in range(2):
                for c in range(NCHUNK):
                    lo = CHUNK * (c % 2)
                    for hh in range(2):
                        mm = nc.tensor.matmul(
                            k.ps[64 * hh:64 * hh + 64, 2 * p + c % 2, P * (c // 2):P * (c // 2) + P],
                            ke_tok(p)[lo:lo + CHUNK, P * (c // 2) + 64 * hh:P * (c // 2) + 64 * hh + 64],
                            v(c // 2, 2 * p + hh)[lo:lo + CHUNK], start=True, stop=True)
                mm.then_inc(s["added"], 1)
            pe.wait_ge(s["k_scaled"], k.at(s["k_scaled"], 2))
            pe.wait_ge(s["q_scaled"], k.at(s["q_scaled"], 2))
            pe.wait_ge(s["state_ready"], k.at(s["state_ready"], 2 * (NCHUNK - 1)))
            for i in range(n + 1):
                if i < n:
                    h, tb = units[i]
                    p, lo = h // 2, 64 * (h % 2)
                    if i >= 2:
                        pe.wait_ge(s["weighted"], k.at(s["weighted"], i - 1))
                    nc.tensor.matmul(k.ps[:, i % 2, 0:P], kt(p)[lo:lo + 64, P * tb:P * tb + P],
                                     q(p)[lo:lo + 64, P * tb:P * tb + P], start=True, stop=True)\
                        .then_inc(s["scored"], 1)
                if i >= 1:
                    h, tb = units[i - 1]
                    p, lo = h // 2, 64 * (h % 2)
                    pe.wait_ge(s["weighted"], k.at(s["weighted"], i))
                    nc.tensor.matmul(k.ps[:, 4 + h, P * tb:P * tb + P], v(tb, h), at(i - 1), start=True, stop=False)
                    for c in (2 * tb, 2 * tb + 1):
                        mm = nc.tensor.matmul(k.ps[:, 4 + h, CHUNK * c:CHUNK * c + CHUNK],
                                              states(p, c)[lo:lo + 64], q(p)[lo:lo + 64, CHUNK * c:CHUNK * c + CHUNK],
                                              start=False, stop=(c % 2 == 1))
                    mm.then_inc(s["unit_summed"], 1)
    k.passed(soft=6, log_f=2, run_f=2, to_end=2, fwd_exp=2, back_exp=2, end_exp=2, q_scaled=2, k_scaled=2, k_end=2,
             end_turned=2, end_laid=2, added=2, state_zero=2, state_ready=2 * (NCHUNK - 1), scored=n, weighted=n,
             unit_summed=n, stored=HEADS)


def compress_phase(k, kv, blk, w1, w2, hid, kc, vc, gates_in, gates):
    nc = k.nc
    ends = k.use([range(w1, w1 + 16), range(w1, w1 + 16), [w2], [w2]], by_slab=False)
    blocks, gelu, stored = k.flag("blocks_ready"), k.flag("gelu_done"), k.flag("stored")
    by_token = kv.rearrange("p (m s) -> p s m", s=CMP_STRIDE)
    with nc.Block() as block:
        @block.sync
        def _(sp):
            k.load_slabs(sp)

        @block.vector
        def _(dve):
            for a in range(2):
                pos = k.v("pos", CMP_STRIDE * a, CMP_STRIDE).unsqueeze(2).broadcast_to([P, CMP_STRIDE, NCMP])
                nc.vector.tensor_tensor(blk[:, CMP_STRIDE * a:CMP_STRIDE * (a + 1), :], by_token[:, :, a:a + NCMP], pos,
                                        ALU.add).then_inc(blocks, 1)

        @block.tensor
        def _(pe):
            pe.wait_ge(blocks, k.at(blocks, 2))
            for j, lo in enumerate((0, 64)):
                for l in range(CMP_LEN):
                    k.need(pe, w1 + l // 2)
                    mm = nc.tensor.matmul(k.ps[lo:lo + 64, j, 0:NCMP],
                                          k.raw_tile(w1 + l // 2)[lo:lo + 64, 64 * (l % 2):64 * (l % 2) + 64],
                                          blk[lo:lo + 64, l, :], start=(l == 0), stop=(l == CMP_LEN - 1))
                mm.then_inc(k.sums_done, 1)
            pe.wait_ge(gelu, k.at(gelu, 2))
            k.need(pe, w2)
            nc.tensor.matmul(k.ps[:, 2, 0:NCMP], k.raw_tile(w2)[0:64, :], hid[0:64, 0:NCMP], start=True, stop=True)\
                .then_inc(k.sums_done, 1)
            nc.tensor.matmul(k.ps[0:NCMP, 3, 0:64], hid[64:128, 0:NCMP], k.raw_tile(w2)[64:128, 0:64], start=True,
                             stop=True).then_inc(k.sums_done, 1)

        @block.scalar
        def _(act):
            nc.scalar.activation(gates, gates_in, ACT.Sigmoid).then_inc(stored, 1)
            for j, lo in enumerate((0, 64)):
                act.wait_ge(k.sums_done, ends[j])
                nc.scalar.activation(hid[lo:lo + 64, 0:NCMP], k.ps[lo:lo + 64, j, 0:NCMP], ACT.Gelu_apprx_tanh)\
                    .then_inc(gelu, 1)
            act.wait_ge(k.sums_done, ends[2])
            nc.scalar.activation(kc, k.ps[:, 2, 0:NCMP], ACT.Copy).then_inc(stored, 1)
            act.wait_ge(k.sums_done, ends[3])
            nc.scalar.activation(vc, k.ps[0:NCMP, 3, 0:64], ACT.Copy).then_inc(stored, 1)
    k.passed(blocks_ready=2, gelu_done=2, stored=3)


def index_phase(k, iq, ik, weight, index):
    nc = k.nc
    scored, relu, summed = [k.flag(n) for n in ("scored", "relu_done", "index_added")]
    units = [(qb, h) for qb in range(1, QB) for h in range(IDX_HEADS)]
    with nc.Block() as block:
        @block.tensor
        def _(pe):
            for i, (qb, h) in enumerate(units):
                lo = 32 * (h % 4)
                if i >= 4:
                    pe.wait_ge(relu, k.at(relu, i - 3))
                nc.tensor.matmul(k.ps[:, i % 4, 0:P * (qb + 1)], iq(h // 4)[lo:lo + 32, P * qb:P * qb + P],
                                 ik[lo:lo + 32, 0:P * (qb + 1)], start=True, stop=True,
                                 tile_position=(lo, 0)).then_inc(scored, 1)

        @block.scalar
        def _(act):
            for i, (qb, h) in enumerate(units):
                act.wait_ge(scored, k.at(scored, i + 1))
                if i >= 8:
                    act.wait_ge(summed, k.at(summed, i - 7 + (i - 8) // 8))
                nc.scalar.activation(k.scr[:, i % 8, 0:P * (qb + 1)], k.ps[:, i % 4, 0:P * (qb + 1)], ACT.Relu,
                                     scale=(IDX_HEADS * 32) ** -0.5).then_inc(relu, 1)

        @block.vector
        def _(dve):
            added = 0
            for i, (qb, h) in enumerate(units):
                w = P * (qb + 1)
                s = index(qb)[:, 0:w]
                r = k.scr[:, i % 8, 0:w]
                dve.wait_ge(relu, k.at(relu, i + 1))
                if h == 0:
                    nc.vector.tensor_scalar(s, r, weight(qb, h), None, ALU.mult).then_inc(summed, 1)
                else:
                    dve.wait_ge(summed, k.at(summed, added))
                    nc.vector.scalar_tensor_tensor(s, r, weight(qb, h), s, ALU.mult, ALU.add)\
                        .then_inc(summed, 1)
                added += 1
                if h < IDX_HEADS - 1:
                    continue
                dve.wait_ge(summed, k.at(summed, added))
                nc.vector.tensor_tensor(s, s, k.c("causal")[:, T - w:T], ALU.add).then_inc(summed, 1)
                added += 1
    k.passed(scored=len(units), relu_done=len(units), index_added=9 * (QB - 1))


def take_top(k, dve, index, steps):
    nc = k.nc
    top, taken = k.flag("top8"), k.flag("top8_taken")
    for t in steps:
        qb = 1 + t // TOP_STEPS
        s = index(qb)[:, 0:P * (qb + 1)]
        best = k.stat[:, 0, 0:8]
        if t > 0:
            dve.wait_ge(taken, k.at(taken, t))
        nc.vector.max(best, s).then_inc(top, 1)
        dve.wait_ge(top, k.at(top, t + 1))
        nc.vector.match_replace(s, best, s, TAKEN).then_inc(taken, 1)
        if t % TOP_STEPS == TOP_STEPS - 1:
            dve.wait_ge(taken, k.at(taken, t + 1))
            nc.vector.tensor_scalar(s, s, TAKEN / 2, NEG, ALU.is_ge, ALU.mult).then_inc(k.flag("select_made"), 1)


def copy_in_phase(k, sources):
    nc = k.nc
    here = k.flag("inputs_here")
    with nc.Block() as block:
        @block.sync
        def _(sp):
            for dst, src in sources:
                sp.dma_start(dst, src).then_inc(here, 16)
            sp.wait_ge(here, k.at(here, 16 * len(sources)))
            k.load_slabs(sp)
    k.passed(inputs_here=16 * len(sources))


def softmax_units(q, key, v, dims, width_of, masks, scale, group0, out, extra=None):
    units = []
    for h in range(HEADS):
        for qb in range(QB):
            w = P * (qb + 1)
            pairs = [(q(h)[:, P * qb:P * qb + P], key(h)[:, 0:w])] + (extra(h, w) if extra else [])
            lo = 64 * (h % 2) if dims == 64 else 0
            units.append(Unit(pairs, w, [v(kb, h) for kb in range(qb + 1)], group0 + QB * h + qb, True, True,
                              (lo, lo + dims), out(h)[lo:lo + dims, P * qb:P * qb + P], scale, mask=masks(qb)))
    return units


def token_job(k, act_tile, at, out):
    s = []
    for tb in range(QB):
        block = slice(P * tb, P * tb + P)
        s.append(([(act_tile(0)[:, block], k.raw_tile(at))], at, block, True, True))
    return {"sum": s, "out": out, "view": lambda bank: bank.rearrange("p (t n) -> p t n", n=P)}


def feature_job(k, act_tile, at, out, depth=KD, split=True, also=(), **more):
    s = []
    for c in range(depth):
        part = k.products(at + c, act_tile(c)) if split else [(k.raw_tile(at + c), act_tile(c))]
        s.append((part, at + c, slice(0, T), c == 0, c == depth - 1 and not also))
    if also:
        s.append(([also], None, slice(0, T), False, True))
    return {"sum": s, "out": out, **more}


def block_one(k):
    nc, big, scr, w = k.nc, k.big, k.scr, WHERE
    k.vec_cols = VEC1
    act = lambda c: (k.in_hi[:, c, :], k.in_lo[:, c, :])
    into = lambda g: [[(k.x[:, c, :], k.act[:, c, :], k.v(g, c), None) for c in range(KD)]]
    tile = lambda base: (lambda j: big[:, base + j, :])
    value = lambda base: (lambda tb, h: big[:, base + tb, P * h:P * h + P])
    small, i_row, f_fx = big[:, 40, :], big[:, 41, :], big[:, 42, :]
    y = lambda n, c: big[:, 12 + 4 * n + c, :]
    token_phase(k, act, [(w[key], lambda tb, n=n: big[:, 4 * n + tb, :], scr[:, 4 + n, :])
                         for n, key in enumerate(("mv", "fv", "gv"))],
                RmsNorm(k, into("norm1_g"), "rms_eps", D, parts=[act(c) for c in range(KD)]))
    jobs = []
    F = lambda key, j, out, **more: feature_job(k, act, w[key][j], out, bias=k.v("b_" + key, j), **more)
    jobs.append(feature_job(k, act, w["small"], small, bias=k.v("b_small")))
    jobs.append(feature_job(k, act, w["mi"], i_row, bias=k.v("b_mi")))
    for j in range(4):
        jobs.append(F("mq", j, big[:, 28 + j, :]))
    for j in range(4):
        jobs.append(F("mk", j, big[:, 32 + j, :]))
    for j in range(4):
        jobs.append(F("mo", j, big[:, 36 + j, :], func=ACT.Sigmoid))
    gemm_phase(k, jobs)
    mlstm_phase(k, tile(28), tile(32), value(0), small, i_row, f_fx, lambda h: y(0, h))
    rms_phase(k, [[(y(0, h), y(0, h), k.v("ml_g", h), big[:, 36 + h, :])] for h in range(4)], "rms_eps", P)
    gemm_phase(k, [F(key, j, big[:, b + j, :]) for key, b in (("fq", 28), ("fk", 32)) for j in range(4)])
    rms_phase(k, [[(big[:, b + h, :], big[:, b + h, :], k.v(g), None)] for b, g in ((28, "fxq_g"), (32, "fxk_g"))
                  for h in range(4)], "rms_eps", P)
    less_f = lambda h, n: [(k.c("negroot", 4)[:, h:h + 1].broadcast_to([4, P]), f_fx[0:4, 0:n])]
    attention_phase(k, softmax_units(tile(28), tile(32), value(4), P, None, lambda qb: k.c("causal")[:, T - P * (qb + 1):T],
                                     P ** -0.5, 0, lambda h: y(1, h), extra=less_f))
    padded = big[:, 28:33, :].rearrange("p a b -> p (a b)")[:, 0:4 * (T + 3)].rearrange("p (j t) -> p j t", j=4)
    gemm_phase(k, [F("rx", j, padded[:, j, 3:T + 3]) for j in range(4)]
               + [F("ry", j, big[:, 33 + j, :], func=ACT.Gelu_apprx_tanh) for j in range(4)])
    xc = lambda j: scr[:, j, :]
    conv_phase(k, padded, xc)
    gemm_phase(k, [feature_job(k, lambda c, j=j: xc(j), w[wk][j], scr[:, b + j, :], depth=1, split=False, bias=k.v(bk, j),
                               func=ACT.Sigmoid) for wk, bk, b in (("wa", "lru_ba", 4), ("wx", "lru_bx", 8))
                   for j in range(4)])
    lru_phase(k, xc, lambda j: scr[:, 4 + j, :], lambda j: scr[:, 8 + j, :], tile(33),
              lambda j: big[:, (37, 38, 39, 43)[j], :], tile(28), lambda j: y(2, j))
    gemm_phase(k, [feature_job(k, act, w[key][j], big[:, b + j, :], bias=b_ap(j), scale=sc)
                   for key, b, b_ap, sc in (("gq", 28, lambda j: k.v("b_gq", j), 1.0),
                                            ("gk", 30, lambda j: k.v("b_gk", j), 1.0)) for j in range(2)]
               + [F("gg", j, big[:, 32 + j, :], func=ACT.Silu) for j in range(4)]
               + [feature_job(k, lambda c: small, w["walpha"][j], big[:, 36 + j, :], depth=1, split=False,
                              bias=k.v("b_alpha", j)) for j in range(2)])
    states = big[:, 40:44, :].rearrange("p a b -> p (a b)").rearrange("p (q c n) -> p q c n", q=2, n=P)
    gla_phase(k, tile(28), tile(30), value(8), tile(36), tile(38), lambda p, c: states[:, p, c, :],
              lambda h: y(3, h))
    rms_phase(k, [[(y(3, h), y(3, h), k.v("gla_g", h), big[:, 32 + h, :])] for h in range(4)], "rms_eps", P)
    merged = lambda d: big[:, d, :]
    y_parts = lambda n, c: (k.parts[:, 28 + 4 * n + c, :], k.parts[:, 12 + 4 * n + c, :])
    split_phase(k, [(y(n, c), *y_parts(n, c)) for n in range(4) for c in range(4)])
    merge_phase(k, w["merge"], y_parts, merged)
    merged_parts = lambda d: (k.parts[:, 8 + d, :], k.parts[:, d, :])
    split_phase(k, [(merged(d), *merged_parts(d)) for d in range(KD)])
    project_phase(k, w["wo"], 1.0, merged_parts)
    norm = RmsNorm(k, into("norm2_g"), "rms_eps", D, parts=[act(c) for c in range(KD)])
    for up, down in w["ffn"]:
        relu2_phase(k, up, down, norm)
        norm = None


def layer(k, l, norm):
    big, w = k.big, WHERE["layers"][l]
    k.vec_cols, k.vec_from = VEC2, VEC1.n + l * VEC2.n
    x = lambda c: (k.in_hi[:, c, :], k.in_lo[:, c, :])
    if norm is None:
        split_phase(k, [(k.x[:, c, :], *x(c)) for c in range(KD)])
    glu_phase(k, *w["ffn1"], norm)
    tile = lambda i: big[:, i, :]
    v_tok = lambda tb: big[:, tb, :]
    v_mla = big[:, 4:6, :].rearrange("p a b -> p (a b)").rearrange("p (t n) -> p t n", n=256)
    token_phase(k, x, [(w["v"], v_tok, None)], LayerNorm(k, "ln1_g", "ln1_b"),
                loads=[(big[:, 33:42, :].rearrange("p a b -> p (a b)"), k.rope_dram)])
    jobs = []
    at = {"cq0": 6, "cq1": 7, "ckv": 8, "krope": 9, "kvcmp": 10, "iq0": 11, "iq1": 12, "ik": 13, "nq0": 14,
          "nq1": 15, "ks": 16, "kw": 17, "dq0": 18, "dq1": 19, "dk": 20, "sq0": 21, "sq1": 22, "sk0": 23, "sk1": 24}
    rope = {"krope": "mq", "kvcmp": "cmp", "iq0": "i4", "iq1": "i4", "ik": "i4", "nq0": "h2", "nq1": "h2",
            "ks": "h2", "kw": "h2", "dq0": "h2", "dq1": "h2", "dk": "h2"}
    jobs += [feature_job(k, x, w[key], tile(i), rope=rope.get(key)) for key, i in at.items()]
    gemm_phase(k, jobs)
    rms_phase(k, [[(tile(6 + j), tile(6 + j), k.v("q_g", j), None) for j in range(2)]], "rms_eps", 256)
    rms_phase(k, [[(tile(8), tile(8), k.v("kv_g"), None)]], "rms_eps", P)
    jobs = [feature_job(k, lambda c: tile(6 + c), w["uq"][h], tile(25 + h), depth=2, split=False, rope="mq") for h in range(HEADS)]
    for h in range(HEADS):
        jobs.append(feature_job(k, lambda c: tile(8), w["uk"][h], tile(29 + h), depth=1, split=False,
                                also=(k.c("ident"), tile(9))))
    jobs += [token_job(k, lambda c: tile(8), w["uv"][q], v_mla[:, :, P * q:P * q + P]) for q in range(2)]
    gemm_phase(k, jobs)
    blk = big[:, 37:39, :].rearrange("p a b -> p (a b)")[:, 0:CMP_LEN * NCMP].rearrange("p (l n) -> p l n", n=NCMP)
    kc, vc, gates = tile(36)[:, 0:NCMP], tile(36)[0:NCMP, 64:128], tile(36)[:, 256:256 + 48].rearrange(
        "p (t g) -> p t g", g=12)
    compress_phase(k, tile(10), blk, w["c1"], w["c2"], tile(36)[:, 128:192], kc, vc,
                   big[:, 0:QB, GT0:GT0 + 12], gates)
    select = lambda qb: tile(32 + qb)
    index_phase(k, lambda j: tile(11 + j), tile(13), lambda qb, h: v_tok(qb)[:, IW0 + h:IW0 + h + 1], select)
    causal = lambda qb: k.c("causal")[:, T - P * (qb + 1):T]
    half = lambda t, h: t[64 * (h % 2):64 * (h % 2) + 64]
    ys = lambda n: (lambda h: k.act[:, 2 * n + h // 2, :])
    units = softmax_units(lambda h: tile(25 + h), lambda h: tile(29 + h),
                          lambda kb, h: v_mla[:, kb, 64 * h:64 * h + 64], 64, None, causal, 96 ** -0.5, 0, ys(0))
    attention_phase(k, units)
    units = []
    for h in range(HEADS):
        lo = 64 * (h % 2)
        q = half(tile(14 + h // 2), h)
        for qb in range(QB):
            wd = P * (qb + 1)
            more = dict(group=QB * h + qb, rows=(lo, lo + 64), scale=64 ** -0.5,
                        out=ys(1)(h)[lo:lo + 64, P * qb:P * qb + P])
            gate = lambda b: gates[:, qb, 4 * b + h:4 * b + h + 1]
            qs = q[:, P * qb:P * qb + P]
            at_cmp = slice(CONST.at["cmp_neg"][0] + NCMP * qb, CONST.at["cmp_neg"][0] + NCMP * (qb + 1))
            at_keep = slice(CONST.at["cmp_keep"][0] + NCMP * qb, CONST.at["cmp_keep"][0] + NCMP * (qb + 1))
            units.append(Unit([(qs, half(kc, h))], NCMP, [vc], first=True, last=False, gate=gate(0),
                              mask=k.const[:, at_cmp], keep=k.const[:, at_keep], **more))
            for b, (kt, col) in enumerate(((16, VS0), (17, VW0))):
                units.append(Unit([(qs, half(tile(kt), h)[:, 0:wd])], wd,
                                  [v_tok(kb)[:, col:col + 64] for kb in range(qb + 1)], first=False, last=(b == 1),
                                  gate=gate(b + 1), mask=causal(qb), **more))
    attention_phase(k, units)
    units = softmax_units(lambda h: half(tile(21 + h // 2), h), lambda h: half(tile(23 + h // 2), h),
                          lambda kb, h: v_tok(kb)[:, VB0 + 64 * h:VB0 + 64 * h + 64], 64, None,
                          lambda qb: k.c("strict")[:, T - P * (qb + 1):T], 64 ** -0.5, 0, ys(3))
    stick_phase(k, units, lambda i: tile((14, 15, 16, 17, 36, 37, 38, 39, 40, 41, 42, 43)[i % 12]),
                lambda i: tile(25 + i % 4), select)
    units = softmax_units(lambda h: half(tile(18 + h // 2), h), lambda h: half(tile(20), h),
                          lambda kb, h: v_tok(kb)[:, VD0:VD0 + 64], 64, None,
                          lambda qb: causal(0) if qb == 0 else select(qb)[:, 0:P * (qb + 1)], 64 ** -0.5, 0, ys(2))
    attention_phase(k, units)
    norm = RmsNorm(k, [[(k.act[:, 2 * g + j, :], k.act[:, 2 * g + j, :], k.v("group_g", 2 * g + j), None)
                        for j in range(2)] for g in range(4)], "rms_eps", 256, parts=[x(c) for c in range(KD)])
    project_phase(k, w["wout"], ALPHA, x, norm)
    glu_phase(k, *w["ffn2"], LayerNorm(k, "ln2_g", "ln2_b"))


def build(nc, x, weights, const, rope, vec1, brow, vec2, out):
    with ExitStack() as ctx:
        k = Core(nc, ctx, weights)
        k.rope_dram = rope
        copy_in_phase(k, [(k.x[:, :, :], x.rearrange("c p t -> p c t")), (k.const[:, :], const),
                          (k.vec[:, 0:VEC1.n], vec1),
                          *[(k.vec[:, VEC1.n + l * VEC2.n:VEC1.n + (l + 1) * VEC2.n], vec2[l]) for l in range(LAYERS)],
                          (k.scr[:, 4:7, :], brow.rearrange("a (b c) -> a b c", c=T).broadcast_to([P, 3, T]))])

        block_one(k)
        norm = None
        for l in range(LAYERS):
            layer(k, l, norm)
            norm = LayerNorm(k, "ln3_g", "ln3_b")
        output_phase(k, "ln3_g", "ln3_b", out)


def pack_weights(inputs):
    packed = np.zeros((len(STREAM.tiles), P, P), np.float32)
    for n, pieces in enumerate(STREAM.tiles):
        for name, lay, row, col, r0, c0, h, w in pieces or ():
            a = inputs[name][lay]
            if isinstance(row, tuple):
                a, row = a[row[0]], row[1]
            packed[n, r0:r0 + h, c0:c0 + w] = a[row:row + h, col:col + w]
    packed = packed.reshape(NSLABS, SLAB, P, P).transpose(0, 2, 1, 3)
    return np.ascontiguousarray(packed).reshape(NSLABS, P, SLAB * P)


def by_column(v):
    return np.asarray(v).reshape(-1, P).T


def pack_vec1(i):
    out = np.zeros((P, VEC1.n), np.float32)

    def put(name, a):
        at, n = VEC1.at[name]
        out[: a.shape[0], at:at + a.shape[1]] = a

    b = i["b_in"][0]
    put("norm1_g", by_column(i["norm1_g"][0]))
    put("norm2_g", by_column(i["norm2_g"][0]))
    for name, at, n in (("b_mq", MQ, 512), ("b_mk", MK, 512), ("b_mo", MO, 512), ("b_fq", FQ, 512),
                        ("b_fk", FK, 512), ("b_rx", RX, 512), ("b_ry", RY, 512), ("b_gq", GQ, 256),
                        ("b_gk", GK, 256), ("b_gg", GG, 512), ("b_gates", GATES, 4096)):
        put(name, by_column(b[at:at + n]))
    small = VEC1.at["b_small"][0]
    out[0:4, small] = b[MF:MF + 4]
    out[32:36, small] = b[FFG:FFG + 4]
    out[96:112, small] = b[GA:GA + 16]
    out[0:4, VEC1.at["b_mi"][0]] = b[MI:MI + 4]
    put("ml_g", by_column(i["ml_norm_g"][0]))
    put("gla_g", by_column(i["gla_norm_g"][0]))
    put("fxq_g", by_column(i["fx_qnorm_g"][0]))
    put("fxk_g", by_column(i["fx_knorm_g"][0]))
    put("conv_w", np.concatenate([by_column(i["lru_conv_w"][0][t]) for t in range(4)], 1))
    put("conv_b", by_column(i["lru_conv_b"][0]))
    put("lru_ba", by_column(i["lru_ba"][0]))
    put("lru_bx", by_column(i["lru_bx"][0]))
    put("lam", by_column(i["lru_lambda"][0]))
    put("b_alpha", by_column(i["gla_b_alpha"][0]))
    return out


def pack_vec2(i):
    out = np.zeros((LAYERS, P, VEC2.n), np.float32)
    for l in range(LAYERS):
        for name, key in (("ln1_g", "ln1_g_2"), ("ln1_b", "ln1_b_2"), ("q_g", "mla_q_norm_2"),
                          ("kv_g", "mla_kv_norm_2"), ("group_g", "group_norm_g_2"), ("ln2_g", "ln2_g_2"),
                          ("ln2_b", "ln2_b_2"), ("ln3_g", "ln3_g_2"), ("ln3_b", "ln3_b_2")):
            at, n = VEC2.at[name]
            out[l, :, at:at + n] = by_column(i[key][l])
        at, n = VEC2.at["pos"]
        out[l, 0:64, at:at + n] = i["nsa_cmp_pos_2"][l].T
        out[l, 64:128, at:at + n] = i["nsa_cmp_pos_2"][l].T
    return out


def arrays_of(inputs):
    i = {name: np.asarray(a) for name, a in inputs.items()}
    b = i["b_in"][0]
    const, rope = constants()
    return {
        "xT": np.ascontiguousarray(i["x"][0].T).reshape(KD, P, T),
        "weights": pack_weights(i),
        "consts": const,
        "rope": rope,
        "vec1": pack_vec1(i),
        "brow": np.concatenate([b[c:c + 512] for c in (MV, FV, GV)])[None, :],
        "vec2": pack_vec2(i),
    }


def kernel(**inputs):
    import concourse.bacc as bacc
    from concourse.bass_utils import run_bass_kernel_spmd

    nc = bacc.Bacc("TRN2", target_bir_lowering=False, num_devices=1)
    arrays = arrays_of(inputs)
    aps = [nc.dram_tensor(name, a.shape, F32, kind="ExternalInput").ap() for name, a in arrays.items()]
    out = nc.dram_tensor("outT", (KD, P, T), F32, kind="ExternalOutput").ap()
    build(nc, *aps, out)
    r = run_bass_kernel_spmd(nc, [arrays], core_ids=[0])
    got = np.asarray(r.results[0]["outT"]).reshape(D, T)
    return np.ascontiguousarray(got.T)[None]
```

```python
from contextlib import ExitStack

import numpy as np

import concourse.bass as bass
from concourse import mybir

F32 = mybir.dt.float32
F32R = mybir.dt.float32r
ALU = mybir.AluOpType
ACT = mybir.ActivationFunctionType
AX = mybir.AxisListType.X

P = 128
T = 512
QB = T // P
D = 1024
KD = D // P
NEG = -1e30
TAKEN = -3e38

BW = 512
FF1 = 4096
HEADS = 4
GLA_TAU = 16.0
LRU_C = 8.0
CHUNK = 64
NCHUNK = T // CHUNK
RMS_EPS, LN_EPS = 1e-6, 1e-5
W1 = (512, 512, 512, 512, 4, 4, 512, 512, 512, 4, 512, 512, 256, 256, 512, 512, 16, 4096)
O1 = np.concatenate([[0], np.cumsum(W1)])
(MQ, MK, MV, MO, MI, MF, FQ, FK, FV, FFG, RX, RY, GQ, GK, GV, GG, GA, GATES) = [int(o) for o in O1[:-1]]

LAYERS = 2
FF2 = 2816
KF2 = FF2 // P
ALPHA = (2.0 * LAYERS) ** 0.25
W2 = (256, 128, 32, 256, 64, 64, 64, 64, 64, 64, 12, 256, 64, 64, 256, 32, 8, 256, 256, 256)
O2 = np.concatenate([[0], np.cumsum(W2)])
(CQ, CKV, KROPE, NQ, NKC, NVC, NKS, NVS, NKW, NVW, NGATE, DQ, DK, DV, IQ, IK, IW, SQ, SK, SV) = [
    int(o) for o in O2[:-1]]
NCMP, CMP_LEN, CMP_STRIDE = 31, 32, 16
TOPK = T // 4
IDX_HEADS = 8
TOP_STEPS = TOPK // 8
TOP_CUTS = (14, 34)
VS0, VW0, VD0, VB0, GT0, IW0 = 0, 64, 128, 192, 448, 460

SLAB = 8
RAW = 3
SPLIT = 3


class Stream:

    def __init__(self):
        self.tiles = []
        self.whole = set()

    def align(self, n):
        while len(self.tiles) % n:
            self.tiles.append(None)

    def add(self, pieces):
        at = len(self.tiles)
        self.tiles.extend(pieces)
        return at

    def columns(self, name, layer, depth, cols, row=0):
        at = len(self.tiles)
        for k in range(depth):
            self.tiles.append([(name, layer, row + k * P, m, 0, c, P, n) for c, m, n in cols])
        return at

    def wide(self, name, layer, depth, cols):
        at = len(self.tiles)
        assert at % SLAB == 0
        for k in range(depth):
            for q in range(T // P):
                lo, hi = q * P, (q + 1) * P
                self.tiles.append([(name, layer, k * P, m + max(c, lo) - c, 0, max(c, lo) - lo, P,
                                    min(c + n, hi) - max(c, lo)) for c, m, n in cols if max(c, lo) < min(c + n, hi)])
        return at

    def plain(self, at, n):
        assert at % SLAB == 0 and n % SLAB == 0
        self.whole.update(range(at // SLAB, (at + n) // SLAB))


def plan():
    s = Stream()
    w = {}
    one = lambda name, layer, depth, col, n: [
        s.columns(name, layer, depth, [(0, col + P * j, P)]) for j in range(n)]
    w["mv"], w["fv"], w["gv"] = [s.wide("w_in", 0, KD, [(0, c, BW)]) for c in (MV, FV, GV)]
    w["small"] = s.columns("w_in", 0, KD, [(0, MF, 4), (32, FFG, 4), (96, GA, 16)])
    w["mi"] = s.columns("w_in", 0, KD, [(0, MI, 4)])
    w["mq"] = one("w_in", 0, KD, MQ, 4)
    w["mk"] = one("w_in", 0, KD, MK, 4)
    w["mo"] = one("w_in", 0, KD, MO, 4)
    w["fq"] = one("w_in", 0, KD, FQ, 4)
    w["fk"] = one("w_in", 0, KD, FK, 4)
    w["rx"] = one("w_in", 0, KD, RX, 4)
    w["ry"] = one("w_in", 0, KD, RY, 4)
    for key, name in (("wa", "lru_wa"), ("wx", "lru_wx")):
        w[key] = [s.add([[(name, 0, (2 * j, 0), 0, 0, 0, 64, 64), (name, 0, (2 * j + 1, 0), 0, 64, 64, 64, 64)]])
                  for j in range(4)]
    s.plain(w["wa"][0], 8)
    w["walpha"] = [s.add([[("gla_w_alpha", 0, 0, P * j, 96, 0, 16, P)]]) for j in range(2)]
    s.align(SLAB)
    s.plain(w["walpha"][0], 8)
    w["gq"] = one("w_in", 0, KD, GQ, 2)
    w["gk"] = one("w_in", 0, KD, GK, 2)
    w["gg"] = one("w_in", 0, KD, GG, 4)
    w["merge"] = []
    for d in range(KD):
        for n in range(4):
            g = s.columns("w_in", 0, KD, [(0, GATES + D * n + P * d, P)])
            b = len(s.tiles)
            for k in range(4):
                s.tiles.append([("w_branch", 0, (n, k * P), P * d, 0, 0, P, P)])
            w["merge"].append((g, b))
    w["wo"] = one("w_o", 0, KD, 0, KD)
    w["ffn"] = []
    for half in range(2):
        at = half * FF1 // 2
        up = one("w_up", 0, KD, at, FF1 // 2 // P)
        w["ffn"].append((up, [s.columns("w_down", 0, FF1 // 2 // P, [(0, P * j, P)], row=at) for j in range(KD)]))
    s.align(SLAB)
    w["layers"] = []
    for l in range(LAYERS):
        v = {}

        def ffn(n):
            up = []
            for f in range(KF2):
                up.append(tuple(s.columns(f"ffn{n}_{m}_2", l, KD, [(0, P * f, P)]) for m in ("w1", "w3")))
            down = [s.columns(f"ffn{n}_w2_2", l, KF2, [(0, P * j, P)]) for j in range(KD)]
            return up, down

        v["ffn1"] = ffn(1)
        spans = [(VS0, NVS, 64), (VW0, NVW, 64), (VD0, DV, 64), (VB0, SV, 256), (GT0, NGATE, 12), (IW0, IW, 8)]
        v["v"] = s.wide("w_in_2", l, KD, spans)
        two = lambda c: [(0, c, 64), (64, c, 64)]
        for key, cols in (
            ("cq0", [(0, CQ, P)]), ("cq1", [(0, CQ + P, P)]), ("ckv", [(0, CKV, P)]),
            ("krope", [(64, KROPE, 32)]), ("kvcmp", [(0, NKC, 64), (64, NVC, 64)]),
            ("iq0", [(0, IQ, P)]), ("iq1", [(0, IQ + P, P)]), ("ik", [(32 * i, IK, 32) for i in range(4)]),
            ("nq0", [(0, NQ, P)]), ("nq1", [(0, NQ + P, P)]), ("ks", two(NKS)), ("kw", two(NKW)),
            ("dq0", [(0, DQ, P)]), ("dq1", [(0, DQ + P, P)]), ("dk", two(DK)),
            ("sq0", [(0, SQ, P)]), ("sq1", [(0, SQ + P, P)]), ("sk0", [(0, SK, P)]), ("sk1", [(0, SK + P, P)]),
        ):
            v[key] = s.columns("w_in_2", l, KD, cols)
        v["uq"] = [s.columns("mla_w_uq_2", l, 2, [(0, 96 * h, 96)]) for h in range(HEADS)]
        v["uk"] = [s.columns("mla_w_ukv_2", l, 1, [(0, 128 * h, 64)]) for h in range(HEADS)]
        v["uv"] = [s.add([[("mla_w_ukv_2", l, 0, 128 * (2 * i + j) + 64, 0, 64 * j, P, 64) for j in range(2)]])
                   for i in range(2)]
        s.align(SLAB)
        v["c1"] = s.add([[(f"nsa_cmp_w{m}1_2", l, 64 * (2 * i + j), 0, r, 64 * j, 64, 64)
                          for m, r in (("k", 0), ("v", 64)) for j in range(2)] for i in range(16)])
        v["c2"] = s.add([[("nsa_cmp_wk2_2", l, 0, 0, 0, 0, 64, 64), ("nsa_cmp_wk2_2", l, 0, 0, 0, 64, 64, 64),
                          ("nsa_cmp_wv2_2", l, 0, 0, 64, 0, 64, 64)]])
        s.align(SLAB)
        s.plain(v["uq"][0], len(s.tiles) - v["uq"][0])
        v["wout"] = [s.columns("w_out_2", l, KD, [(0, P * j, P)]) for j in range(KD)]
        v["ffn2"] = ffn(2)
        s.align(SLAB)
        w["layers"].append(v)
    s.align(SLAB)
    return s, w


STREAM, WHERE = plan()
NSLABS = len(STREAM.tiles) // SLAB
SPLITS = [n for n in range(NSLABS) if n not in STREAM.whole]
SPLIT_AT = {n: m for m, n in enumerate(SPLITS)}


class Columns:

    def __init__(self):
        self.at, self.n = {}, 0

    def add(self, name, n):
        self.at[name] = (self.n, n)
        self.n += n


CONST = Columns()
for _n, _w in (("ident", P), ("ones", P), ("negident", 4), ("negroot", 4), ("causal", T), ("strict", T), ("tri", P),
               ("chunk_tri", P), ("cmp_neg", QB * NCMP), ("cmp_keep", QB * NCMP), ("goes_on", T),
               ("rms_eps", 1), ("ln_eps", 1), ("one", 1)):
    CONST.add(_n, _w)

ROPE = Columns()
for _n in ("h2", "i4", "mq", "cmp"):
    ROPE.add("cos_" + _n, T)
    ROPE.add("sin_" + _n, T)
for _n in ("h2", "i4", "mq", "cmp"):
    ROPE.add("rot_" + _n, P)

VEC1 = Columns()
for _n, _w in (("norm1_g", 8), ("norm2_g", 8), ("b_mq", 4), ("b_mk", 4), ("b_mo", 4), ("b_fq", 4), ("b_fk", 4),
               ("b_rx", 4), ("b_ry", 4), ("b_gq", 2), ("b_gk", 2), ("b_gg", 4), ("b_small", 1), ("b_mi", 1),
               ("b_gates", 32), ("ml_g", 4), ("gla_g", 4), ("fxq_g", 1), ("fxk_g", 1), ("conv_w", 16),
               ("conv_b", 4), ("lru_ba", 4), ("lru_bx", 4), ("lam", 4), ("b_alpha", 2), ("decay", 4), ("tmp", 4)):
    VEC1.add(_n, _w)
VEC2 = Columns()
for _n, _w in (("ln1_g", 8), ("ln1_b", 8), ("q_g", 2), ("kv_g", 1), ("group_g", 8), ("ln2_g", 8), ("ln2_b", 8),
               ("ln3_g", 8), ("ln3_b", 8), ("pos", CMP_LEN)):
    VEC2.add(_n, _w)
NVEC = VEC1.n + LAYERS * VEC2.n
BROW = 3 * 512


def constants():
    c = np.zeros((P, CONST.n), np.float32)
    rope = np.zeros((P, ROPE.n), np.float32)

    def put(name, a):
        where, to = (ROPE, rope) if name in ROPE.at else (CONST, c)
        at, n = where.at[name]
        to[: a.shape[0], at:at + n] = a

    put("ident", np.eye(P))
    put("ones", np.ones((P, P)))
    put("negident", -np.eye(4))
    put("negroot", -np.eye(4) * np.sqrt(128.0))

    def rotation(spans):
        r = np.zeros((P, P))
        for a, n in spans:
            for i in range(n // 2):
                r[a + n // 2 + i, a + i] = -1
                r[a + i, a + n // 2 + i] = 1
        return r

    def tables(spans):
        cos, sin = np.ones((P, T)), np.zeros((P, T))
        for a, n in spans:
            inv = np.float32(10000.0) ** (-np.arange(0, n, 2, dtype=np.float32) / np.float32(n))
            ang = (np.arange(T, dtype=np.float32)[None, :] * inv.astype(np.float32)[:, None]).astype(np.float32)
            for half in range(2):
                cos[a + half * n // 2:a + (half + 1) * n // 2] = np.cos(ang.astype(np.float64))
                sin[a + half * n // 2:a + (half + 1) * n // 2] = np.sin(ang.astype(np.float64))
        return cos, sin

    for kind, spans in (("h2", [(0, 64), (64, 64)]), ("i4", [(32 * i, 32) for i in range(4)]),
                        ("mq", [(64, 32)]), ("cmp", [(0, 64)])):
        put("rot_" + kind, rotation(spans))
        cos, sin = tables(spans)
        put("cos_" + kind, cos)
        put("sin_" + kind, sin)
    i = np.arange(P)
    before = np.zeros((P, T - P))
    put("causal", np.concatenate([before, np.where(i[None, :] <= i[:, None], 0, NEG)], 1))
    put("strict", np.concatenate([before, np.where(i[None, :] < i[:, None], 0, NEG)], 1))
    put("tri", (i[:, None] <= i[None, :]).astype(float))
    put("chunk_tri", ((i[:, None] <= i[None, :]) & (i[:, None] // CHUNK == i[None, :] // CHUNK)).astype(float))
    ends = np.arange(NCMP) * CMP_STRIDE + CMP_LEN - 1
    seen = ends[None, None, :] <= (np.arange(QB)[None, :, None] * P + i[:, None, None])
    put("cmp_keep", seen.astype(float).reshape(P, -1))
    put("cmp_neg", np.where(seen, 0, NEG).reshape(P, -1))
    put("goes_on", np.tile((np.arange(T) % CHUNK != 0).astype(float), (P, 1)))
    put("rms_eps", np.full((P, 1), RMS_EPS))
    put("ln_eps", np.full((P, 1), LN_EPS))
    put("one", np.ones((P, 1)))
    return c, rope


class Signal:

    def __init__(self, sem):
        self, self.base = sem, 0


def wait(eng, signal, count):
    assert count >= 1
    eng.wait_ge(signal, signal.base + count)


class Core:

    def __init__(self, nc, ctx, weights):
        self.nc, self.ctx, self.weights = nc, ctx, weights
        at = [0]
        total = 4 * (T * (KD + 2 * KD + 44 + 12) + SLAB * P * (RAW + 2 * SPLIT)) // 4
        first = nc.sbuf_base + (-nc.sbuf_base) % 64
        ctx.enter_context(nc.sbuf_tensor("arena", [P, total + 16], F32))

        def place(name, shape, dt=F32, over=None):
            size = int(np.prod(shape[1:]))
            start = at[0] if over is None else over
            if over is None:
                at[0] += size
            assert at[0] <= total
            return nc.alloc_sbuf_tensor_at(name, shape, dt, offset=first + 4 * start)

        self.x = place("x_resid", [P, KD, T])
        self.in_hi = place("in_hi", [P, KD, T], F32R)
        self.act = place("act", [P, KD, T])
        self.in_lo = place("in_lo", [P, KD, T], F32R, over=at[0] - KD * T)
        self.big = place("big", [P, 44, T])
        self.parts = place("parts", [P, 44, T], F32R, over=at[0] - 44 * T)
        self.scr = place("scratch", [P, 12, T])
        self.total = self.scr[:, 9, :]
        self.raw = place("raw_slabs", [P, RAW, SLAB * P])
        self.w_hi = place("w_hi", [P, SPLIT, SLAB * P], F32R)
        self.w_lo = place("w_lo", [P, SPLIT, SLAB * P], F32R)
        sb = lambda name, shape: ctx.enter_context(nc.sbuf_tensor(name, shape, F32))
        self.const = sb("const_cols", [P, CONST.n])
        self.vec = sb("vector_cols", [P, NVEC])
        self.stat = sb("stats", [P, 2, 64])
        self.ps = ctx.enter_context(nc.psum_tensor("ps", [P, 8, T], F32))
        self.flags = {}
        self.base = {}
        self.slab_loaded = [ctx.enter_context(nc.semaphore(f"slab_loaded{i}")) for i in range(RAW)]
        self.hi_made, self.lo_made = self.flag("w_hi_made"), self.flag("w_lo_made")
        self.sums_done = self.flag("sums_done")
        self.loaded = 0
        self.high = self.low = 0
        self.last_sum = {}
        self.sums = 0
        self.seen_slab = -1
        self.vec_cols, self.vec_from = VEC1, 0

    def flag(self, name):
        if name not in self.flags:
            self.flags[name] = self.ctx.enter_context(self.nc.semaphore(name))
            self.base[name] = 0
        return self.flags[name]

    def at(self, flag, count):
        assert count >= 1
        return next(self.base[name] for name, f in self.flags.items() if f is flag) + count

    def passed(self, **counts):
        for name, n in counts.items():
            if n:
                self.base[name] += n

    def c(self, name, rows=P):
        at, n = CONST.at[name]
        return self.const[0:rows, at:at + n]

    def rope(self, name):
        at, n = ROPE.at[name]
        return self.big[:, 33 + at // T, at % T:at % T + n]

    def v(self, name, j=0, n=1):
        at, _ = self.vec_cols.at[name]
        at += self.vec_from
        return self.vec[:, at + j:at + j + n]

    def raw_tile(self, i):
        slab, c = divmod(i, SLAB)
        return self.raw[:, slab % RAW, c * P:(c + 1) * P]

    def w_parts(self, i):
        slab, c = divmod(i, SLAB)
        at = SPLIT_AT[slab] % SPLIT
        return self.w_hi[:, at, c * P:(c + 1) * P], self.w_lo[:, at, c * P:(c + 1) * P]

    def wide_parts(self, i):
        slab, c = divmod(i, SLAB)
        at = SPLIT_AT[slab] % SPLIT
        return self.w_hi[:, at, c * P:(c + 4) * P], self.w_lo[:, at, c * P:(c + 4) * P]

    def products(self, i, x):
        (wh, wl), (xh, xl) = self.w_parts(i), x
        return [(wh, xh), (wh, xl), (wl, xh)]

    def use(self, jobs, by_slab=True):
        ends = []
        for tiles in jobs:
            tiles = list(tiles)
            for n, i in enumerate(tiles):
                if n == len(tiles) - 1 or (by_slab and i % SLAB == SLAB - 1):
                    self.sums += 1
                self.last_sum[i // SLAB] = self.sums + (0 if n == len(tiles) - 1 or i % SLAB == SLAB - 1 else 1)
            for i in tiles if not by_slab else ():
                self.last_sum[i // SLAB] = self.sums
            ends.append(self.sums)
        return ends

    def load_slabs(self, sp):
        last = max(self.last_sum) if self.last_sum else -1
        while self.loaded < min(NSLABS, last + 1 + RAW):
            n = self.loaded
            if n >= RAW and n - RAW in SPLIT_AT:
                sp.wait_ge(self.lo_made, SPLIT_AT[n - RAW] + 1)
            elif n >= RAW:
                sp.wait_ge(self.sums_done, self.last_sum[n - RAW])
            sp.dma_start(self.raw[:, n % RAW, :], self.weights[n]).then_inc(self.slab_loaded[n % RAW], 16)
            self.loaded += 1

    def high_slabs(self, act, i):
        last = max(self.last_sum)
        while self.high < len(SPLITS) and SPLITS[self.high] <= min(i // SLAB + SPLIT - 1, self.loaded - 1):
            m = self.high
            n = SPLITS[m]
            if m >= SPLIT and SPLITS[m - SPLIT] > last:
                break
            act.wait_ge(self.slab_loaded[n % RAW], 16 * (n // RAW + 1))
            if m >= SPLIT:
                act.wait_ge(self.sums_done, self.last_sum[SPLITS[m - SPLIT]])
            self.nc.scalar.activation(self.w_hi[:, m % SPLIT, :], self.raw[:, n % RAW, :], ACT.Copy)\
                .then_inc(self.hi_made, 1)
            self.high += 1

    def low_slabs(self, pool):
        while self.low < self.high:
            m = self.low
            n = SPLITS[m]
            pool.wait_ge(self.hi_made, m + 1)
            self.nc.gpsimd.tensor_tensor(self.w_lo[:, m % SPLIT, :], self.raw[:, n % RAW, :],
                                         self.w_hi[:, m % SPLIT, :].bitcast(F32), ALU.subtract)\
                .then_inc(self.lo_made, 1)
            self.low += 1

    def need(self, pe, i):
        slab = i // SLAB
        if self.seen_slab < slab:
            if slab in SPLIT_AT:
                pe.wait_ge(self.lo_made, SPLIT_AT[slab] + 1)
            else:
                pe.wait_ge(self.slab_loaded[slab % RAW], 16 * (slab // RAW + 1))
            self.seen_slab = slab


def add_up(k, pe, out, tiles, wait_tile=None):
    for c, (i, x) in enumerate(tiles):
        k.need(pe, i)
        if wait_tile:
            wait_tile(pe, c)
        last = c == len(tiles) - 1
        for m, (lhsT, rhs) in enumerate(k.products(i, x)):
            mm = k.nc.tensor.matmul(out, lhsT, rhs, start=(c == 0 and m == 0), stop=(last and m == 2))
        if last or i % SLAB == SLAB - 1:
            mm.then_inc(k.sums_done, 1)


def tiles_of(job):
    return [i for _, i, *_ in job["sum"] if i is not None]


def gemm_phase(k, jobs, norm=None, scalar=None, vector=None):
    nc = k.nc
    ends = k.use([tiles_of(j) for j in jobs], by_slab=False)
    taken, rotated, joined, part = [k.flag(n) for n in ("taken", "rotated", "joined", "rope_part")]
    ropes = [j for j, job in enumerate(jobs) if job.get("rope")]
    banks = 4 if ropes or norm else 8

    with nc.Block() as block:
        @block.sync
        def _(sp):
            k.load_slabs(sp)

        @block.tensor
        def _(pe):
            if norm:
                norm.tensor(pe)

            def rotate(r):
                job = jobs[ropes[r]]
                pe.wait_ge(taken, k.at(taken, ropes[r] + 1))
                if r >= 2:
                    pe.wait_ge(joined, k.at(joined, r - 1))
                nc.tensor.matmul(k.ps[:, 4 + r % 2, :], k.rope("rot_" + job["rope"]), job["out"],
                                 start=True, stop=True).then_inc(rotated, 1)

            for j, job in enumerate(jobs):
                if j >= banks:
                    pe.wait_ge(taken, k.at(taken, j - banks + 1))
                for part, i, cols, start, stop in job["sum"]:
                    if i is not None:
                        k.need(pe, i)
                    for m, (lhsT, rhs) in enumerate(part):
                        mm = nc.tensor.matmul(k.ps[:, j % banks, cols], lhsT, rhs, start=(start and m == 0),
                                              stop=(stop and m == len(part) - 1))
                mm.then_inc(k.sums_done, 1)
                if j - 1 in ropes:
                    rotate(ropes.index(j - 1))
            if len(jobs) - 1 in ropes:
                rotate(len(ropes) - 1)

        @block.scalar
        def _(act):
            if norm:
                norm.scalar(act)
            for j, job in enumerate(jobs):
                if scalar and j in scalar:
                    scalar[j](act)
                k.high_slabs(act, max(tiles_of(job)))
                act.wait_ge(k.sums_done, ends[j])
                nc.scalar.activation(job["out"], job.get("view", lambda bank: bank)(k.ps[:, j % banks, :]),
                                     job.get("func", ACT.Identity), bias=job.get("bias", 0.0),
                                     scale=job.get("scale", 1.0)).then_inc(taken, 1)

        if ropes or norm or vector:
            @block.vector
            def _(dve):
                if norm:
                    norm.vector(dve)
                if vector:
                    vector(dve)
                for r, j in enumerate(ropes):
                    job = jobs[j]
                    turned = k.scr[:, 10 + r % 2, :]
                    dve.wait_ge(rotated, k.at(rotated, r + 1))
                    nc.vector.tensor_tensor(turned, k.ps[:, 4 + r % 2, :], k.rope("sin_" + job["rope"]),
                                            ALU.mult).then_inc(part, 1)
                    nc.vector.tensor_tensor(job["out"], job["out"], k.rope("cos_" + job["rope"]),
                                            ALU.mult).then_inc(part, 1)
                    dve.wait_ge(part, k.at(part, 2 * r + 2))
                    nc.vector.tensor_tensor(job["out"], job["out"], turned, ALU.add).then_inc(joined, 1)

        @block.gpsimd
        def _(pool):
            k.low_slabs(pool)
    if norm:
        norm.passed()
    k.passed(taken=len(jobs), rotated=len(ropes), joined=len(ropes), rope_part=2 * len(ropes))


def token_phase(k, x, jobs, norm, loads=()):
    nc = k.nc
    depth = KD
    ends = k.use([range(at, at + 4 * depth) for at, _, _ in jobs])
    taken, here = k.flag("taken"), k.flag("inputs_here")
    with nc.Block() as block:
        @block.sync
        def _(sp):
            for dst, src in loads:
                sp.dma_start(dst, src).then_inc(here, 16)
            k.load_slabs(sp)
            if loads:
                sp.wait_ge(here, k.at(here, 16 * len(loads)))

        @block.tensor
        def _(pe):
            norm.tensor(pe)
            for j, (at, _, _) in enumerate(jobs):
                if j >= 2:
                    pe.wait_ge(taken, k.at(taken, QB * (j - 1)))
                for c in range(depth):
                    i = at + 4 * c
                    k.need(pe, i)
                    if j == 0:
                        norm.wait_tile(pe, c)
                    xh, xl = x(c)
                    wh, wl = k.wide_parts(i)
                    for tb in range(QB):
                        block = slice(P * tb, P * tb + P)
                        for m, (lhsT, rhs) in enumerate(((xh, wh), (xh, wl), (xl, wh))):
                            mm = nc.tensor.matmul(k.ps[:, QB * (j % 2) + tb, :], lhsT[:, block], rhs,
                                                  start=(c == 0 and m == 0), stop=(c == depth - 1 and m == 2))
                    if (i + 3) % SLAB == SLAB - 1:
                        mm.then_inc(k.sums_done, 1)

        @block.scalar
        def _(act):
            k.high_slabs(act, jobs[0][0])
            norm.scalar(act)
            for j, (at, _, _) in enumerate(jobs):
                k.high_slabs(act, at + 4 * depth - 1)

        @block.vector
        def _(dve):
            norm.vector(dve)
            for j, (_, out, bias) in enumerate(jobs):
                dve.wait_ge(k.sums_done, ends[j])
                for tb in range(QB):
                    bank = k.ps[:, QB * (j % 2) + tb, :]
                    if bias is None:
                        nc.vector.tensor_copy(out(tb), bank).then_inc(taken, 1)
                    else:
                        nc.vector.tensor_tensor(out(tb), bank, bias, ALU.add).then_inc(taken, 1)

        @block.gpsimd
        def _(pool):
            k.low_slabs(pool)
    norm.passed()
    k.passed(taken=QB * len(jobs), inputs_here=16 * len(loads))


class RmsNorm:

    BATCH = 4

    def __init__(self, k, groups, eps, width, parts=(), bank=0):
        self.k, self.groups, self.eps, self.parts, self.bank = k, groups, eps, parts, bank
        self.widths = width if isinstance(width, tuple) else (width,) * len(groups)
        self.flat = [(g, t) for g, group in enumerate(groups) for t in group]
        self.first = [sum(len(x) for x in groups[:g]) for g in range(len(groups) + 1)]
        self.squared, self.summed, self.logged, self.rooted, self.ungated, self.normed, self.hi, self.lo = [
            k.flag(n) for n in ("squared", "summed", "norm_logged", "rooted", "ungated", "normed", "norm_hi", "norm_lo")]

    def inv(self, g):
        return self.k.scr[:, 8 + g % self.BATCH, :]

    def tensor(self, pe):
        k, first = self.k, self.first
        for n, (g, t) in enumerate(self.flat):
            if g >= self.BATCH and n == first[g]:
                pe.wait_ge(self.rooted, k.at(self.rooted, g - self.BATCH + 1))
            pe.wait_ge(self.squared, k.at(self.squared, n + 1))
            k.nc.tensor.matmul(k.ps[:, self.bank + g % self.BATCH, :], k.c("ones"), k.scr[:, n % 4, :], start=(n == first[g]),
                               stop=(n == first[g + 1] - 1)).then_inc(self.summed, 1)

    def wait_tile(self, pe, c):
        pe.wait_ge(self.lo, self.k.at(self.lo, c + 1))

    def scalar(self, act):
        k, first, nc = self.k, self.first, self.k.nc
        for b in range(0, len(self.groups), self.BATCH):
            batch = range(b, min(b + self.BATCH, len(self.groups)))
            for n in range(first[b], first[batch[-1] + 1]):
                if n >= 4:
                    act.wait_ge(self.summed, k.at(self.summed, n - 3))
                nc.scalar.activation(k.scr[:, n % 4, :], self.flat[n][1][0], ACT.Square).then_inc(self.squared, 1)
            for g in batch:
                act.wait_ge(self.summed, k.at(self.summed, first[g + 1]))
                if g >= self.BATCH:
                    act.wait_ge(self.normed, k.at(self.normed, first[g - self.BATCH + 1]))
                nc.scalar.activation(self.inv(g), k.ps[:, self.bank + g % self.BATCH, :], ACT.Ln, bias=k.c(self.eps),
                                     scale=1.0 / self.widths[g]).then_inc(self.logged, 1)
            for g in batch:
                act.wait_ge(self.logged, k.at(self.logged, g + 1))
                nc.scalar.activation(self.inv(g), self.inv(g), ACT.Exp, scale=-0.5).then_inc(self.rooted, 1)
        for n, (hi, _) in enumerate(self.parts):
            act.wait_ge(self.normed, k.at(self.normed, n + 1))
            nc.scalar.activation(hi, self.flat[n][1][1], ACT.Copy).then_inc(self.hi, 1)

    def vector(self, dve):
        k, nc = self.k, self.k.nc
        gated = 0
        for n in range(len(self.flat) + 1):
            if n < len(self.flat):
                g, (src, out, gain, gate) = self.flat[n]
                dve.wait_ge(self.rooted, k.at(self.rooted, g + 1))
                if gate is None:
                    nc.vector.scalar_tensor_tensor(out, src, gain, self.inv(g), ALU.mult, ALU.mult)\
                        .then_inc(self.normed, 1)
                else:
                    nc.vector.scalar_tensor_tensor(out, src, gain, self.inv(g), ALU.mult, ALU.mult)\
                        .then_inc(self.ungated, 1)
                    gated += 1
                    dve.wait_ge(self.ungated, k.at(self.ungated, gated))
                    nc.vector.tensor_tensor(out, out, gate, ALU.mult).then_inc(self.normed, 1)
            if self.parts and n >= 1:
                hi, lo = self.parts[n - 1]
                dve.wait_ge(self.hi, k.at(self.hi, n))
                nc.vector.tensor_tensor(lo, self.flat[n - 1][1][1], hi.bitcast(F32), ALU.subtract).then_inc(self.lo, 1)

    def passed(self):
        n, g = len(self.flat), len(self.groups)
        self.k.passed(squared=n, summed=n, norm_logged=g, rooted=g, normed=n, norm_hi=len(self.parts),
                      norm_lo=len(self.parts), ungated=sum(1 for _, t in self.flat if t[3] is not None))


def rms_phase(k, groups, eps, width):
    norm = RmsNorm(k, groups, eps, width)
    with k.nc.Block() as block:
        @block.scalar
        def _(act):
            norm.scalar(act)

        @block.tensor
        def _(pe):
            norm.tensor(pe)

        @block.vector
        def _(dve):
            norm.vector(dve)
    norm.passed()


def total_x(k, dve, j):
    totalled = k.flag("totalled")
    if j >= 1:
        if j >= 2:
            dve.wait_ge(totalled, k.at(totalled, j - 1))
        dve.wait_ge(k.flag("resid_added"), k.at(k.flag("resid_added"), j + 1))
        k.nc.vector.tensor_tensor(k.total, k.x[:, 0, :] if j == 1 else k.total, k.x[:, j, :], ALU.add)\
            .then_inc(totalled, 1)


class LayerNorm:

    def __init__(self, k, gain, shift, split=True):
        self.k, self.gain, self.shift, self.split = k, gain, shift, split
        self.cols = k.vec_cols
        self.added, self.centred, self.squared, self.summed, self.logged, self.rooted, self.normed, self.hi, \
            self.lo, self.shifted = [k.flag(n) for n in (
                "added", "centred", "squared", "summed", "norm_logged", "rooted", "normed", "norm_hi", "norm_lo",
                "shifted")]
        self.gain_at = [k.v(gain, n) for n in range(KD)]
        self.shift_at = [k.v(shift, n) for n in range(KD)]

    def tensor(self, pe):
        k, nc = self.k, self.k.nc
        nc.tensor.matmul(k.ps[:, 0, :], k.c("ones"), k.total, start=True, stop=True).then_inc(self.added, 1)
        for n in range(KD):
            pe.wait_ge(self.squared, k.at(self.squared, n + 1))
            nc.tensor.matmul(k.ps[:, 1, :], k.c("ones"), k.scr[:, n % 4, :], start=(n == 0),
                             stop=(n == KD - 1)).then_inc(self.summed, 1)

    def wait_tile(self, pe, c):
        pe.wait_ge(self.lo, self.k.at(self.lo, c + 1))

    def vector(self, dve):
        k, nc = self.k, self.k.nc
        dve.wait_ge(self.added, k.at(self.added, 1))
        for n in range(KD):
            nc.vector.scalar_tensor_tensor(k.x[:, n, :], k.ps[:, 0, :], -1.0 / D, k.x[:, n, :], ALU.mult,
                                           ALU.add).then_inc(self.centred, 1)
        dve.wait_ge(self.rooted, k.at(self.rooted, 1))
        for n in range(KD + 1):
            if n < KD:
                nc.vector.scalar_tensor_tensor(k.x[:, n, :], k.x[:, n, :], self.gain_at[n], k.scr[:, 8, :],
                                               ALU.mult, ALU.mult).then_inc(self.normed, 1)
            if self.split and n >= 1:
                dve.wait_ge(self.hi, k.at(self.hi, n))
                nc.vector.scalar_tensor_tensor(k.in_lo[:, n - 1, :], k.x[:, n - 1, :], self.shift_at[n - 1],
                                               k.in_hi[:, n - 1, :].bitcast(F32), ALU.add, ALU.subtract)\
                    .then_inc(self.lo, 1)

    def scalar(self, act):
        k, nc = self.k, self.k.nc
        for n in range(KD):
            act.wait_ge(self.centred, k.at(self.centred, n + 1))
            if n >= 4:
                act.wait_ge(self.summed, k.at(self.summed, n - 3))
            nc.scalar.activation(k.scr[:, n % 4, :], k.x[:, n, :], ACT.Square).then_inc(self.squared, 1)
        act.wait_ge(self.summed, k.at(self.summed, KD))
        nc.scalar.activation(k.scr[:, 8, :], k.ps[:, 1, :], ACT.Ln, bias=k.c("ln_eps"), scale=1.0 / D)\
            .then_inc(self.logged, 1)
        act.wait_ge(self.logged, k.at(self.logged, 1))
        nc.scalar.activation(k.scr[:, 8, :], k.scr[:, 8, :], ACT.Exp, scale=-0.5).then_inc(self.rooted, 1)
        for n in range(KD) if self.split else ():
            act.wait_ge(self.normed, k.at(self.normed, n + 1))
            nc.scalar.activation(k.in_hi[:, n, :], k.x[:, n, :], ACT.Identity, bias=self.shift_at[n])\
                .then_inc(self.hi, 1)
        for n in range(KD):
            if self.split:
                act.wait_ge(self.lo, k.at(self.lo, n + 1))
            else:
                act.wait_ge(self.normed, k.at(self.normed, n + 1))
            nc.scalar.activation(k.x[:, n, :], k.x[:, n, :], ACT.Identity, bias=self.shift_at[n])\
                .then_inc(self.shifted, 1)

    def passed(self):
        parts = KD if self.split else 0
        self.k.passed(norm_hi=parts, norm_lo=parts, added=1, centred=KD, squared=KD, summed=KD, rooted=1, normed=KD,
                      norm_logged=1, shifted=KD)


def output_phase(k, gain, shift, out):
    norm = LayerNorm(k, gain, shift, split=False)
    sent = k.flag("output_sent")
    with k.nc.Block() as block:
        @block.scalar
        def _(act):
            norm.scalar(act)

        @block.tensor
        def _(pe):
            norm.tensor(pe)

        @block.vector
        def _(dve):
            norm.vector(dve)

        @block.sync
        def _(sp):
            for n in range(KD):
                sp.wait_ge(norm.shifted, k.at(norm.shifted, n + 1))
                sp.dma_start(out[n], k.x[:, n, :]).then_inc(sent, 16)
            sp.wait_ge(sent, k.at(sent, 16 * KD))
    norm.passed()


def glu_phase(k, up, down, norm=None):
    nc = k.nc
    ends = k.use([range(a, a + KD) for pair in up for a in pair] + [range(a, a + KF2) for a in down])
    silu, hidden, hi_ready, lo_ready, resid = [k.flag(n) for n in (
        "silu_done", "hidden_made", "hi_ready", "lo_ready", "resid_added")]
    made = lambda f: k.big[:, KF2 + f, :]
    hi, lo = lambda f: k.parts[:, f, :], lambda f: k.parts[:, KF2 + f, :]
    with nc.Block() as block:
        @block.sync
        def _(sp):
            k.load_slabs(sp)

        @block.tensor
        def _(pe):
            def hidden_tile(pe, c):
                pe.wait_ge(lo_ready, k.at(lo_ready, c + 1))

            if norm:
                norm.tensor(pe)
            x = lambda c: (k.in_hi[:, c, :], k.in_lo[:, c, :])
            for f, pair in enumerate(up):
                if f >= 3:
                    pe.wait_ge(hidden, k.at(hidden, f - 2))
                for b, at in enumerate(pair):
                    add_up(k, pe, k.ps[:, 2 * (f % 3) + b, :], [(at + c, x(c)) for c in range(KD)],
                           norm.wait_tile if norm and f == b == 0 else None)
            for j, at in enumerate(down):
                if j >= 2:
                    pe.wait_ge(resid, k.at(resid, j - 1))
                add_up(k, pe, k.ps[:, 6 + j % 2, :], [(at + c, (hi(c), lo(c))) for c in range(KF2)],
                       hidden_tile if j == 0 else None)

        @block.scalar
        def _(act):
            if norm:
                norm.scalar(act)
            for f in range(KF2 + 1):
                if f < KF2:
                    k.high_slabs(act, up[f][1])
                    act.wait_ge(k.sums_done, ends[2 * f])
                    if f >= 2:
                        act.wait_ge(hidden, k.at(hidden, f - 1))
                    nc.scalar.activation(k.scr[:, f % 2, :], k.ps[:, 2 * (f % 3), :], ACT.Silu).then_inc(silu, 1)
                if f >= 1:
                    act.wait_ge(hidden, k.at(hidden, f))
                    nc.scalar.activation(hi(f - 1), made(f - 1), ACT.Copy).then_inc(hi_ready, 1)
            k.high_slabs(act, down[-1] + KF2 - 1)

        @block.vector
        def _(dve):
            if norm:
                norm.vector(dve)
            for f in range(KF2 + 1):
                if f < KF2:
                    dve.wait_ge(silu, k.at(silu, f + 1))
                    dve.wait_ge(k.sums_done, ends[2 * f + 1])
                    nc.vector.scalar_tensor_tensor(made(f), k.ps[:, 2 * (f % 3) + 1, :], 0.5, k.scr[:, f % 2, :],
                                                   ALU.mult, ALU.mult).then_inc(hidden, 1)
                if f >= 1:
                    dve.wait_ge(hi_ready, k.at(hi_ready, f))
                    nc.vector.tensor_tensor(lo(f - 1), made(f - 1), hi(f - 1).bitcast(F32), ALU.subtract)\
                        .then_inc(lo_ready, 1)
            for j in range(KD):
                dve.wait_ge(k.sums_done, ends[2 * KF2 + j])
                nc.vector.scalar_tensor_tensor(k.x[:, j, :], k.x[:, j, :], ALPHA, k.ps[:, 6 + j % 2, :],
                                               ALU.mult, ALU.add).then_inc(resid, 1)
                total_x(k, dve, j)

        @block.gpsimd
        def _(pool):
            k.low_slabs(pool)
    if norm:
        norm.passed()
    k.passed(silu_done=KF2, hidden_made=KF2, hi_ready=KF2, lo_ready=KF2, resid_added=KD, totalled=KD - 1)


def relu2_phase(k, up, down, norm=None):
    nc = k.nc
    n = len(up)
    ends = k.use([range(a, a + KD) for a in up] + [range(a, a + n) for a in down])
    relu, hidden, hi_ready, lo_ready, resid = [k.flag(x) for x in (
        "relu_done", "hidden_made", "hi_ready", "lo_ready", "resid_added")]
    made = lambda f: k.big[:, n + f, :]
    hi, lo = lambda f: k.parts[:, f, :], lambda f: k.parts[:, n + f, :]
    with nc.Block() as block:
        @block.sync
        def _(sp):
            k.load_slabs(sp)

        @block.tensor
        def _(pe):
            def hidden_tile(pe, c):
                pe.wait_ge(lo_ready, k.at(lo_ready, c + 1))

            if norm:
                norm.tensor(pe)
            for f, at in enumerate(up):
                if f >= 4:
                    pe.wait_ge(hidden, k.at(hidden, f - 3))
                add_up(k, pe, k.ps[:, f % 4, :], [(at + c, (k.in_hi[:, c, :], k.in_lo[:, c, :])) for c in range(KD)],
                       norm.wait_tile if norm and f == 0 else None)
            for j, at in enumerate(down):
                if j >= 2:
                    pe.wait_ge(resid, k.at(resid, j - 1))
                add_up(k, pe, k.ps[:, 4 + j % 2, :], [(at + c, (hi(c), lo(c))) for c in range(n)],
                       hidden_tile if j == 0 else None)

        @block.scalar
        def _(act):
            if norm:
                norm.scalar(act)
            for f in range(n + 1):
                if f < n:
                    k.high_slabs(act, up[f])
                    act.wait_ge(k.sums_done, ends[f])
                    if f >= 2:
                        act.wait_ge(hidden, k.at(hidden, f - 1))
                    nc.scalar.activation(k.scr[:, f % 2, :], k.ps[:, f % 4, :], ACT.Relu).then_inc(relu, 1)
                if f >= 1:
                    act.wait_ge(hidden, k.at(hidden, f))
                    nc.scalar.activation(hi(f - 1), made(f - 1), ACT.Copy).then_inc(hi_ready, 1)
            k.high_slabs(act, down[-1] + n - 1)

        @block.vector
        def _(dve):
            if norm:
                norm.vector(dve)
            for f in range(n + 1):
                if f < n:
                    dve.wait_ge(relu, k.at(relu, f + 1))
                    nc.vector.tensor_tensor(made(f), k.ps[:, f % 4, :], k.scr[:, f % 2, :], ALU.mult)\
                        .then_inc(hidden, 1)
                if f >= 1:
                    dve.wait_ge(hi_ready, k.at(hi_ready, f))
                    nc.vector.tensor_tensor(lo(f - 1), made(f - 1), hi(f - 1).bitcast(F32), ALU.subtract)\
                        .then_inc(lo_ready, 1)
            for j in range(KD):
                dve.wait_ge(k.sums_done, ends[n + j])
                nc.vector.tensor_tensor(k.x[:, j, :], k.x[:, j, :], k.ps[:, 4 + j % 2, :], ALU.add)\
                    .then_inc(resid, 1)

        @block.gpsimd
        def _(pool):
            k.low_slabs(pool)
    if norm:
        norm.passed()
    k.passed(relu_done=n, hidden_made=n, hi_ready=n, lo_ready=n, resid_added=KD)


def split_phase(k, items):
    nc = k.nc
    hi_ready, lo_ready = k.flag("hi_ready"), k.flag("lo_ready")
    with nc.Block() as block:
        @block.scalar
        def _(act):
            for t, hi, _ in items:
                nc.scalar.activation(hi, t, ACT.Copy).then_inc(hi_ready, 1)

        @block.vector
        def _(dve):
            for n, (t, hi, lo) in enumerate(items):
                dve.wait_ge(hi_ready, k.at(hi_ready, n + 1))
                nc.vector.tensor_tensor(lo, t, hi.bitcast(F32), ALU.subtract).then_inc(lo_ready, 1)
    k.passed(hi_ready=len(items), lo_ready=len(items))


def project_phase(k, tiles, alpha, parts, norm=None):
    nc = k.nc
    ends = k.use([range(a, a + KD) for a in tiles])
    resid = k.flag("resid_added")
    with nc.Block() as block:
        @block.sync
        def _(sp):
            k.load_slabs(sp)

        @block.tensor
        def _(pe):
            if norm:
                norm.tensor(pe)
            for j, at in enumerate(tiles):
                if j >= 4:
                    pe.wait_ge(resid, k.at(resid, j - 3))
                add_up(k, pe, k.ps[:, j % 4, :], [(at + c, parts(c)) for c in range(KD)],
                       norm.wait_tile if norm and j == 0 else None)

        @block.scalar
        def _(act):
            if norm:
                norm.scalar(act)
            k.high_slabs(act, tiles[-1] + KD - 1)

        @block.vector
        def _(dve):
            if norm:
                norm.vector(dve)
            for j in range(len(tiles)):
                dve.wait_ge(k.sums_done, ends[j])
                nc.vector.scalar_tensor_tensor(k.x[:, j, :], k.x[:, j, :], alpha, k.ps[:, j % 4, :],
                                               ALU.mult, ALU.add).then_inc(resid, 1)
                total_x(k, dve, j)

        @block.gpsimd
        def _(pool):
            k.low_slabs(pool)
    if norm:
        norm.passed()
    k.passed(resid_added=len(tiles), totalled=KD - 1)


def merge_phase(k, tiles, y, y_parts, out, norm):
    nc = k.nc
    ends = k.use([r for g, b in tiles for r in (range(g, g + KD), range(b, b + 4))])
    hi_ready, lo_ready = k.flag("hi_ready"), k.flag("lo_ready")
    early, late = [(0, c) for c in range(4)], [(n, c) for n in (1, 2) for c in range(4)]
    gate, merged, product = [k.flag(n) for n in ("gate_ready", "merged", "gated_product")]
    n_jobs = len(tiles)
    with nc.Block() as block:
        @block.sync
        def _(sp):
            k.load_slabs(sp)

        def high(items):
            for n, c in items:
                nc.scalar.activation(y_parts(n, c)[0], y(n, c), ACT.Copy).then_inc(hi_ready, 1)

        def low(dve, at, items):
            for m, (n, c) in enumerate(items):
                dve.wait_ge(hi_ready, k.at(hi_ready, at + m + 1))
                nc.vector.tensor_tensor(y_parts(n, c)[1], y(n, c), y_parts(n, c)[0].bitcast(F32), ALU.subtract)\
                    .then_inc(lo_ready, 1)

        @block.tensor
        def _(pe):
            def branch_tile(pe, c):
                if j == 3:
                    norm.wait_tile(pe, c)
                else:
                    pe.wait_ge(lo_ready, k.at(lo_ready, 4 * j + c + 1))

            norm.tensor(pe)
            for j, (g, b) in enumerate(tiles):
                if j >= 4:
                    pe.wait_ge(product, k.at(product, j - 3))
                add_up(k, pe, k.ps[:, 2 * (j % 4), :], [(g + c, (k.in_hi[:, c, :], k.in_lo[:, c, :]))
                                                        for c in range(KD)])
                add_up(k, pe, k.ps[:, 2 * (j % 4) + 1, :], [(b + c, y_parts(j % 4, c)) for c in range(4)],
                       branch_tile if j < 4 else None)

        @block.scalar
        def _(act):
            high(early)
            norm.scalar(act)
            high(late)
            for j in range(n_jobs):
                k.high_slabs(act, tiles[j][1] + 3)
                act.wait_ge(k.sums_done, ends[2 * j])
                if j >= 2:
                    act.wait_ge(product, k.at(product, j - 1))
                d, n = divmod(j, 4)
                nc.scalar.activation(k.scr[:, j % 2, :], k.ps[:, 2 * (j % 4), :], ACT.Sigmoid,
                                     bias=k.v("b_gates", 8 * n + d)).then_inc(gate, 1)

        @block.vector
        def _(dve):
            low(dve, 0, early)
            norm.vector(dve)
            low(dve, len(early), late)
            for j in range(n_jobs):
                d, n = divmod(j, 4)
                dve.wait_ge(gate, k.at(gate, j + 1))
                dve.wait_ge(k.sums_done, ends[2 * j + 1])
                to = out(d) if n == 0 else k.scr[:, 2 + j % 2, :]
                if n > 0 and j > 4:
                    dve.wait_ge(merged, k.at(merged, j - 1 - (j - 2) // 4 - 1))
                nc.vector.tensor_tensor(to, k.scr[:, j % 2, :], k.ps[:, 2 * (j % 4) + 1, :], ALU.mult)\
                    .then_inc(product, 1)
                if n > 0:
                    dve.wait_ge(product, k.at(product, j + 1))
                    if n > 1:
                        dve.wait_ge(merged, k.at(merged, 3 * d + n - 1))
                    nc.vector.tensor_tensor(out(d), out(d), to, ALU.add).then_inc(merged, 1)

        @block.gpsimd
        def _(pool):
            k.low_slabs(pool)
    norm.passed()
    k.passed(hi_ready=len(early + late), lo_ready=len(early + late), gate_ready=n_jobs, gated_product=n_jobs, merged=3 * n_jobs // 4)


class MlstmGates:

    def __init__(self, k, f_row, i_row, f_fx, taken):
        self.k, self.tiles, self.taken = k, (f_row, i_row, f_fx), taken
        self.flags = {n: k.flag(n) for n in ("soft", "log_f", "run_f", "u_ready", "m_ready", "m_sum", "fx_copied")}

    def scalar(self, act):
        k, nc, s = self.k, self.k.nc, self.flags
        f_row, tmp = self.tiles[0], k.scr[:, 0, :]
        act.wait_ge(self.taken, k.at(self.taken, 2))
        nc.scalar.activation(tmp, f_row, ACT.Abs).then_inc(s["soft"], 1)
        act.wait_ge(s["soft"], k.at(s["soft"], 1))
        nc.scalar.activation(tmp, tmp, ACT.Exp, scale=-1.0).then_inc(s["soft"], 1)
        act.wait_ge(s["soft"], k.at(s["soft"], 2))
        nc.scalar.activation(tmp, tmp, ACT.Ln, bias=1.0).then_inc(s["soft"], 1)

    def vector(self, dve):
        k, nc, s = self.k, self.k.nc, self.flags
        f_row, i_row, f_fx = self.tiles
        tmp, run_f, u, m, em = [k.scr[:, i, :] for i in range(5)]
        one = k.c("one").broadcast_to([P, T])
        one4 = k.c("one", 4).broadcast_to([4, T])
        dve.wait_ge(s["soft"], k.at(s["soft"], 3))
        nc.vector.scalar_tensor_tensor(tmp, f_row, 0.0, tmp, ALU.min, ALU.subtract).then_inc(s["log_f"], 1)
        dve.wait_ge(s["log_f"], k.at(s["log_f"], 1))
        nc.vector.tensor_tensor_scan(run_f, one, tmp, 0.0, ALU.mult, ALU.add).then_inc(s["run_f"], 1)
        dve.wait_ge(s["run_f"], k.at(s["run_f"], 1))
        nc.vector.tensor_copy(f_fx[0:4], run_f[32:36]).then_inc(s["fx_copied"], 1)
        nc.vector.tensor_tensor(u[0:4], i_row[0:4], run_f[0:4], ALU.subtract).then_inc(s["u_ready"], 1)
        dve.wait_ge(s["u_ready"], k.at(s["u_ready"], 1))
        nc.vector.tensor_tensor_scan(m[0:4], one4, u[0:4], 0.0, ALU.mult, ALU.max).then_inc(s["m_ready"], 1)
        dve.wait_ge(s["m_ready"], k.at(s["m_ready"], 1))
        nc.vector.tensor_tensor(em[0:4], run_f[0:4], m[0:4], ALU.add).then_inc(s["m_sum"], 1)

    def passed(self):
        self.k.passed(soft=3, log_f=1, run_f=1, u_ready=1, m_ready=1, m_sum=1, fx_copied=1)


def mlstm_phase(k, q, key, v, y):
    nc = k.nc
    names = ("stabil", "u_turned", "u_col", "max_row", "scored", "arg_ready", "weight", "tri_done", "weighted", "head_summed", "em_row", "abs_den",
             "den_ready", "den_inv", "head_done", "unit_summed")
    s = {n: k.flag(n) for n in names}
    u, m, em = [k.scr[:, i, :] for i in (2, 3, 4)]
    ucol = k.stat[:, 0, 0:16]
    units = [(h, b) for h in range(HEADS) for b in range(QB)]
    n = len(units)
    with nc.Block() as block:
        @block.scalar
        def _(act):
            nc.scalar.activation(em[0:4], em[0:4], ACT.Exp, scale=-1.0).then_inc(s["stabil"], 1)
            act.wait_ge(s["u_turned"], k.at(s["u_turned"], 1))
            nc.scalar.activation(ucol, k.ps[:, 0, 0:16], ACT.Copy).then_inc(s["u_col"], 1)
            for i in range(n + 2):
                if i < n:
                    e = k.scr[:, 6 + i % 2, 0:T - P * units[i][1]]
                    act.wait_ge(s["arg_ready"], k.at(s["arg_ready"], i + 1))
                    nc.scalar.activation(e, e, ACT.Exp).then_inc(s["weight"], 1)
                if i >= 5 and (i - 5) % 4 == 0:
                    h = (i - 5) // 4
                    act.wait_ge(s["head_summed"], k.at(s["head_summed"], h + 1))
                    if h >= 1:
                        act.wait_ge(s["den_ready"], k.at(s["den_ready"], h))
                    nc.scalar.activation(k.scr[:, 10, :], k.ps[:, 6 + h % 2, :], ACT.Abs)\
                        .then_inc(s["abs_den"], 1)

        @block.tensor
        def _(pe):
            for b in range(QB):
                mm = nc.tensor.transpose(k.ps[:, 0, 4 * b:4 * b + 4], u[0:4, P * b:P * b + P], k.c("ident", 4)[:, 0:4])
            mm.then_inc(s["u_turned"], 1)
            pe.wait_ge(s["u_col"], k.at(s["u_col"], 1))
            pe.wait_ge(s["stabil"], k.at(s["stabil"], 1))
            for i in range(n + 1):
                if i < n:
                    h, b = units[i]
                    if b == 0:
                        if h >= 2:
                            pe.wait_ge(s["head_done"], k.at(s["head_done"], h - 1))
                        nc.tensor.matmul(k.ps[:, h % 2, :], k.c("negident", 4)[:, h:h + 1].broadcast_to([4, P]),
                                         m[0:4], start=True, stop=True).then_inc(s["max_row"], 1)
                    if i >= 2:
                        pe.wait_ge(s["weighted"], k.at(s["weighted"], i - 1))
                    nc.tensor.matmul(k.ps[:, 2 + i % 2, 0:T - P * b], key(h)[:, P * b:P * b + P], q(h)[:, P * b:T],
                                     start=True, stop=True).then_inc(s["scored"], 1)
                if i >= 1:
                    h, b = units[i - 1]
                    w = k.scr[:, 8 + (i - 1) % 2, 0:T - P * b]
                    pe.wait_ge(s["weighted"], k.at(s["weighted"], i))
                    if b == 0 and h >= 2:
                        pe.wait_ge(s["head_done"], k.at(s["head_done"], h - 1))
                    nc.tensor.matmul(k.ps[:, 4 + h % 2, P * b:T], v(b, h), w, start=(b == 0), stop=(b == QB - 1))
                    nc.tensor.matmul(k.ps[:, 6 + h % 2, P * b:T], k.c("ones"), w, start=(b == 0),
                                     stop=(b == QB - 1)).then_inc(s["unit_summed"], 1)
                    if b == QB - 1:
                        nc.tensor.matmul(k.ps[:, h % 2, :], k.c("ident", 4)[:, h:h + 1].broadcast_to([4, P]),
                                         em[0:4], start=True, stop=True).then_inc(s["head_summed"], 1)

        @block.vector
        def _(dve):
            dve.wait_ge(s["u_col"], k.at(s["u_col"], 1))

            def argument(i):
                h, b = units[i]
                if b == 0:
                    dve.wait_ge(s["max_row"], k.at(s["max_row"], h + 1))
                if i >= 2:
                    dve.wait_ge(s["weighted"], k.at(s["weighted"], i - 1))
                nc.vector.tensor_scalar(k.scr[:, 6 + i % 2, 0:T - P * b], k.ps[:, h % 2, P * b:T],
                                        ucol[:, 4 * b + h:4 * b + h + 1], 0.0, ALU.add, ALU.min)\
                    .then_inc(s["arg_ready"], 1)

            argument(0)
            for i in range(n + 2):
                if i + 1 < n:
                    argument(i + 1)
                if i < n:
                    h, b = units[i]
                    e = k.scr[:, 6 + i % 2, :]
                    dve.wait_ge(s["weight"], k.at(s["weight"], i + 1))
                    nc.vector.tensor_tensor(e[:, 0:P], e[:, 0:P], k.c("tri"), ALU.mult).then_inc(s["tri_done"], 1)
                    dve.wait_ge(s["tri_done"], k.at(s["tri_done"], i + 1))
                    dve.wait_ge(s["scored"], k.at(s["scored"], i + 1))
                    if i >= 2:
                        dve.wait_ge(s["unit_summed"], k.at(s["unit_summed"], i - 1))
                    nc.vector.scalar_tensor_tensor(k.scr[:, 8 + i % 2, 0:T - P * b],
                                                   k.ps[:, 2 + i % 2, 0:T - P * b], P ** -0.5,
                                                   e[:, 0:T - P * b], ALU.mult, ALU.mult)\
                        .then_inc(s["weighted"], 1)
                if i >= 5 and (i - 5) % 4 == 0:
                    h = (i - 5) // 4
                    den = k.scr[:, 11, :]
                    dve.wait_ge(s["abs_den"], k.at(s["abs_den"], h + 1))
                    nc.vector.tensor_tensor(den, k.scr[:, 10, :], k.ps[:, h % 2, :], ALU.max)\
                        .then_inc(s["den_ready"], 1)
                    dve.wait_ge(s["den_ready"], k.at(s["den_ready"], h + 1))
                    nc.vector.reciprocal(den, den).then_inc(s["den_inv"], 1)
                    dve.wait_ge(s["den_inv"], k.at(s["den_inv"], h + 1))
                    nc.vector.tensor_tensor(y(h), den, k.ps[:, 4 + h % 2, :], ALU.mult)\
                        .then_inc(s["head_done"], 1)
    k.passed(stabil=1, u_turned=1, u_col=1, max_row=HEADS, scored=n, arg_ready=n, weight=n, tri_done=n, weighted=n, head_summed=HEADS,
             abs_den=HEADS, den_ready=HEADS, den_inv=HEADS, head_done=HEADS, unit_summed=n)


class Unit:

    def __init__(self, scores, width, values, group, first, last, rows, out, scale, mask=None, keep=None, gate=None):
        self.scores, self.width, self.values = scores, width, values
        self.group, self.first, self.last, self.rows, self.out = group, first, last, rows, out
        self.scale, self.mask, self.keep, self.gate = scale, mask, keep, gate
        self.blocks = [(a, min(P, width - a)) for a in range(0, width, P)]


def attend(k, pe, u, n, units, probs, ready, turned, laid, unit_done, stored):
    nc = k.nc
    if 0 <= u < n:
        pe.wait_ge(ready, k.at(ready, u + 1))
        if u >= 2:
            pe.wait_ge(laid, k.at(laid, u - 1))
        for a, w in units[u].blocks:
            mm = nc.tensor.transpose(k.ps[0:w, 3 + u % 2, a:a + P], probs(u)[:, a:a + w], k.c("ident"))
        mm.then_inc(turned, 1)
    if 0 <= u - 2 < n:
        one = units[u - 2]
        pe.wait_ge(laid, k.at(laid, u - 1))
        if one.first and one.group >= 3:
            pe.wait_ge(stored, k.at(stored, one.group - 2))
        lo, hi = one.rows
        for j, ((a, w), val) in enumerate(zip(one.blocks, one.values)):
            mm = nc.tensor.matmul(k.ps[lo:hi, 5 + one.group % 3, 0:P], val, k.scr[0:w, 6 + (u - 2) % 3, a:a + P],
                                  start=(one.first and j == 0), stop=(one.last and j == len(one.blocks) - 1))
        mm.then_inc(unit_done, 1)


def lay_and_store(k, act, u, n, units, turned, laid, unit_done, stored):
    nc = k.nc
    if 0 <= u < n:
        act.wait_ge(turned, k.at(turned, u + 1))
        if u >= 3:
            act.wait_ge(unit_done, k.at(unit_done, u - 2))
        rows = units[u].blocks[0][1]
        cols = P * len(units[u].blocks)
        nc.scalar.activation(k.scr[0:rows, 6 + u % 3, 0:cols], k.ps[0:rows, 3 + u % 2, 0:cols], ACT.Copy)\
            .then_inc(laid, 1)
    if 0 <= u - 3 < n and units[u - 3].last:
        one = units[u - 3]
        lo, hi = one.rows
        act.wait_ge(unit_done, k.at(unit_done, u - 2))
        nc.scalar.activation(one.out, k.ps[lo:hi, 5 + one.group % 3, 0:P], ACT.Copy).then_inc(stored, 1)


def attention_phase(k, units, index=None, steps=range(0)):
    nc = k.nc
    scored, masked, row_max, expd, row_inv, row_gate, probs_ready, turned, laid, unit_done, stored = [
        k.flag(n) for n in ("scored", "masked", "row_max", "probs_expd", "row_inv", "row_gate", "probs_ready",
                              "turned", "laid", "unit_done", "stored")]
    n = len(units)
    ring, lag = 6, 3
    probs = lambda i: k.scr[:, i % ring, :]
    col = lambda kind, i: k.stat[:, kind, i:i + 1]
    gates = [sum(1 for u in units[:i + 1] if u.gate is not None) for i in range(n)]
    groups = sum(1 for u in units if u.last)
    assert n <= 56
    with nc.Block() as block:
        @block.tensor
        def _(pe):
            for i in range(n + lag + 2):
                if i < n:
                    u = units[i]
                    if i >= 3:
                        pe.wait_ge(masked, k.at(masked, i - 2))
                    for j, (lhsT, rhs) in enumerate(u.scores):
                        mm = nc.tensor.matmul(k.ps[:, i % 3, 0:u.width], lhsT, rhs, start=(j == 0),
                                              stop=(j == len(u.scores) - 1))
                    mm.then_inc(scored, 1)
                attend(k, pe, i - lag, n, units, probs, probs_ready, turned, laid, unit_done, stored)

        @block.vector
        def _(dve):
            for i in range(n + 1):
                if i < n:
                    u = units[i]
                    s = probs(i)[:, 0:u.width]
                    dve.wait_ge(scored, k.at(scored, i + 1))
                    if i >= ring:
                        dve.wait_ge(turned, k.at(turned, i - ring + 1))
                    nc.vector.scalar_tensor_tensor(s, k.ps[:, i % 3, 0:u.width], u.scale, u.mask, ALU.mult, ALU.add)\
                        .then_inc(masked, 1)
                    dve.wait_ge(masked, k.at(masked, i + 1))
                    nc.vector.tensor_reduce(col(0, i), s, AX, ALU.max, negate=True).then_inc(row_max, 1)
                take_top(k, dve, index, share(steps, i, n + 1), steps.start)
                if i >= 1:
                    u = units[i - 1]
                    p = probs(i - 1)[:, 0:u.width]
                    inv = col(1, i - 1)
                    dve.wait_ge(expd, k.at(expd, i))
                    nc.vector.reciprocal(inv, inv).then_inc(row_inv, 1)
                    dve.wait_ge(row_inv, k.at(row_inv, i))
                    if u.gate is not None:
                        nc.vector.tensor_tensor(inv, inv, u.gate, ALU.mult).then_inc(row_gate, 1)
                        dve.wait_ge(row_gate, k.at(row_gate, gates[i - 1]))
                    if u.keep is None:
                        nc.vector.tensor_scalar(p, p, inv, None, ALU.mult).then_inc(probs_ready, 1)
                    else:
                        nc.vector.scalar_tensor_tensor(p, p, inv, u.keep, ALU.mult, ALU.mult)\
                            .then_inc(probs_ready, 1)

        @block.scalar
        def _(act):
            for i in range(n + lag + 3):
                if i < n:
                    p = probs(i)[:, 0:units[i].width]
                    act.wait_ge(row_max, k.at(row_max, i + 1))
                    nc.scalar.activation(p, p, ACT.Exp, bias=col(0, i), accum_out=col(1, i)).then_inc(expd, 1)
                lay_and_store(k, act, i - lag, n, units, turned, laid, unit_done, stored)
    k.passed(scored=n, masked=n, row_max=n, probs_expd=n, row_inv=n, row_gate=gates[-1], probs_ready=n, turned=n,
             laid=n, unit_done=n, stored=groups, top8=len(steps), top8_taken=len(steps), select_made=rows_done(steps))


def stick_phase(k, units, probs, soft_at, index, steps):
    nc = k.nc
    scored, masked, soft, logged, broken, rest, exponent, probs_ready, turned, laid, unit_done, stored = [
        k.flag(n) for n in ("scored", "masked", "soft", "logged", "broken", "rest", "exponent", "probs_ready",
                              "turned", "laid", "unit_done", "stored")]
    n, batch = len(units), 4
    ring = 3 * batch
    batches = n // batch
    rest_at = lambda i: k.scr[:, 10 + i % 2, :]
    groups = sum(1 for u in units if u.last)
    with nc.Block() as block:
        @block.tensor
        def _(pe):
            for i in range(n + 2 * batch + 2):
                if i < n:
                    u = units[i]
                    if i >= 3:
                        pe.wait_ge(masked, k.at(masked, i - 2))
                    nc.tensor.matmul(k.ps[:, i % 3, 0:u.width], u.scores[0][0], u.scores[0][1], start=True,
                                     stop=True).then_inc(scored, 1)
                attend(k, pe, i - 2 * batch, n, units, probs, probs_ready, turned, laid, unit_done, stored)

        @block.vector
        def _(dve):
            for g in range(batches + 1):
                for i in range(batch * g, batch * (g + 1)) if g < batches else ():
                    u = units[i]
                    dve.wait_ge(scored, k.at(scored, i + 1))
                    if i >= ring:
                        dve.wait_ge(turned, k.at(turned, i - ring + 1))
                    nc.vector.scalar_tensor_tensor(probs(i)[:, 0:u.width], k.ps[:, i % 3, 0:u.width], u.scale,
                                                   u.mask, ALU.mult, ALU.add).then_inc(masked, 1)
                for i in range(batch * (g - 1), batch * g) if g >= 1 else ():
                    w = units[i].width
                    z, l, r = [x(i)[:, 0:w] for x in (probs, soft_at, rest_at)]
                    dve.wait_ge(logged, k.at(logged, i + 1))
                    nc.vector.scalar_tensor_tensor(l, z, 0.0, l, ALU.max, ALU.add).then_inc(broken, 1)
                    dve.wait_ge(broken, k.at(broken, i + 1))
                    if i >= 2:
                        dve.wait_ge(exponent, k.at(exponent, i - 1))
                    nc.vector.tensor_tensor_scan(r[:, ::-1], k.c("one").broadcast_to([P, w]), l[:, ::-1], 0.0,
                                                 ALU.mult, ALU.add).then_inc(rest, 1)
                if g < batches:
                    take_top(k, dve, index, share(steps, g, batches), steps.start)

        @block.gpsimd
        def _(pool):
            for i in range(n):
                z, r = [x(i)[:, 0:units[i].width] for x in (probs, rest_at)]
                pool.wait_ge(rest, k.at(rest, i + 1))
                nc.gpsimd.tensor_tensor(z, z, r, ALU.subtract).then_inc(exponent, 1)

        @block.scalar
        def _(act):
            for g in range(batches + 2):
                new = range(batch * g, batch * (g + 1)) if g < batches else ()
                old = range(batch * (g - 1), batch * g) if 1 <= g <= batches else ()
                for i in new:
                    z, l = probs(i)[:, 0:units[i].width], soft_at(i)[:, 0:units[i].width]
                    act.wait_ge(masked, k.at(masked, i + 1))
                    if i >= batch:
                        act.wait_ge(rest, k.at(rest, i - batch + 1))
                    nc.scalar.activation(l, z, ACT.Abs).then_inc(soft, 1)
                    act.wait_ge(soft, k.at(soft, 2 * i + 1))
                    nc.scalar.activation(l, l, ACT.Exp, scale=-1.0).then_inc(soft, 1)
                for i in old:
                    p = probs(i)[:, 0:units[i].width]
                    act.wait_ge(exponent, k.at(exponent, i + 1))
                    nc.scalar.activation(p, p, ACT.Exp).then_inc(probs_ready, 1)
                for j in range(batch):
                    if new:
                        i = new[j]
                        l = soft_at(i)[:, 0:units[i].width]
                        act.wait_ge(soft, k.at(soft, 2 * i + 2))
                        nc.scalar.activation(l, l, ACT.Ln, bias=1.0).then_inc(logged, 1)
                    if g >= 1:
                        lay_and_store(k, act, batch * (g - 1) + j, n, units, turned, laid, unit_done, stored)
    k.passed(scored=n, masked=n, soft=2 * n, logged=n, broken=n, rest=n, exponent=n, probs_ready=n, turned=n,
             laid=n, unit_done=n, stored=groups, top8=len(steps), top8_taken=len(steps), select_made=rows_done(steps))


def conv_vector(k, dve, padded, out, taken):
    nc = k.nc
    edge, step = k.flag("edge"), k.flag("conv_step")
    nc.vector.memset(padded[:, :, 0:3], 0.0).then_inc(edge, 1)
    dve.wait_ge(edge, k.at(edge, 1))
    done = 0
    for j in range(4):
        dve.wait_ge(taken, k.at(taken, j + 1))
        for t in range(4):
            x = padded[:, j, t:t + T]
            w = k.v("conv_w", 4 * t + j)
            if t == 0:
                nc.vector.tensor_scalar(out(j), x, w, k.v("conv_b", j), ALU.mult, ALU.add).then_inc(step, 1)
            else:
                dve.wait_ge(step, k.at(step, done))
                nc.vector.scalar_tensor_tensor(out(j), x, w, out(j), ALU.mult, ALU.add).then_inc(step, 1)
            done += 1


class Lru:

    def __init__(self, k, xc, r, i, ygate, u, sq, y):
        self.k, self.tiles = k, (xc, r, i, ygate, u, sq, y)
        self.flags = {n: k.flag(n) for n in (
            "soft", "lam_min", "lam_ready", "tanh_done", "a_ready", "a_squared", "one_minus", "rooted", "gated_in",
            "u_ready", "scanned", "head_done")}

    def scalar(self, act):
        k, nc, s = self.k, self.k.nc, self.flags
        xc, r, i, ygate, u, sq, y = self.tiles
        tmp = k.v("tmp", 0, 4)
        nc.scalar.activation(tmp, k.v("lam", 0, 4), ACT.Abs).then_inc(s["soft"], 1)
        act.wait_ge(s["soft"], k.at(s["soft"], 1))
        nc.scalar.activation(tmp, tmp, ACT.Exp, scale=-1.0).then_inc(s["soft"], 1)
        act.wait_ge(s["soft"], k.at(s["soft"], 2))
        nc.scalar.activation(tmp, tmp, ACT.Ln, bias=1.0).then_inc(s["soft"], 1)
        act.wait_ge(s["lam_ready"], k.at(s["lam_ready"], 1))
        for j in range(4):
            nc.scalar.activation(u(j), r(j), ACT.Tanh, scale=k.v("decay", j)).then_inc(s["tanh_done"], 1)
        for j in range(4):
            nc.scalar.activation(r(j), r(j), ACT.Exp, scale=k.v("decay", j)).then_inc(s["a_ready"], 1)
        for j in range(4):
            act.wait_ge(s["a_ready"], k.at(s["a_ready"], j + 1))
            nc.scalar.activation(sq(j), r(j), ACT.Square).then_inc(s["a_squared"], 1)
        for j in range(4):
            act.wait_ge(s["one_minus"], k.at(s["one_minus"], j + 1))
            nc.scalar.activation(u(j), u(j), ACT.Sqrt, scale=-1.0).then_inc(s["rooted"], 1)

    def vector(self, dve):
        k, nc, s = self.k, self.k.nc, self.flags
        xc, r, i, ygate, u, sq, y = self.tiles
        tmp = k.v("tmp", 0, 4)
        dve.wait_ge(s["soft"], k.at(s["soft"], 3))
        nc.vector.scalar_tensor_tensor(tmp, k.v("lam", 0, 4), 0.0, tmp, ALU.min, ALU.subtract)\
            .then_inc(s["lam_min"], 1)
        dve.wait_ge(s["lam_min"], k.at(s["lam_min"], 1))
        nc.vector.tensor_scalar(k.v("decay", 0, 4), tmp, LRU_C, None, ALU.mult).then_inc(s["lam_ready"], 1)
        for j in range(4):
            dve.wait_ge(s["a_squared"], k.at(s["a_squared"], j + 1))
            nc.vector.scalar_tensor_tensor(u(j), sq(j), 1.0, u(j), ALU.add, ALU.mult)\
                .then_inc(s["one_minus"], 1)
            nc.vector.tensor_tensor(i(j), i(j), xc(j), ALU.mult).then_inc(s["gated_in"], 1)
        for j in range(4):
            dve.wait_ge(s["rooted"], k.at(s["rooted"], j + 1))
            dve.wait_ge(s["gated_in"], k.at(s["gated_in"], j + 1))
            nc.vector.tensor_tensor(u(j), u(j), i(j), ALU.mult).then_inc(s["u_ready"], 1)
            dve.wait_ge(s["u_ready"], k.at(s["u_ready"], j + 1))
            nc.vector.tensor_tensor_scan(y(j), r(j), u(j), 0.0, ALU.mult, ALU.add).then_inc(s["scanned"], 1)
            dve.wait_ge(s["scanned"], k.at(s["scanned"], j + 1))
            nc.vector.tensor_tensor(y(j), y(j), ygate(j), ALU.mult).then_inc(s["head_done"], 1)

    def passed(self):
        self.k.passed(soft=3, lam_min=1, lam_ready=1, tanh_done=4, a_ready=4, a_squared=4, one_minus=4, rooted=4, gated_in=4,
                      u_ready=4, scanned=4, head_done=4)


class GlaGates:

    def __init__(self, k, q, key, z, bc, taken, after):
        self.k, self.q, self.key, self.z, self.bc, self.taken, self.after = k, q, key, z, bc, taken, after
        self.fwd = lambda p: k.scr[:, p, :]
        self.kt = lambda p: k.scr[:, 2 + p, :]
        self.ke = lambda p: k.scr[:, 4 + p, :]
        self.tmp = lambda p: k.scr[:, 10 + p, :]
        self.flags = {n: k.flag(n) for n in (
            "z_soft", "log_f", "run_f", "to_end", "fwd_exp", "back_exp", "end_exp", "q_scaled", "k_scaled", "k_end")}

    def scalar_soft(self, act):
        k, nc, s, z, tmp = self.k, self.k.nc, self.flags, self.z, self.tmp
        act.wait_ge(*self.after)
        act.wait_ge(self.taken, k.at(self.taken, 2))
        for p in range(2):
            nc.scalar.activation(tmp(p), z(p), ACT.Abs).then_inc(s["z_soft"], 1)
            act.wait_ge(s["z_soft"], k.at(s["z_soft"], 3 * p + 1))
            nc.scalar.activation(tmp(p), tmp(p), ACT.Exp, scale=-1.0).then_inc(s["z_soft"], 1)
            act.wait_ge(s["z_soft"], k.at(s["z_soft"], 3 * p + 2))
            nc.scalar.activation(tmp(p), tmp(p), ACT.Ln, bias=1.0).then_inc(s["z_soft"], 1)

    def scalar_exp(self, act):
        k, nc, s, bc, fwd, kt, ke = self.k, self.k.nc, self.flags, self.bc, self.fwd, self.kt, self.ke
        for p in range(2):
            act.wait_ge(s["run_f"], k.at(s["run_f"], p + 1))
            nc.scalar.activation(fwd(p), bc(p), ACT.Exp, scale=1.0 / GLA_TAU).then_inc(s["fwd_exp"], 1)
            nc.scalar.activation(kt(p), bc(p), ACT.Exp, scale=-1.0 / GLA_TAU).then_inc(s["back_exp"], 1)
            act.wait_ge(s["to_end"], k.at(s["to_end"], p + 1))
            nc.scalar.activation(ke(p), ke(p), ACT.Exp, scale=1.0 / GLA_TAU).then_inc(s["end_exp"], 1)

    def vector(self, dve):
        k, nc, s, z, bc, tmp = self.k, self.k.nc, self.flags, self.z, self.bc, self.tmp
        q, key, fwd, kt, ke = self.q, self.key, self.fwd, self.kt, self.ke
        chunks = lambda x: x.rearrange("p (c t) -> p c t", t=CHUNK)
        for p in range(2):
            dve.wait_ge(s["z_soft"], k.at(s["z_soft"], 3 * p + 3))
            nc.vector.scalar_tensor_tensor(z(p), z(p), 0.0, tmp(p), ALU.min, ALU.subtract)\
                .then_inc(s["log_f"], 1)
            dve.wait_ge(s["log_f"], k.at(s["log_f"], p + 1))
            nc.vector.tensor_tensor_scan(bc(p), k.c("goes_on"), z(p), 0.0, ALU.mult, ALU.add)\
                .then_inc(s["run_f"], 1)
            dve.wait_ge(s["run_f"], k.at(s["run_f"], p + 1))
            nc.vector.tensor_tensor(chunks(ke(p)), chunks(bc(p))[:, :, CHUNK - 1:CHUNK].broadcast_to(
                [P, NCHUNK, CHUNK]), chunks(bc(p)), ALU.subtract).then_inc(s["to_end"], 1)
        dve.wait_ge(self.taken, k.at(self.taken, 6))
        for p in range(2):
            dve.wait_ge(s["end_exp"], k.at(s["end_exp"], p + 1))
            nc.vector.tensor_tensor(ke(p), ke(p), key(p), ALU.mult).then_inc(s["k_end"], 1)
            nc.vector.tensor_tensor(kt(p), kt(p), key(p), ALU.mult).then_inc(s["k_scaled"], 1)
            nc.vector.scalar_tensor_tensor(q(p), q(p), CHUNK ** -0.5, fwd(p), ALU.mult, ALU.mult)\
                .then_inc(s["q_scaled"], 1)

    def passed(self):
        self.k.passed(z_soft=6, log_f=2, run_f=2, to_end=2, fwd_exp=2, back_exp=2, end_exp=2, q_scaled=2, k_scaled=2,
                      k_end=2)


def gla_phase(k, gates, q, v, states, y):
    nc = k.nc
    s = {n: k.flag(n) for n in (
        "end_turned", "end_laid", "added", "state_zero", "state_ready", "scored", "weighted", "unit_summed",
        "stored")}
    fwd, kt, ke = gates.fwd, gates.kt, gates.ke
    ke_tok = lambda p: k.scr[:, 6 + p, :]
    at = lambda i: k.scr[:, 8 + i % 2, 0:P]
    units = [(h, tb) for h in range(HEADS) for tb in range(QB)]
    n = len(units)
    with nc.Block() as block:
        @block.scalar
        def _(act):
            for p in range(2):
                act.wait_ge(s["end_turned"], k.at(s["end_turned"], p + 1))
                nc.scalar.activation(ke_tok(p), k.ps[:, p, :], ACT.Copy).then_inc(s["end_laid"], 1)
            for h in range(HEADS):
                act.wait_ge(s["unit_summed"], k.at(s["unit_summed"], QB * (h + 1)))
                nc.scalar.activation(y(h), k.ps[:, 4 + h, :], ACT.Copy).then_inc(s["stored"], 1)

        @block.vector
        def _(dve):
            nc.vector.memset(states(0, 0), 0.0).then_inc(s["state_zero"], 1)
            nc.vector.memset(states(1, 0), 0.0).then_inc(s["state_zero"], 1)
            dve.wait_ge(s["state_zero"], k.at(s["state_zero"], 2))
            for c in range(NCHUNK - 1):
                for p in range(2):
                    if c > 0:
                        dve.wait_ge(s["state_ready"], k.at(s["state_ready"], 2 * (c - 1) + p + 1))
                    dve.wait_ge(s["added"], k.at(s["added"], p + 1))
                    nc.vector.scalar_tensor_tensor(
                        states(p, c + 1), states(p, c), fwd(p)[:, CHUNK * (c + 1) - 1:CHUNK * (c + 1)],
                        k.ps[:, 2 * p + c % 2, P * (c // 2):P * (c // 2) + P], ALU.mult, ALU.add)\
                        .then_inc(s["state_ready"], 1)
            for i in range(n):
                dve.wait_ge(s["scored"], k.at(s["scored"], i + 1))
                if i >= 2:
                    dve.wait_ge(s["unit_summed"], k.at(s["unit_summed"], i - 1))
                nc.vector.tensor_tensor(at(i), k.ps[:, i % 2, 0:P], k.c("chunk_tri"), ALU.mult)\
                    .then_inc(s["weighted"], 1)

        @block.tensor
        def _(pe):
            for p in range(2):
                for tb in range(QB):
                    mm = nc.tensor.transpose(k.ps[:, p, P * tb:P * tb + P], ke(p)[:, P * tb:P * tb + P], k.c("ident"))
                mm.then_inc(s["end_turned"], 1)
            pe.wait_ge(s["end_laid"], k.at(s["end_laid"], 2))
            for p in range(2):
                for c in range(NCHUNK):
                    lo = CHUNK * (c % 2)
                    for hh in range(2):
                        mm = nc.tensor.matmul(
                            k.ps[64 * hh:64 * hh + 64, 2 * p + c % 2, P * (c // 2):P * (c // 2) + P],
                            ke_tok(p)[lo:lo + CHUNK, P * (c // 2) + 64 * hh:P * (c // 2) + 64 * hh + 64],
                            v(c // 2, 2 * p + hh)[lo:lo + CHUNK], start=True, stop=True)
                mm.then_inc(s["added"], 1)
            pe.wait_ge(s["state_ready"], k.at(s["state_ready"], 2 * (NCHUNK - 1)))
            for i in range(n + 1):
                if i < n:
                    h, tb = units[i]
                    p, lo = h // 2, 64 * (h % 2)
                    if i >= 2:
                        pe.wait_ge(s["weighted"], k.at(s["weighted"], i - 1))
                    nc.tensor.matmul(k.ps[:, i % 2, 0:P], kt(p)[lo:lo + 64, P * tb:P * tb + P],
                                     q(p)[lo:lo + 64, P * tb:P * tb + P], start=True, stop=True)\
                        .then_inc(s["scored"], 1)
                if i >= 1:
                    h, tb = units[i - 1]
                    p, lo = h // 2, 64 * (h % 2)
                    pe.wait_ge(s["weighted"], k.at(s["weighted"], i))
                    nc.tensor.matmul(k.ps[:, 4 + h, P * tb:P * tb + P], v(tb, h), at(i - 1), start=True, stop=False)
                    for c in (2 * tb, 2 * tb + 1):
                        mm = nc.tensor.matmul(k.ps[:, 4 + h, CHUNK * c:CHUNK * c + CHUNK],
                                              states(p, c)[lo:lo + 64], q(p)[lo:lo + 64, CHUNK * c:CHUNK * c + CHUNK],
                                              start=False, stop=(c % 2 == 1))
                    mm.then_inc(s["unit_summed"], 1)
    k.passed(end_turned=2, end_laid=2, added=2, state_zero=2, state_ready=2 * (NCHUNK - 1), scored=n, weighted=n,
             unit_summed=n, stored=HEADS)


class Compress:

    def __init__(self, k, kv, blk, w1, w2, hid, kc, vc, gates_in, gates):
        self.k, self.blk, self.w1, self.w2, self.hid, self.kc, self.vc = k, blk, w1, w2, hid, kc, vc
        self.gates_in, self.gates = gates_in, gates
        self.by_token = kv.rearrange("p (m s) -> p s m", s=CMP_STRIDE)
        self.ends = k.use([range(w1, w1 + 16), range(w1, w1 + 16), [w2], [w2]], by_slab=False)
        self.blocks, self.gelu, self.stored = k.flag("blocks_ready"), k.flag("gelu_done"), k.flag("stored")

    def vector(self, dve):
        k = self.k
        for a in range(2):
            pos = k.v("pos", CMP_STRIDE * a, CMP_STRIDE).unsqueeze(2).broadcast_to([P, CMP_STRIDE, NCMP])
            k.nc.vector.tensor_tensor(self.blk[:, CMP_STRIDE * a:CMP_STRIDE * (a + 1), :],
                                      self.by_token[:, :, a:a + NCMP], pos, ALU.add).then_inc(self.blocks, 1)

    def tensor_hidden(self, pe):
        k = self.k
        pe.wait_ge(self.blocks, k.at(self.blocks, 2))
        for j, lo in enumerate((0, 64)):
            for l in range(CMP_LEN):
                at = self.w1 + l // 2
                k.need(pe, at)
                mm = k.nc.tensor.matmul(k.ps[lo:lo + 64, 4 + j, 0:NCMP],
                                        k.raw_tile(at)[lo:lo + 64, 64 * (l % 2):64 * (l % 2) + 64],
                                        self.blk[lo:lo + 64, l, :], start=(l == 0), stop=(l == CMP_LEN - 1))
            mm.then_inc(k.sums_done, 1)

    def tensor_out(self, pe):
        k, nc, hid, w2 = self.k, self.k.nc, self.hid, self.w2
        pe.wait_ge(self.gelu, k.at(self.gelu, 2))
        k.need(pe, w2)
        nc.tensor.matmul(k.ps[:, 6, 0:NCMP], k.raw_tile(w2)[0:64, :], hid[0:64, 0:NCMP], start=True, stop=True)\
            .then_inc(k.sums_done, 1)
        nc.tensor.matmul(k.ps[0:NCMP, 7, 0:64], hid[64:128, 0:NCMP], k.raw_tile(w2)[64:128, 0:64], start=True,
                         stop=True).then_inc(k.sums_done, 1)

    def scalar_hidden(self, act):
        k, nc, hid = self.k, self.k.nc, self.hid
        nc.scalar.activation(self.gates, self.gates_in, ACT.Sigmoid).then_inc(self.stored, 1)
        for j, lo in enumerate((0, 64)):
            act.wait_ge(k.sums_done, self.ends[j])
            nc.scalar.activation(hid[lo:lo + 64, 0:NCMP], k.ps[lo:lo + 64, 4 + j, 0:NCMP], ACT.Gelu_apprx_tanh)\
                .then_inc(self.gelu, 1)

    def scalar_out(self, act):
        k, nc = self.k, self.k.nc
        act.wait_ge(k.sums_done, self.ends[2])
        nc.scalar.activation(self.kc, k.ps[:, 6, 0:NCMP], ACT.Copy).then_inc(self.stored, 1)
        act.wait_ge(k.sums_done, self.ends[3])
        nc.scalar.activation(self.vc, k.ps[0:NCMP, 7, 0:64], ACT.Copy).then_inc(self.stored, 1)

    def passed(self):
        self.k.passed(blocks_ready=2, gelu_done=2, stored=3)


def index_phase(k, iq, ik, weight, index, compress):
    nc = k.nc
    scored, relu, summed = [k.flag(n) for n in ("scored", "relu_done", "index_added")]
    units = [(qb, h) for qb in range(1, QB) for h in range(IDX_HEADS)]
    with nc.Block() as block:
        @block.sync
        def _(sp):
            k.load_slabs(sp)

        @block.tensor
        def _(pe):
            for i, (qb, h) in enumerate(units):
                if i == 4:
                    compress.tensor_hidden(pe)
                if i == 12:
                    compress.tensor_out(pe)
                lo = 32 * (h % 4)
                if i >= 4:
                    pe.wait_ge(relu, k.at(relu, i - 3))
                nc.tensor.matmul(k.ps[:, i % 4, 0:P * (qb + 1)], iq(h // 4)[lo:lo + 32, P * qb:P * qb + P],
                                 ik[lo:lo + 32, 0:P * (qb + 1)], start=True, stop=True,
                                 tile_position=(lo, 0)).then_inc(scored, 1)

        @block.scalar
        def _(act):
            for i, (qb, h) in enumerate(units):
                if i == 4:
                    compress.scalar_hidden(act)
                if i == 12:
                    compress.scalar_out(act)
                act.wait_ge(scored, k.at(scored, i + 1))
                if i >= 8:
                    act.wait_ge(summed, k.at(summed, i - 7 + (i - 8) // 8))
                nc.scalar.activation(k.scr[:, i % 8, 0:P * (qb + 1)], k.ps[:, i % 4, 0:P * (qb + 1)], ACT.Relu,
                                     scale=(IDX_HEADS * 32) ** -0.5).then_inc(relu, 1)

        @block.vector
        def _(dve):
            compress.vector(dve)
            added = 0
            for i, (qb, h) in enumerate(units):
                w = P * (qb + 1)
                s = index(qb)[:, 0:w]
                r = k.scr[:, i % 8, 0:w]
                dve.wait_ge(relu, k.at(relu, i + 1))
                if h == 0:
                    nc.vector.tensor_scalar(s, r, weight(qb, h), None, ALU.mult).then_inc(summed, 1)
                else:
                    dve.wait_ge(summed, k.at(summed, added))
                    nc.vector.scalar_tensor_tensor(s, r, weight(qb, h), s, ALU.mult, ALU.add)\
                        .then_inc(summed, 1)
                added += 1
                if h < IDX_HEADS - 1:
                    continue
                dve.wait_ge(summed, k.at(summed, added))
                nc.vector.tensor_tensor(s, s, k.c("causal")[:, T - w:T], ALU.add).then_inc(summed, 1)
                added += 1
    compress.passed()
    k.passed(scored=len(units), relu_done=len(units), index_added=9 * (QB - 1))


def take_top(k, dve, index, steps, first):
    nc = k.nc
    top, taken = k.flag("top8"), k.flag("top8_taken")
    for t in steps:
        qb = 1 + t // TOP_STEPS
        s = index(qb)[:, 0:P * (qb + 1)]
        best = k.stat[:, 0, 56:64]
        if t > first:
            dve.wait_ge(taken, k.at(taken, t - first))
        nc.vector.max(best, s).then_inc(top, 1)
        dve.wait_ge(top, k.at(top, t - first + 1))
        nc.vector.match_replace(s, best, s, TAKEN).then_inc(taken, 1)
        if t % TOP_STEPS == TOP_STEPS - 1:
            dve.wait_ge(taken, k.at(taken, t - first + 1))
            nc.vector.tensor_scalar(s, s, TAKEN / 2, NEG, ALU.is_ge, ALU.mult).then_inc(k.flag("select_made"), 1)


def share(steps, i, n):
    return range(steps.start + len(steps) * i // n, steps.start + len(steps) * (i + 1) // n)


def rows_done(steps):
    return sum(1 for t in steps if t % TOP_STEPS == TOP_STEPS - 1)


def copy_in_phase(k, sources):
    nc = k.nc
    here = k.flag("inputs_here")
    with nc.Block() as block:
        @block.sync
        def _(sp):
            for dst, src in sources:
                sp.dma_start(dst, src).then_inc(here, 16)
            k.load_slabs(sp)
            sp.wait_ge(here, k.at(here, 16 * len(sources)))
    k.passed(inputs_here=16 * len(sources))


def softmax_units(q, key, v, dims, width_of, masks, scale, group0, out, extra=None):
    units = []
    for h in range(HEADS):
        for qb in range(QB):
            w = P * (qb + 1)
            pairs = [(q(h)[:, P * qb:P * qb + P], key(h)[:, 0:w])] + (extra(h, w) if extra else [])
            lo = 64 * (h % 2) if dims == 64 else 0
            units.append(Unit(pairs, w, [v(kb, h) for kb in range(qb + 1)], group0 + QB * h + qb, True, True,
                              (lo, lo + dims), out(h)[lo:lo + dims, P * qb:P * qb + P], scale, mask=masks(qb)))
    return units


def token_job(k, act_tile, at, out):
    s = []
    for tb in range(QB):
        block = slice(P * tb, P * tb + P)
        s.append(([(act_tile(0)[:, block], k.raw_tile(at))], at, block, True, True))
    return {"sum": s, "out": out, "view": lambda bank: bank.rearrange("p (t n) -> p t n", n=P)}


def feature_job(k, act_tile, at, out, depth=KD, split=True, also=(), **more):
    s = []
    for c in range(depth):
        part = k.products(at + c, act_tile(c)) if split else [(k.raw_tile(at + c), act_tile(c))]
        s.append((part, at + c, slice(0, T), c == 0, c == depth - 1 and not also))
    if also:
        s.append(([also], None, slice(0, T), False, True))
    return {"sum": s, "out": out, **more}


def block_one(k):
    nc, big, scr, w = k.nc, k.big, k.scr, WHERE
    k.vec_cols = VEC1
    act = lambda c: (k.in_hi[:, c, :], k.in_lo[:, c, :])
    into = lambda g: [[(k.x[:, c, :], k.act[:, c, :], k.v(g, c), None) for c in range(KD)]]
    tile = lambda base: (lambda j: big[:, base + j, :])
    value = lambda base: (lambda tb, h: big[:, base + tb, P * h:P * h + P])
    small, i_row, f_fx = big[:, 40, :], big[:, 41, :], big[:, 42, :]
    y = lambda n, c: big[:, 12 + 4 * n + c, :]
    token_phase(k, act, [(w[key], lambda tb, n=n: big[:, 4 * n + tb, :], scr[:, 4 + n, :])
                         for n, key in enumerate(("mv", "fv", "gv"))],
                RmsNorm(k, into("norm1_g"), "rms_eps", D, parts=[act(c) for c in range(KD)]))
    jobs = []
    F = lambda key, j, out, **more: feature_job(k, act, w[key][j], out, bias=k.v("b_" + key, j), **more)
    jobs.append(feature_job(k, act, w["small"], small, bias=k.v("b_small")))
    jobs.append(feature_job(k, act, w["mi"], i_row, bias=k.v("b_mi")))
    for j in range(4):
        jobs.append(F("mq", j, big[:, 28 + j, :]))
    for j in range(4):
        jobs.append(F("mk", j, big[:, 32 + j, :]))
    for j in range(4):
        jobs.append(F("mo", j, big[:, 36 + j, :], func=ACT.Sigmoid))
    gates = MlstmGates(k, small, i_row, f_fx, k.flag("taken"))
    gemm_phase(k, jobs, scalar={2: gates.scalar}, vector=gates.vector)
    gates.passed()
    mlstm_phase(k, tile(28), tile(32), value(0), lambda h: y(0, h))
    norm = RmsNorm(k, [[(y(0, h), y(0, h), k.v("ml_g", h), big[:, 36 + h, :])] for h in range(4)], "rms_eps", P,
                   bank=4)
    gemm_phase(k, [F(key, j, big[:, b + j, :]) for key, b in (("fq", 28), ("fk", 32)) for j in range(4)],
               norm)
    rms_phase(k, [[(big[:, b + h, :], big[:, b + h, :], k.v(g), None)] for b, g in ((28, "fxq_g"), (32, "fxk_g"))
                  for h in range(4)], "rms_eps", P)
    less_f = lambda h, n: [(k.c("negroot", 4)[:, h:h + 1].broadcast_to([4, P]), f_fx[0:4, 0:n])]
    attention_phase(k, softmax_units(tile(28), tile(32), value(4), P, None, lambda qb: k.c("causal")[:, T - P * (qb + 1):T],
                                     P ** -0.5, 0, lambda h: y(1, h), extra=less_f))
    padded = big[:, 28:33, :].rearrange("p a b -> p (a b)")[:, 0:4 * (T + 3)].rearrange("p (j t) -> p j t", j=4)
    xc = lambda j: scr[:, j, :]
    gemm_phase(k, [F("rx", j, padded[:, j, 3:T + 3]) for j in range(4)]
               + [F("ry", j, big[:, 24 + j, :], func=ACT.Gelu_apprx_tanh) for j in range(4)],
               vector=lambda dve: conv_vector(k, dve, padded, xc, k.flag("taken")))
    k.passed(edge=1, conv_step=16)
    gemm_phase(k, [feature_job(k, lambda c, j=j: xc(j), w[wk][j], scr[:, b + j, :], depth=1, split=False, bias=k.v(bk, j),
                               func=ACT.Sigmoid) for wk, bk, b in (("wa", "lru_ba", 4), ("wx", "lru_bx", 8))
                   for j in range(4)])
    lru = Lru(k, xc, lambda j: scr[:, 4 + j, :], lambda j: scr[:, 8 + j, :], tile(24), tile(4), tile(0),
              lambda j: y(2, j))
    states = big[:, 40:44, :].rearrange("p a b -> p (a b)").rearrange("p (q c n) -> p q c n", q=2, n=P)
    done = k.flag("head_done")
    gates = GlaGates(k, tile(28), tile(30), tile(36), tile(38), k.flag("taken"), (done, k.at(done, 4)))

    def beside(dve):
        lru.vector(dve)
        gates.vector(dve)

    gemm_phase(k, [feature_job(k, lambda c: small, w["walpha"][j], big[:, 36 + j, :], depth=1, split=False,
                               bias=k.v("b_alpha", j)) for j in range(2)]
               + [F(key, j, big[:, b + j, :]) for key, b in (("gq", 28), ("gk", 30)) for j in range(2)]
               + [F("gg", j, big[:, 32 + j, :], func=ACT.Silu) for j in range(4)],
               scalar={0: lru.scalar, 4: gates.scalar_soft, 7: gates.scalar_exp}, vector=beside)
    lru.passed()
    gates.passed()
    gla_phase(k, gates, tile(28), value(8), lambda p, c: states[:, p, c, :], lambda h: y(3, h))
    merged = lambda d: big[:, d, :]
    y_parts = lambda n, c: (k.parts[:, 28 + 4 * n + c, :], k.parts[:, 12 + 4 * n + c, :])
    norm = RmsNorm(k, [[(y(3, h), y(3, h), k.v("gla_g", h), big[:, 32 + h, :])] for h in range(4)], "rms_eps", P,
                   parts=[y_parts(3, c) for c in range(4)], bank=4)
    merge_phase(k, w["merge"], y, y_parts, merged, norm)
    merged_parts = lambda d: (k.parts[:, 8 + d, :], k.parts[:, d, :])
    split_phase(k, [(merged(d), *merged_parts(d)) for d in range(KD)])
    project_phase(k, w["wo"], 1.0, merged_parts)
    norm = RmsNorm(k, into("norm2_g"), "rms_eps", D, parts=[act(c) for c in range(KD)])
    for up, down in w["ffn"]:
        relu2_phase(k, up, down, norm)
        norm = None


def layer(k, l, norm):
    big, w = k.big, WHERE["layers"][l]
    k.vec_cols, k.vec_from = VEC2, VEC1.n + l * VEC2.n
    x = lambda c: (k.in_hi[:, c, :], k.in_lo[:, c, :])
    if norm is None:
        split_phase(k, [(k.x[:, c, :], *x(c)) for c in range(KD)])
    glu_phase(k, *w["ffn1"], norm)
    tile = lambda i: big[:, i, :]
    v_tok = lambda tb: big[:, tb, :]
    v_mla = big[:, 4:6, :].rearrange("p a b -> p (a b)").rearrange("p (t n) -> p t n", n=256)
    token_phase(k, x, [(w["v"], v_tok, None)], LayerNorm(k, "ln1_g", "ln1_b"),
                loads=[(big[:, 33:42, :].rearrange("p a b -> p (a b)"), k.rope_dram)])
    jobs = []
    at = {"cq0": 6, "cq1": 7, "ckv": 8, "krope": 9, "kvcmp": 10, "iq0": 11, "iq1": 12, "ik": 13, "nq0": 14,
          "nq1": 15, "ks": 16, "kw": 17, "dq0": 18, "dq1": 19, "dk": 20, "sq0": 21, "sq1": 22, "sk0": 23, "sk1": 24}
    rope = {"krope": "mq", "kvcmp": "cmp", "iq0": "i4", "iq1": "i4", "ik": "i4", "nq0": "h2", "nq1": "h2",
            "ks": "h2", "kw": "h2", "dq0": "h2", "dq1": "h2", "dk": "h2"}
    jobs += [feature_job(k, x, w[key], tile(i), rope=rope.get(key)) for key, i in at.items()]
    gemm_phase(k, jobs)
    rms_phase(k, [[(tile(6 + j), tile(6 + j), k.v("q_g", j), None) for j in range(2)],
                  [(tile(8), tile(8), k.v("kv_g"), None)]], "rms_eps", (256, P))
    jobs = [feature_job(k, lambda c: tile(6 + c), w["uq"][h], tile(25 + h), depth=2, split=False, rope="mq") for h in range(HEADS)]
    for h in range(HEADS):
        jobs.append(feature_job(k, lambda c: tile(8), w["uk"][h], tile(29 + h), depth=1, split=False,
                                also=(k.c("ident"), tile(9))))
    jobs += [token_job(k, lambda c: tile(8), w["uv"][q], v_mla[:, :, P * q:P * q + P]) for q in range(2)]
    gemm_phase(k, jobs)
    blk = big[:, 37:39, :].rearrange("p a b -> p (a b)")[:, 0:CMP_LEN * NCMP].rearrange("p (l n) -> p l n", n=NCMP)
    kc, vc, gates = tile(36)[:, 0:NCMP], tile(36)[0:NCMP, 64:128], tile(36)[:, 256:256 + 48].rearrange(
        "p (t g) -> p t g", g=12)
    compress = Compress(k, tile(10), blk, w["c1"], w["c2"], tile(36)[:, 128:192], kc, vc,
                        big[:, 0:QB, GT0:GT0 + 12], gates)
    select = lambda qb: tile(32 + qb)
    index_phase(k, lambda j: tile(11 + j), tile(13), lambda qb, h: v_tok(qb)[:, IW0 + h:IW0 + h + 1], select,
                compress)
    causal = lambda qb: k.c("causal")[:, T - P * (qb + 1):T]
    half = lambda t, h: t[64 * (h % 2):64 * (h % 2) + 64]
    ys = lambda n: (lambda h: k.act[:, 2 * n + h // 2, :])
    units = softmax_units(lambda h: tile(25 + h), lambda h: tile(29 + h),
                          lambda kb, h: v_mla[:, kb, 64 * h:64 * h + 64], 64, None, causal, 96 ** -0.5, 0, ys(0))
    attention_phase(k, units, select, range(0, TOP_CUTS[0]))
    units = []
    for h in range(HEADS):
        lo = 64 * (h % 2)
        q = half(tile(14 + h // 2), h)
        for qb in range(QB):
            wd = P * (qb + 1)
            more = dict(group=QB * h + qb, rows=(lo, lo + 64), scale=64 ** -0.5,
                        out=ys(1)(h)[lo:lo + 64, P * qb:P * qb + P])
            gate = lambda b: gates[:, qb, 4 * b + h:4 * b + h + 1]
            qs = q[:, P * qb:P * qb + P]
            at_cmp = slice(CONST.at["cmp_neg"][0] + NCMP * qb, CONST.at["cmp_neg"][0] + NCMP * (qb + 1))
            at_keep = slice(CONST.at["cmp_keep"][0] + NCMP * qb, CONST.at["cmp_keep"][0] + NCMP * (qb + 1))
            units.append(Unit([(qs, half(kc, h))], NCMP, [vc], first=True, last=False, gate=gate(0),
                              mask=k.const[:, at_cmp], keep=k.const[:, at_keep], **more))
            for b, (kt, col) in enumerate(((16, VS0), (17, VW0))):
                units.append(Unit([(qs, half(tile(kt), h)[:, 0:wd])], wd,
                                  [v_tok(kb)[:, col:col + 64] for kb in range(qb + 1)], first=False, last=(b == 1),
                                  gate=gate(b + 1), mask=causal(qb), **more))
    attention_phase(k, units, select, range(*TOP_CUTS))
    units = softmax_units(lambda h: half(tile(21 + h // 2), h), lambda h: half(tile(23 + h // 2), h),
                          lambda kb, h: v_tok(kb)[:, VB0 + 64 * h:VB0 + 64 * h + 64], 64, None,
                          lambda qb: k.c("strict")[:, T - P * (qb + 1):T], 64 ** -0.5, 0, ys(3))
    stick_phase(k, units, lambda i: tile((14, 15, 16, 17, 36, 37, 38, 39, 40, 41, 42, 43)[i % 12]),
                lambda i: tile(25 + i % 4), select,
                range(TOP_CUTS[1], TOP_STEPS * (QB - 1)))
    units = softmax_units(lambda h: half(tile(18 + h // 2), h), lambda h: half(tile(20), h),
                          lambda kb, h: v_tok(kb)[:, VD0:VD0 + 64], 64, None,
                          lambda qb: causal(0) if qb == 0 else select(qb)[:, 0:P * (qb + 1)], 64 ** -0.5, 0, ys(2))
    attention_phase(k, units)
    norm = RmsNorm(k, [[(k.act[:, 2 * g + j, :], k.act[:, 2 * g + j, :], k.v("group_g", 2 * g + j), None)
                        for j in range(2)] for g in range(4)], "rms_eps", 256, parts=[x(c) for c in range(KD)])
    project_phase(k, w["wout"], ALPHA, x, norm)
    glu_phase(k, *w["ffn2"], LayerNorm(k, "ln2_g", "ln2_b"))


def build(nc, x, weights, const, rope, vec1, brow, vec2, out):
    with ExitStack() as ctx:
        k = Core(nc, ctx, weights)
        k.rope_dram = rope
        copy_in_phase(k, [(k.x[:, :, :], x.rearrange("c p t -> p c t")), (k.const[:, :], const),
                          (k.vec[:, 0:VEC1.n], vec1),
                          *[(k.vec[:, VEC1.n + l * VEC2.n:VEC1.n + (l + 1) * VEC2.n], vec2[l]) for l in range(LAYERS)],
                          (k.scr[:, 4:7, :], brow.rearrange("a (b c) -> a b c", c=T).broadcast_to([P, 3, T]))])

        block_one(k)
        norm = None
        for l in range(LAYERS):
            layer(k, l, norm)
            norm = LayerNorm(k, "ln3_g", "ln3_b")
        output_phase(k, "ln3_g", "ln3_b", out)


def pack_weights(inputs):
    packed = np.zeros((len(STREAM.tiles), P, P), np.float32)
    for n, pieces in enumerate(STREAM.tiles):
        for name, lay, row, col, r0, c0, h, w in pieces or ():
            a = inputs[name][lay]
            if isinstance(row, tuple):
                a, row = a[row[0]], row[1]
            packed[n, r0:r0 + h, c0:c0 + w] = a[row:row + h, col:col + w]
    packed = packed.reshape(NSLABS, SLAB, P, P).transpose(0, 2, 1, 3)
    return np.ascontiguousarray(packed).reshape(NSLABS, P, SLAB * P)


def by_column(v):
    return np.asarray(v).reshape(-1, P).T


def pack_vec1(i):
    out = np.zeros((P, VEC1.n), np.float32)

    def put(name, a):
        at, n = VEC1.at[name]
        out[: a.shape[0], at:at + a.shape[1]] = a

    b = i["b_in"][0]
    put("norm1_g", by_column(i["norm1_g"][0]))
    put("norm2_g", by_column(i["norm2_g"][0]))
    for name, at, n in (("b_mq", MQ, 512), ("b_mk", MK, 512), ("b_mo", MO, 512), ("b_fq", FQ, 512),
                        ("b_fk", FK, 512), ("b_rx", RX, 512), ("b_ry", RY, 512), ("b_gq", GQ, 256),
                        ("b_gk", GK, 256), ("b_gg", GG, 512), ("b_gates", GATES, 4096)):
        put(name, by_column(b[at:at + n]))
    small = VEC1.at["b_small"][0]
    out[0:4, small] = b[MF:MF + 4]
    out[32:36, small] = b[FFG:FFG + 4]
    out[96:112, small] = b[GA:GA + 16]
    out[0:4, VEC1.at["b_mi"][0]] = b[MI:MI + 4]
    put("ml_g", by_column(i["ml_norm_g"][0]))
    put("gla_g", by_column(i["gla_norm_g"][0]))
    put("fxq_g", by_column(i["fx_qnorm_g"][0]))
    put("fxk_g", by_column(i["fx_knorm_g"][0]))
    put("conv_w", np.concatenate([by_column(i["lru_conv_w"][0][t]) for t in range(4)], 1))
    put("conv_b", by_column(i["lru_conv_b"][0]))
    put("lru_ba", by_column(i["lru_ba"][0]))
    put("lru_bx", by_column(i["lru_bx"][0]))
    put("lam", by_column(i["lru_lambda"][0]))
    put("b_alpha", by_column(i["gla_b_alpha"][0]))
    return out


def pack_vec2(i):
    out = np.zeros((LAYERS, P, VEC2.n), np.float32)
    for l in range(LAYERS):
        for name, key in (("ln1_g", "ln1_g_2"), ("ln1_b", "ln1_b_2"), ("q_g", "mla_q_norm_2"),
                          ("kv_g", "mla_kv_norm_2"), ("group_g", "group_norm_g_2"), ("ln2_g", "ln2_g_2"),
                          ("ln2_b", "ln2_b_2"), ("ln3_g", "ln3_g_2"), ("ln3_b", "ln3_b_2")):
            at, n = VEC2.at[name]
            out[l, :, at:at + n] = by_column(i[key][l])
        at, n = VEC2.at["pos"]
        out[l, 0:64, at:at + n] = i["nsa_cmp_pos_2"][l].T
        out[l, 64:128, at:at + n] = i["nsa_cmp_pos_2"][l].T
    return out


def arrays_of(inputs):
    i = {name: np.asarray(a) for name, a in inputs.items()}
    b = i["b_in"][0]
    const, rope = constants()
    return {
        "xT": np.ascontiguousarray(i["x"][0].T).reshape(KD, P, T),
        "weights": pack_weights(i),
        "consts": const,
        "rope": rope,
        "vec1": pack_vec1(i),
        "brow": np.concatenate([b[c:c + 512] for c in (MV, FV, GV)])[None, :],
        "vec2": pack_vec2(i),
    }


def kernel(**inputs):
    import concourse.bacc as bacc
    from concourse.bass_utils import run_bass_kernel_spmd

    nc = bacc.Bacc("TRN2", target_bir_lowering=False, num_devices=1)
    arrays = arrays_of(inputs)
    aps = [nc.dram_tensor(name, a.shape, F32, kind="ExternalInput").ap() for name, a in arrays.items()]
    out = nc.dram_tensor("outT", (KD, P, T), F32, kind="ExternalOutput").ap()
    build(nc, *aps, out)
    r = run_bass_kernel_spmd(nc, [arrays], core_ids=[0])
    got = np.asarray(r.results[0]["outT"]).reshape(D, T)
    return np.ascontiguousarray(got.T)[None]
```
